# Optimizing a Trainium2 kernel written in Bass

```python
import numpy as np
import jax, jax.numpy as jnp
from jax import lax

D_MODEL = 1024
BATCH = 1
SEQ = 1024
DEPTH = 1

N_META = 16
CHUNK = 128
PAD = CHUNK - N_META
RET_HEADS = 4
RET_QK_DIM = 128
RET_V_DIM = 256
SWA_Q_HEADS = 16
SWA_KV_HEADS = 4
SWA_GROUP = SWA_Q_HEADS // SWA_KV_HEADS
SWA_HEAD_DIM = 64
SWA_WINDOW = 128
D_FF = 4 * D_MODEL
EPS = 1e-6
RET_QK_W = RET_HEADS * RET_QK_DIM
RET_V_W = RET_HEADS * RET_V_DIM
SWA_Q_W = SWA_Q_HEADS * SWA_HEAD_DIM
SWA_KV_W = SWA_KV_HEADS * SWA_HEAD_DIM
IN_SPLITS = (RET_QK_W, RET_QK_W, RET_V_W, RET_V_W, SWA_Q_W, SWA_KV_W, SWA_KV_W, D_MODEL, D_MODEL)
D_IN = 2 * RET_QK_W + 2 * RET_V_W + SWA_Q_W + 2 * SWA_KV_W + 2 * D_MODEL

kernel_name = 'hybrid_retention_swa_block'

def rms_norm(x, g):
    xf = x.astype(jnp.float32)
    y = xf * lax.rsqrt(jnp.mean(xf * xf, axis=-1, keepdims=True) + EPS)
    return (y * g.astype(jnp.float32)).astype(x.dtype)

def retention(q, k, v):
    B, Lp = q.shape[0], q.shape[1]
    nb = Lp // CHUNK
    log_gamma = jnp.log1p(-(2.0 ** (-5.0 - jnp.arange(RET_HEADS, dtype=jnp.float32))))
    idx = jnp.arange(CHUNK, dtype=jnp.float32)
    diff = idx[:, None] - idx[None, :]
    intra = jnp.where(diff >= 0, jnp.exp(log_gamma[:, None, None] * jnp.maximum(diff, 0.0)), 0.0)
    q_decay = jnp.exp(log_gamma[:, None] * (idx + 1.0))[:, :, None]
    k_decay = jnp.exp(log_gamma[:, None] * (CHUNK - 1.0 - idx))[:, :, None]
    chunk_decay = jnp.exp(log_gamma * CHUNK)[:, None, None]
    k = k * (RET_QK_DIM ** -0.5)
    to_chunks = lambda t: t.reshape(B, nb, CHUNK, RET_HEADS, t.shape[-1]).transpose(1, 0, 3, 2, 4)
    qc, kc, vc = to_chunks(q), to_chunks(k), to_chunks(v)

    def step(state, inp):
        qn, kn, vn = inp
        s = jnp.einsum('bhqd,bhkd->bhqk', qn, kn) * intra
        o = (jnp.einsum('bhqk,bhkv->bhqv', s, vn)
             + jnp.einsum('bhqd,bhdv->bhqv', qn * q_decay, state))
        state = chunk_decay * state + jnp.einsum('bhkd,bhkv->bhdv', kn * k_decay, vn)
        return state, o

    state0 = jnp.zeros((B, RET_HEADS, RET_QK_DIM, RET_V_DIM), jnp.float32)
    _, o = lax.scan(step, state0, (qc, kc, vc))
    return o.transpose(1, 0, 3, 2, 4).reshape(B, Lp, RET_HEADS, RET_V_DIM).astype(q.dtype)

def sliding_window_attention(q, k, v, q_norm_g, k_norm_g, sinks):
    B, Lp = q.shape[0], q.shape[1]
    nb = Lp // CHUNK
    q = rms_norm(q, q_norm_g) * (SWA_HEAD_DIM ** -0.5)
    k = rms_norm(k, k_norm_g)
    qb = jnp.moveaxis(q.reshape(B, nb, CHUNK, SWA_KV_HEADS, SWA_GROUP, SWA_HEAD_DIM), 1, 0)
    kb = k.reshape(B, nb, CHUNK, SWA_KV_HEADS, SWA_HEAD_DIM)
    vb = v.reshape(B, nb, CHUNK, SWA_KV_HEADS, SWA_HEAD_DIM)
    shift = lambda t: jnp.pad(t, ((0, 0), (1, 0), (0, 0), (0, 0), (0, 0)))[:, :-1]
    k_band = jnp.moveaxis(jnp.concatenate([shift(kb), kb], axis=2), 1, 0)
    v_band = jnp.moveaxis(jnp.concatenate([shift(vb), vb], axis=2), 1, 0)
    k_meta = k[:, PAD:CHUNK]
    v_meta = v[:, PAD:CHUNK]
    slopes = (2.0 ** (-8.0 * jnp.arange(1, SWA_Q_HEADS + 1, dtype=jnp.float32) / SWA_Q_HEADS)
              ).reshape(SWA_KV_HEADS, SWA_GROUP)[:, :, None, None]
    sink = sinks.astype(jnp.float32).reshape(SWA_KV_HEADS, SWA_GROUP)[:, :, None, None]
    is_meta = jnp.arange(N_META + 2 * CHUNK) < N_META

    def block(args):
        qn, kn, vn, n = args
        t = n * CHUNK + jnp.arange(CHUNK)
        s = jnp.concatenate([PAD + jnp.arange(N_META), (n - 1) * CHUNK + jnp.arange(2 * CHUNK)])
        dist = t[:, None] - s[None, :]
        valid = (dist >= 0) & (is_meta[None, :] | ((dist < SWA_WINDOW) & (s[None, :] >= CHUNK)))
        keys = jnp.concatenate([k_meta, kn], axis=1)
        vals = jnp.concatenate([v_meta, vn], axis=1)
        scores = (jnp.einsum('bqhgd,bkhd->bhgqk', qn, keys).astype(jnp.float32)
                  - slopes * dist.astype(jnp.float32))
        scores = jnp.where(valid, scores, -jnp.inf)
        m = jnp.maximum(jnp.max(scores, axis=-1, keepdims=True), sink)
        p = jnp.exp(scores - m)
        probs = p / (jnp.sum(p, axis=-1, keepdims=True) + jnp.exp(sink - m))
        return jnp.einsum('bhgqk,bkhd->bqhgd', probs.astype(vals.dtype), vals)

    out = lax.map(block, (qb, k_band, v_band, jnp.arange(nb, dtype=jnp.int32)))
    return jnp.moveaxis(out, 0, 1).reshape(B, Lp, SWA_Q_W)

def mixer_layer(h, mix_norm_g, w_in, ret_norm_g, q_norm_g, k_norm_g, sinks, w_ret_branch, w_swa_branch, w_out):
    B, L = h.shape[0], h.shape[1]
    Lp = L + PAD
    hn = rms_norm(h, mix_norm_g)
    proj = hn @ w_in
    split_points = np.cumsum(IN_SPLITS)[:-1].tolist()
    rq, rk, rv, rg, sq, sk, sv, gr, gs = jnp.split(proj, split_points, axis=-1)
    pad = lambda t, nh: jnp.pad(t, ((0, 0), (PAD, 0), (0, 0))).reshape(B, Lp, nh, -1)
    y_ret = retention(pad(rq, RET_HEADS), pad(rk, RET_HEADS), pad(rv, RET_HEADS))[:, PAD:]
    y_ret = rms_norm(y_ret, ret_norm_g).reshape(B, L, RET_V_W) * jax.nn.silu(rg)
    y_swa = sliding_window_attention(pad(sq, SWA_Q_HEADS), pad(sk, SWA_KV_HEADS), pad(sv, SWA_KV_HEADS),
                                     q_norm_g, k_norm_g, sinks)[:, PAD:]
    merged = (jax.nn.sigmoid(gr) * (y_ret @ w_ret_branch)
              + jax.nn.sigmoid(gs) * (y_swa @ w_swa_branch))
    return merged @ w_out

def setup_inputs(seed: int = 0) -> dict:
    key = jax.random.key(seed)
    ks = jax.random.split(key, 16)
    f = jnp.float32
    nrm = lambda k, shape, scale: jax.random.normal(k, shape, f) * scale
    return {
        'x': nrm(ks[0], (BATCH, SEQ, D_MODEL), 1.0),
        'meta_tokens': nrm(ks[1], (N_META, D_MODEL), 1.0),
        'mix_norm_g': 1.0 + nrm(ks[2], (DEPTH, D_MODEL), 0.02),
        'w_in': nrm(ks[3], (DEPTH, D_MODEL, D_IN), D_MODEL ** -0.5),
        'ret_norm_g': 1.0 + nrm(ks[4], (DEPTH, RET_HEADS, RET_V_DIM), 0.02),
        'q_norm_g': 1.0 + nrm(ks[5], (DEPTH, SWA_HEAD_DIM), 0.02),
        'k_norm_g': 1.0 + nrm(ks[6], (DEPTH, SWA_HEAD_DIM), 0.02),
        'sinks': nrm(ks[7], (DEPTH, SWA_Q_HEADS), 0.5),
        'w_ret_branch': nrm(ks[8], (DEPTH, RET_V_W, D_MODEL), RET_V_W ** -0.5),
        'w_swa_branch': nrm(ks[9], (DEPTH, SWA_Q_W, D_MODEL), SWA_Q_W ** -0.5),
        'w_out': nrm(ks[10], (DEPTH, D_MODEL, D_MODEL), D_MODEL ** -0.5),
        'mlp_norm_g': 1.0 + nrm(ks[11], (DEPTH, D_MODEL), 0.02),
        'w_up': nrm(ks[12], (DEPTH, D_MODEL, D_FF), D_MODEL ** -0.5),
        'w_down': nrm(ks[13], (DEPTH, D_FF, D_MODEL), D_FF ** -0.5),
    }

def reference(x, meta_tokens, mix_norm_g, w_in, ret_norm_g, q_norm_g, k_norm_g, sinks,
              w_ret_branch, w_swa_branch, w_out, mlp_norm_g, w_up, w_down):
    B = x.shape[0]
    meta = jnp.broadcast_to(meta_tokens[None].astype(x.dtype), (B, N_META, D_MODEL))
    h = jnp.concatenate([meta, x], axis=1)
    for layer in range(DEPTH):
        h = h + mixer_layer(h, mix_norm_g[layer], w_in[layer], ret_norm_g[layer], q_norm_g[layer],
                            k_norm_g[layer], sinks[layer], w_ret_branch[layer], w_swa_branch[layer],
                            w_out[layer])
        hn = rms_norm(h, mlp_norm_g[layer])
        h = h + jnp.square(jax.nn.relu(hn @ w_up[layer])) @ w_down[layer]
    return h[:, N_META:]


_drawn_inputs = setup_inputs


def setup_inputs(seed=0):
    import zlib

    import numpy as np

    out = dict(_drawn_inputs(seed))
    spreads = {}
    factors = {'mix_norm_g': 3.69,
     'ret_norm_g': 8.0,
     'q_norm_g': 8.0,
     'k_norm_g': 8.0,
     'sinks': 8.0,
     'mlp_norm_g': 3.228}
    for name, (base, spread) in spreads.items():
        noise = np.random.default_rng([zlib.crc32(name.encode()), seed]).standard_normal(out[name].shape)
        drawn = base * np.exp(spread * noise) if base else spread * noise
        out[name] = __import__('jax').numpy.asarray(drawn.astype(out[name].dtype))
    for name, factor in factors.items():
        out[name] = (out[name] * factor).astype(out[name].dtype)
    return out
```

```python
from contextlib import ExitStack

import numpy as np

import concourse.bass as bass
import concourse.mybir as mybir

F32 = mybir.dt.float32
F32R = mybir.dt.float32r
ALU = mybir.AluOpType
ACT = mybir.ActivationFunctionType
AX_X = mybir.AxisListType.X

P = 128
D = 1024
KT = D // P
T = 1024
NB = T // P
META = 16
SL = 512
HR, RV = 4, 256
HS, HD = 16, 64
NKEY = META + 2 * P
EPS = 1e-6
FF_GROUPS = 4
COL_GR, COL_GS, COL_RG, COL_SQ, COL_KV = 4608, 5632, 2048, 3072, 4096

SLAB_B, SLAB_C, SLAB_D, SLAB_E, SLAB_F, SLAB_H = 4, 6, 9, 13, 17, 19
ACT_B, ACT_C, ACT_D, ACT_H = 32, 48, 72, 104
DVE_F, DVE_H = 32, 48
START = 1
KS_D = [[0, 1, 2], [3, 4, 5], [6, 7]]
SLOPES = [float(2.0 ** (-8.0 * (h + 1) / HS)) for h in range(HS)]
GAMMA = [1.0 - 2.0 ** (-5.0 - h) for h in range(HR)]


def shape_constants():
    ident = np.eye(P, dtype=np.float32)
    i = np.arange(P, dtype=np.float64)
    lg = np.log1p(-(2.0 ** (-5.0 - np.arange(HR, dtype=np.float64))))
    kscale = 128.0 ** -0.5
    mask = (i[:, None] <= i[None, :])[:, None, :] * np.exp(-P * lg)[None, :, None]
    kdec = np.exp(lg[None, :] * (P - 1 - i)[:, None]) * kscale
    kdec_meta = np.zeros((P, HR))
    kdec_meta[:META] = kdec[P - META:]
    qsq = np.exp(2 * lg[None, :] * (i + 1)[:, None]) / RV
    qhalf = 0.5 * np.exp(lg[None, :] * (i + 1)[:, None])
    cols = np.concatenate([kdec, kdec_meta, qsq, qhalf], axis=1)
    dist = np.full((NB + 1, P, NKEY), -1e30)
    for n in range(NB):
        dist[n, :, :META] = -((n + 1) * P + i[:, None] - (P - META + np.arange(META))[None, :])
        own = META + P * (n % 2)
        other = META + P * (1 - n % 2)
        d = i[:, None] - i[None, :]
        dist[n, :, own:own + P] = np.where(d >= 0, -d, -1e30)
        if n > 0:
            d = d + P
            dist[n, :, other:other + P] = np.where(d < P, -d, -1e30)
    f = lambda a: np.ascontiguousarray(a, dtype=np.float32)
    return {"c_ident": f(ident), "c_mask": f(mask.reshape(P, HR * P)), "c_cols": f(cols), "c_dist": f(dist)}


def build(nc, x, meta, g_mix, w_in, g_ret, g_q, g_k, sinks, w_ret, w_swa, w_out, g_mlp, w_up, w_down,
          c_ident, c_mask, c_cols, c_dist, out):
    with ExitStack() as ctx:
        base = (nc.sbuf_base + 63) // 64 * 64
        O_R0, O_R1 = 0, 32768
        O_Q = 2 * KT * (T + META) * 4
        O_V = O_Q + 32768
        O_M = O_V + 32768
        O_WH = O_M + 32768
        O_WL = O_WH + KT * SL * 4
        O_RAW = O_WL + KT * SL * 4
        O_ST = O_RAW + 4 * SL * 4
        O_TB = O_ST + D * 4
        O_ID = O_TB + 2 * SL * 4
        O_SM = O_ID + P * 4
        O_X = O_SM + 1088

        def at(name, off, shape, dt=F32):
            return nc.alloc_sbuf_tensor_at(name, [P, *shape], dt, offset=base + off)

        HN = at("HN", 0, [2, KT, META + T], F32R)
        RT = at("RT", O_Q, [4, NB, SL])
        YR = [at("YR0", O_R0, [2, KT, SL], F32R), at("YR1", O_R1, [2, KT, SL], F32R)]
        YS = [at("YS0", O_V, [2, KT, SL], F32R), at("YS1", O_R0, [2, KT, SL], F32R)]
        HN2 = [at("HN20", O_V, [2, KT, SL], F32R), at("HN21", O_R0, [2, KT, SL], F32R)]
        H1 = at("H1", O_R1, [NB, D])
        MR = at("MR", O_M, [KT, T])
        MG = [at("MGH", O_M, [KT, T], F32R), at("MGL", O_Q, [KT, T], F32R)]
        U = [at("UH", O_M, [KT, T], F32R), at("UL", O_Q, [KT, T], F32R)]
        WH = at("WH", O_WH, [KT, SL], F32R)
        WL = at("WL", O_WL, [KT, SL], F32R)
        RAW = at("RAW", O_RAW, [4, SL])
        ST = at("ST", O_ST, [D])
        TB = at("TB", O_TB, [2, SL])
        IDN = at("IDN", O_ID, [P])
        SS = at("SS", O_SM, [16])
        STD = at("STD", O_SM + 64, [16])
        RSTD = at("RSTD", O_SM + 128, [16])
        SS2 = at("SS2", O_SM + 192, [NB])
        STD2 = at("STD2", O_SM + 224, [NB])
        RSTD2 = at("RSTD2", O_SM + 256, [NB])
        COLS = at("COLS", O_SM + 288, [4, HR])
        SSR = at("SSR", O_SM + 352, [NB, HR])
        SCR = at("SCR", O_SM + 480, [NB, HR])
        EPSC = at("EPSC", O_SM + 608, [1])
        GQK = at("GQK", O_SM + 640, [3])
        SK = at("SK", O_SM + 672, [HS])
        NSK = at("NSK", O_SM + 736, [HS])
        SSM = at("SSM", O_SM + 800, [8])
        GBC = at("GBC", O_M, [D])
        XR = at("XR", O_M + 4096, [4, D])
        MRK = at("MRK", O_M + 24576, [3, SL])
        JUNK = at("JUNK", O_X, [D])
        QS = at("QS", O_M, [SL])
        KD = at("KD", O_M + 2048, [SL])
        QTR = at("QTR", O_M + 4096, [SL])
        KTR = at("KTR", O_M + 6144, [SL])
        SMK = at("SMK", O_M + 8192, [SL])
        STA = at("STA", O_M + 10240, [HR * RV])
        KDM = at("KDM", O_M + 14336, [SL])
        MASK = at("MASK", O_X + 4096, [SL])
        KV = at("KV", O_M, [NB + 1, SL])
        MKV = at("MKV", O_M + 18432, [SL])
        KN = at("KN", O_M + 20480, [256])
        QT = at("QT", O_M + 21504, [8, P])
        KTT = at("KTT", O_M + 25600, [2, NKEY])
        PTS = at("PTS", O_M + 27776, [2, 4, P])
        RSW = at("RSW", O_M + 31872, [NB, 20])
        PR = at("PR", O_X, [2, 2, NKEY])
        PTM = at("PTM", O_X + 4352, [2, 2, P])
        DT = at("DT", O_X + 6400, [2, NKEY])
        MX = at("MX", O_X + 8576, [2, HS])
        NM = at("NM", O_X + 8704, [2, HS])
        SE = at("SE", O_X + 8832, [2, HS])
        RS = at("RS", O_X + 8960, [2, HS])
        ES = at("ES", O_X + 9088, [2, HS])
        GB = at("GB", O_M + 16384, [2, KT, P])
        GBR = at("GBR", O_M + 28672, [D])
        TH = at("TH", O_X, [4, SL])
        GBM = at("GBM", O_X, [D])
        TU = at("TU", O_X + 4096, [2, SL])
        JUNK2 = at("JUNK2", O_X + 4096, [D])

        B = [ctx.enter_context(nc.psum_tensor(f"bank{i}", [P, SL], F32)) for i in range(8)]

        gates = nc.dram_tensor("gates", [6, 2, 4, P, SL], F32, kind="Internal").ap()

        def sem(name):
            return ctx.enter_context(nc.semaphore(name))

        raw_full = [sem(f"raw_full{i}") for i in range(4)]
        w_hi, w_ready, w_free = sem("w_hi"), sem("w_ready"), sem("w_free")
        a_full, a_free, d_full, d_free = sem("a_full"), sem("a_free"), sem("d_full"), sem("d_free")
        id_full, c_full = sem("id_full"), sem("c_full")
        g_full = sem("g_full")
        x_full = [sem(f"x_full{i}") for i in range(4)]
        ss_rdy, std_rdy, rstd_rdy, xn_rdy = sem("ss_rdy"), sem("std_rdy"), sem("rstd_rdy"), sem("xn_rdy")
        xt_full, hn_hi, hn_lo = sem("xt_full"), sem("hn_hi"), sem("hn_lo")
        meta_full, meta_free = sem("meta_full"), sem("meta_free")
        eps_set = sem("eps_set")
        kdm_rdy, kd_rdy, qs_rdy = sem("kdm_rdy"), sem("kd_rdy"), sem("qs_rdy")
        qt_full, kt_full, qT_rdy, kT_rdy = sem("qt_full"), sem("kt_full"), sem("qT_rdy"), sem("kT_rdy")
        s_full, sm_rdy, o_full, u_full = sem("s_full"), sem("sm_rdy"), sem("o_full"), sem("u_full")
        st_rdy, oraw_rdy, sqr_rdy = sem("st_rdy"), sem("oraw_rdy"), sem("sqr_rdy")
        gst_done = [sem("gst_done0"), sem("gst_done1")]
        c_sq, c_red, c_std, c_rstd, scr_step = sem("c_sq"), sem("c_red"), sem("c_std"), sem("c_rstd"), sem("scr_step")
        d_small, d_set = sem("d_small"), sem("d_set")
        mk_rdy, mkt_full, mkT_rdy = sem("mk_rdy"), sem("mkt_full"), sem("mkT_rdy")
        qn_rdy, kn_rdy, aq_full, ak_full = sem("qn_rdy"), sem("kn_rdy"), sem("aq_full"), sem("ak_full")
        aqT_rdy, akT_rdy = sem("aqT_rdy"), sem("akT_rdy")
        sc_full, sc_rdy, mx_rdy, nm_rdy, se_rdy, e_rdy = (sem("sc_full"), sem("sc_rdy"), sem("mx_rdy"), sem("nm_rdy"),
                                                         sem("se_rdy"), sem("e_rdy"))
        pt_full, ptm_full, ptv_rdy, ptm_rdy = sem("pt_full"), sem("ptm_full"), sem("ptv_rdy"), sem("ptm_rdy")
        pv_full, y_rdy, den_rdy = sem("pv_full"), sem("y_rdy"), sem("den_rdy")
        dt_full = [sem("dt_full0"), sem("dt_full1")]
        th_rdy = sem("th_rdy")
        gb_full = [sem("gb_full0"), sem("gb_full1")]
        ysc_rdy, yt_full, yt_rdy, yh_rdy, yl_rdy = sem("ysc_rdy"), sem("yt_full"), sem("yt_rdy"), sem("yh_rdy"), sem("yl_rdy")
        st_full, sh_rdy, ysl_rdy = sem("st_full"), sem("sh_rdy"), sem("ysl_rdy")
        tg_full = [sem(f"tg_full{i}") for i in range(4)]
        e2_sum, e2_hi, e2_step, mg_rdy = sem("e2_sum"), sem("e2_hi"), sem("e2_step"), sem("mg_rdy")
        xres_full = [sem(f"xres_full{i}") for i in range(NB)]
        gm_full = sem("gm_full")
        sq_rdy, uh_rdy, u_rdy = sem("sq_rdy"), sem("uh_rdy"), sem("u_rdy")
        out_done = sem("out_done")

        block = ctx.enter_context(nc.Block())

        @block.sync
        def _(sp):
            def load_slab(slab, source, first=False):
                for k in range(KT):
                    if not (first and k < 4):
                        sp.wait_ge(w_ready, 8 * slab + k - 3)
                    sp.dma_start(RAW[:, k % 4, :], source(k)).then_inc(raw_full[k % 4], 16)

            def w_cols(w, col):
                return lambda k: w[k * P:(k + 1) * P, col:col + SL] if isinstance(col, int) else \
                    w[k * P:(k + 1) * P, bass.ds(col, SL)]

            load_slab(0, w_cols(w_in, 0), first=True)
            with sp.Fori(1, 4) as c:
                load_slab(c, w_cols(w_in, c * SL))
            with sp.Fori(0, 2) as c:
                load_slab(SLAB_B + c, w_cols(w_in, COL_GR + c * SL))
            load_slab(SLAB_C, w_cols(w_in, COL_KV))
            with sp.Fori(0, 2) as c:
                load_slab(SLAB_C + 1 + c, w_cols(w_in, COL_SQ + c * SL))
            with sp.Fori(0, 2) as c:
                load_slab(SLAB_D + c, w_cols(w_in, COL_GS + c * SL))
            with sp.Fori(0, 2) as c:
                load_slab(SLAB_D + 2 + c, w_cols(w_in, COL_RG + c * SL))
            for i, w in enumerate((w_ret, w_swa, w_out)):
                with sp.Fori(0, 2) as c:
                    load_slab(SLAB_E + 2 * i + c, w_cols(w, c * SL))
            with sp.Fori(0, FF_GROUPS) as g:
                for c in range(2):
                    load_slab(SLAB_H + 4 * g + c, w_cols(w_up, g * D + c * SL))
                for c in range(2):
                    load_slab(SLAB_H + 4 * g + 2 + c,
                              lambda k: w_down[bass.ds(g * D + k * P, P), c * SL:(c + 1) * SL])
            for c in range(2):
                for b in range(NB):
                    sp.wait_ge(d_free, DVE_H + 16 * (FF_GROUPS - 1) + 8 * c + b + 1)
                    sp.dma_start(out[b * P:(b + 1) * P, c * SL:(c + 1) * SL],
                                 H1[:, b, c * SL:(c + 1) * SL]).then_inc(out_done, 16)
            sp.wait_ge(out_done, 16 * 2 * NB)

        @block.gpsimd
        def _(pool):
            pool.dma_start(IDN[:, :], c_ident).then_inc(id_full, 16)
            pool.dma_start(GBC[:, :], g_mix.partition_broadcast(P)).then_inc(g_full, 16)

            def load_x(b):
                if b >= 4:
                    pool.wait_ge(xn_rdy, b - 3)
                if b < NB:
                    pool.dma_start(XR[:, b % 4, :], x[b * P:(b + 1) * P, :]).then_inc(x_full[b % 4], 16)
                else:
                    pool.dma_start(XR[0:META, b % 4, :], meta).then_inc(x_full[b % 4], 16)

            for b in range(4):
                load_x(b)
            pool.dma_start(MASK[:, :], c_mask).then_inc(gst_done[0], 16)
            pool.dma_start(COLS[:, :, :], c_cols.rearrange("p (a h) -> p a h", a=4)).then_inc(gst_done[1], 16)
            pool.dma_start(SK[:, :], sinks.partition_broadcast(P)).then_inc(c_full, 16)
            for half in range(2):
                pool.dma_start(GQK[half * HD:(half + 1) * HD, 0:1], g_q).then_inc(c_full, 16)
                pool.dma_start(GQK[half * HD:(half + 1) * HD, 1:2], g_k).then_inc(c_full, 16)
            for b in range(4, NB + 1):
                load_x(b)

            def store_gate(a_index, slab6, gi):
                pool.wait_ge(a_free, a_index + 1)
                pool.dma_start(gates[slab6, gi // 4, gi % 4], TB[:, gi % 2, :]).then_inc(gst_done[gi % 2], 16)

            with pool.Fori(0, 2) as it:
                for gi in range(8):
                    store_gate(ACT_B + 8 * it + gi, it, gi)
            pool.wait_ge(st_rdy, NB + 1)
            pool.wait_ge(sqr_rdy, NB)
            pool.dma_start(DT[:, 0, :], c_dist[0]).then_inc(dt_full[0], 16)
            with pool.Fori(0, 4) as pr:
                for s in range(2):
                    pool.wait_ge(sc_rdy, HS * (2 * pr + s) + START)
                    pool.dma_start(DT[:, 1 - s, :], c_dist[2 * pr + s + 1]).then_inc(dt_full[1 - s], 16)
                    for q in range(4):
                        store_gate(ACT_D + 8 * pr + 4 * s + q, 2 + pr, 4 * s + q)
            pool.wait_ge(gst_done[0], 16 * (24 + START))
            pool.wait_ge(gst_done[1], 16 * (24 + START))
            pool.wait_ge(y_rdy, 8 * NB + START)
            pool.wait_ge(dt_full[0], 16 * 5)
            pool.dma_start(GBR[:, :], g_ret.partition_broadcast(P)).then_inc(gm_full, 16)

            def load_tg(i):
                if i >= 4:
                    pool.wait_ge(d_free, i - 3)
                pool.dma_start(TH[:, i % 4, :], gates[i // 8, (i // 4) % 2, i % 4]).then_inc(tg_full[i % 4], 16)

            def load_gb(b):
                if b >= 2:
                    pool.wait_ge(yt_rdy, 2 * (b - 1))
                for c in range(2):
                    pool.dma_start(GB[:, b % 2, 4 * c:4 * c + 4, :],
                                   gates[4 + c, b // 4, :, :, (b % 4) * P:(b % 4 + 1) * P].rearrange(
                                       "f p t -> p f t")).then_inc(gb_full[b % 2], 16)

            for b in range(4):
                load_gb(b)
            for i in range(4):
                load_tg(i)
            for b in range(4, NB):
                load_gb(b)
                load_tg(b)
            for i in range(NB, 16):
                load_tg(i)
            pool.wait_ge(d_full, 16)
            for b in range(NB):
                pool.dma_start(H1[:, b, :], x[b * P:(b + 1) * P, :]).then_inc(xres_full[b], 16)
            for i in range(16, 32):
                load_tg(i)
            pool.wait_ge(d_free, DVE_F)
            pool.dma_start(GBM[:, :], g_mlp.partition_broadcast(P)).then_inc(gm_full, 16)

        @block.tensor
        def _(pe):
            for one in (qt_full, kt_full, s_full, o_full, sc_full, pv_full, aq_full, ak_full):
                pe.sem_inc(one, START)
            def three(bank, ahi, alo, bhi, blo, first, last, frees):
                mm = pe.matmul(bank, ahi, bhi, start=first, stop=False)
                if frees:
                    mm.then_inc(w_free, 1)
                pe.matmul(bank, alo, bhi, start=False, stop=False)
                return pe.matmul(bank, ahi, blo, start=False, stop=last)

            def step(form, bank, k, f, act, slab, opening, closing):
                if opening:
                    pe.wait_ge(w_ready, 8 * slab + k + 1)
                frees = opening and k == 0 and not (isinstance(slab, int) and slab == 0)
                hi, lo = act(k)
                if form == "S":
                    fs = slice(f * P, (f + 1) * P)
                    mm = three(bank[:, :], WH[:, k, fs], WL[:, k, fs], hi, lo, k == 0, k == KT - 1, frees)
                else:
                    mm = three(bank[:, :], hi, lo, WH[:, k, :], WL[:, k, :], k == 0, k == KT - 1, frees)
                if closing and k < KT - 1:
                    mm.then_inc(w_free, 1)
                return mm

            def hn_block(b):
                lo = META + b * P
                return lambda k: (HN[:, 0, k, lo:lo + P], HN[:, 1, k, lo:lo + P])

            def hn_meta(k):
                return HN[:, 0, k, 0:P], HN[:, 1, k, 0:P]

            def hn_half(half):
                lo = META + half * SL
                return lambda k: (HN[:, 0, k, lo:lo + SL], HN[:, 1, k, lo:lo + SL])

            def halves(pair, half):
                return lambda k: (pair[half][:, 0, k, :], pair[half][:, 1, k, :])

            def tokens(pair, b):
                return lambda k: (pair[0][:, k, b * P:(b + 1) * P], pair[1][:, k, b * P:(b + 1) * P])

            def bank_wait(j, loop=False):
                if loop or j >= 2:
                    pe.wait_ge(a_free, j - 1)

            def dense_a(form, j, bank, f, act, slab, opening, closing, loop=True, middle=None):
                bank_wait(j, loop)
                for k in range(KT):
                    mm = step(form, bank, k, f, act, slab, opening, closing)
                    if middle and k == 3:
                        middle()
                mm.then_inc(a_full, 1)

            pe.wait_ge(id_full, 16)

            def transpose_x(b):
                pe.wait_ge(xn_rdy, b + 1)
                if b >= 1:
                    pe.wait_ge(hn_lo, 2 * b)
                rows, w = (P, P) if b < NB else (META, META)
                for k in range(KT):
                    bank = B[2 + k // 4]
                    mm = pe.transpose(bank[:, (k % 4) * w:(k % 4) * w + w], ST[0:rows, k * P:(k + 1) * P],
                                      IDN[0:rows, 0:rows])
                    if k % 4 == 3:
                        mm.then_inc(xt_full, 1)

            transpose_x(0)
            for b in range(NB):
                pe.wait_ge(hn_lo, 2 * (b + 1))
                dense_a("M", b, B[b % 2], 0, hn_block(b), 0, b == 0, b == NB - 1, loop=False,
                        middle=lambda b=b: transpose_x(b + 1))
            pe.wait_ge(hn_lo, 2 * (NB + 1))
            with pe.Fori(1, 4) as c:
                for b in range(NB):
                    dense_a("M", 8 * c + b, B[b % 2], 0, hn_block(b), c, b == 0, False)
                pe.wait_ge(meta_free, c - 1 + START)
                for k in range(KT):
                    mm = step("M", B[6], k, 0, hn_meta, c, False, True)
                mm.then_inc(meta_full, 1)

            pe.wait_ge(kdm_rdy, 1)
            pe.wait_ge(meta_free, 3 + START)
            for h in range(HR):
                mm = pe.matmul(B[6 + h // 2][:, (h % 2) * RV:(h % 2 + 1) * RV], KDM[0:META, h * P:(h + 1) * P],
                               MRK[0:META, 1 + h // 2, (h % 2) * RV:(h % 2 + 1) * RV], start=True, stop=True)
            mm.then_inc(u_full, 1)
            with pe.Fori(0, 2) as it:
                for r in range(4):
                    n = 4 * it + r

                    def weave(slot):
                        gi = 2 * r + slot // 2
                        j = ACT_B + 8 * it + gi
                        if slot % 2 == 0:
                            pe.wait_ge(a_free, j - 1)
                        for k in range(4 * (slot % 2), 4 * (slot % 2) + 4):
                            mm = step("S", B[gi % 2], k, gi % 4, hn_half(gi // 4), SLAB_B + it, gi == 0, gi == 7)
                        if slot % 2 == 1:
                            mm.then_inc(a_full, 1)

                    weave(0)
                    pe.wait_ge(qs_rdy, n + 1)
                    pe.wait_ge(sm_rdy, n + START)
                    for h in range(HR):
                        mm = pe.transpose(B[2][:, h * P:(h + 1) * P], QS[:, h * P:(h + 1) * P], IDN[:, :])
                    mm.then_inc(qt_full, 1)
                    pe.wait_ge(kd_rdy, n + 1)
                    pe.wait_ge(kT_rdy, n + START)
                    for h in range(HR):
                        mm = pe.transpose(B[3][:, h * P:(h + 1) * P], KD[:, h * P:(h + 1) * P], IDN[:, :])
                    mm.then_inc(kt_full, 1)
                    weave(1)
                    pe.wait_ge(qT_rdy, n + 1)
                    pe.wait_ge(kT_rdy, n + 1 + START)
                    for h in range(HR):
                        mm = pe.matmul(B[2][:, h * P:(h + 1) * P], KTR[:, h * P:(h + 1) * P],
                                       QTR[:, h * P:(h + 1) * P], start=True, stop=True)
                    mm.then_inc(s_full, 1)
                    pe.wait_ge(st_rdy, n + 1)
                    for h in range(HR):
                        mm = pe.matmul(B[6 + h // 2][:, (h % 2) * RV:(h % 2 + 1) * RV], KD[:, h * P:(h + 1) * P],
                                       RT[:, 2 + h // 2, n, (h % 2) * RV:(h % 2 + 1) * RV], start=True, stop=True)
                    mm.then_inc(u_full, 1)
                    weave(2)
                    pe.wait_ge(sm_rdy, n + 1 + START)
                    pe.wait_ge(oraw_rdy, n + START)
                    for h in range(HR):
                        o = B[4 + h // 2][:, (h % 2) * RV:(h % 2 + 1) * RV]
                        pe.matmul(o, SMK[:, h * P:(h + 1) * P],
                                  RT[:, 2 + h // 2, n, (h % 2) * RV:(h % 2 + 1) * RV], start=True, stop=False)
                        mm = pe.matmul(o, QTR[:, h * P:(h + 1) * P], STA[:, h * RV:(h + 1) * RV],
                                       start=False, stop=True)
                    mm.then_inc(o_full, 1)
                    weave(3)

            for b in range(NB):
                dense_a("M", ACT_C + b, B[b % 2], 0, hn_block(b), SLAB_C, b == 0, False)
            pe.wait_ge(st_rdy, NB + 1)
            for k in range(KT):
                mm = step("M", B[6], k, 0, hn_meta, SLAB_C, False, True)
            mm.then_inc(meta_full, 1)
            with pe.Fori(0, 2) as c:
                for b in range(NB):
                    dense_a("M", ACT_C + 8 + 8 * c + b, B[b % 2], 0, hn_block(b), SLAB_C + 1 + c, b == 0, b == NB - 1)

            pe.wait_ge(mk_rdy, 1)
            for t in range(2):
                mm = pe.transpose(B[6][:, t * META:(t + 1) * META], ST[0:META, t * P:(t + 1) * P],
                                  IDN[0:META, 0:META])
            mm.then_inc(mkt_full, 1)
            pe.wait_ge(mkT_rdy, 1)
            for kind in range(2):
                with pe.Fori(2 * kind, 2 * kind + 2) as pr:
                    for s in range(2):
                        n = 2 * pr + s

                        def weave(t):
                            q = t // 3
                            j = ACT_D + 8 * pr + 4 * s + q
                            if t % 3 == 0:
                                pe.wait_ge(a_free, j - 1)
                            for k in KS_D[t % 3]:
                                mm = step("S", B[q % 2], k, q, hn_half(s), SLAB_D + pr, s == 0 and q == 0,
                                          s == 1 and q == 3)
                            if t % 3 == 2:
                                mm.then_inc(a_full, 1)

                        for t in range(12):
                            weave(t)
                            if t == 0:
                                pe.wait_ge(qn_rdy, n + 1)
                                pe.wait_ge(ptv_rdy, 8 * n + START)
                                for j in range(8):
                                    mm = pe.transpose(B[4 + j // 4][:, (j % 4) * P:(j % 4 + 1) * P],
                                                      ST[:, j * P:(j + 1) * P], IDN[:, :])
                                    if j % 4 == 3:
                                        mm.then_inc(aq_full, 1)
                                pe.wait_ge(kn_rdy, n + 1)
                                pe.wait_ge(ptm_rdy, 8 * n + START)
                                for j in range(2):
                                    mm = pe.transpose(B[6][:, j * P:(j + 1) * P], KN[:, j * P:(j + 1) * P], IDN[:, :])
                                mm.then_inc(ak_full, 1)
                            if 3 <= t <= 10:
                                p = t - 3
                                pe.wait_ge(e_rdy, 8 * n + p + 1)
                                if p >= 2:
                                    pe.wait_ge(ptv_rdy, 8 * n + p - 1 + START)
                                for hl in range(2):
                                    for sl in range(2):
                                        c = 2 * hl + sl
                                        mm = pe.transpose(B[4 + p % 2][:, c * P:(c + 1) * P],
                                                          PR[:, p % 2, hl, META + sl * P:META + (sl + 1) * P], IDN[:, :])
                                mm.then_inc(pt_full, 1)
                                if p >= 1:
                                    pe.wait_ge(ptm_rdy, 8 * n + p + START)
                                for hl in range(2):
                                    mm = pe.transpose(B[6][0:META, hl * P:(hl + 1) * P], PR[:, p % 2, hl, 0:META],
                                                      IDN[:, :])
                                mm.then_inc(ptm_full, 1)
                            if 1 <= t <= 8:
                                p = t - 1
                                if p == 0:
                                    pe.wait_ge(aqT_rdy, 2 * n + 2)
                                    pe.wait_ge(akT_rdy, n + 1)
                                for hh in (2 * p, 2 * p + 1):
                                    g = hh // 4
                                    row, tile = HD * (g % 2), 4 * (g // 2) + hh % 4
                                    if hh > 0:
                                        pe.wait_ge(sc_rdy, HS * n + hh - 1 + START)
                                    pe.matmul(B[2 + hh % 2][:, 0:NKEY], QT[row:row + HD, tile, :],
                                              KTT[row:row + HD, g // 2, :], start=True, stop=True).then_inc(sc_full, 1)
                            if t >= 4:
                                p = t - 4
                                pe.wait_ge(ptv_rdy, 8 * n + p + 1 + START)
                                pe.wait_ge(ptm_rdy, 8 * n + p + 1 + START)
                                pe.wait_ge(y_rdy, 8 * n + p + START)
                                for hl in range(2):
                                    g = (2 * p + hl) // 4
                                    vs = slice(256 + g * HD, 256 + (g + 1) * HD)
                                    o = B[7][:, hl * HD:(hl + 1) * HD]
                                    for sl in range(2):
                                        blk = n + 1 if sl == s else n
                                        pe.matmul(o, PTS[:, p % 2, 2 * hl + sl, :], KV[:, blk, vs],
                                                  start=sl == 0, stop=False)
                                    mm = pe.matmul(o, PTM[0:META, p % 2, hl, :], MKV[0:META, vs],
                                                   start=False, stop=True)
                                mm.then_inc(pv_full, 1)

            def transpose_yr(b):
                pe.wait_ge(ysc_rdy, b + 1)
                if b >= 1:
                    pe.wait_ge(yt_rdy, 2 * b)
                for k in range(KT):
                    mm = pe.transpose(B[2 + k // 4][:, (k % 4) * P:(k % 4 + 1) * P], ST[:, k * P:(k + 1) * P], IDN[:, :])
                    if k % 4 == 3:
                        mm.then_inc(yt_full, 1)

            def transpose_ys(b):
                if b >= 1:
                    pe.wait_ge(ysl_rdy, 2 * b)
                for k in range(KT):
                    mm = pe.transpose(B[4 + k // 4][:, (k % 4) * P:(k % 4 + 1) * P],
                                      RT[:, k // 4, b, (k % 4) * P:(k % 4 + 1) * P], IDN[:, :])
                    if k % 4 == 3:
                        mm.then_inc(st_full, 1)

            pe.wait_ge(y_rdy, 8 * NB + START)
            for b in range(4):
                transpose_yr(b)
            for j in range(32):
                branch, c, half, f = j // 16, (j // 8) % 2, (j // 4) % 2, j % 4
                slab = SLAB_E + 2 * branch + c
                if j >= 2:
                    pe.wait_ge(d_free, j - 1)
                if branch == 0 and c == 0 and f == 0:
                    pe.wait_ge(yl_rdy, 8 * (half + 1))
                if branch == 1 and c == 0 and f == 0:
                    pe.wait_ge(ysl_rdy, 8 * (half + 1))
                act = halves(YR if branch == 0 else YS, half)
                for k in range(KT):
                    mm = step("S", B[6 + j % 2], k, f, act, slab, half == 0 and f == 0, half == 1 and f == 3)
                    if k == 3:
                        if j < 4:
                            transpose_yr(4 + j)
                        elif j < 8:
                            transpose_ys(j - 4)
                        elif 12 <= j < 16:
                            transpose_ys(j - 8)
                mm.then_inc(d_full, 1)

            def transpose_h(b):
                pe.wait_ge(xn_rdy, NB + 1 + b + 1)
                pe.wait_ge(hn_lo, 2 * (NB + 1) + 2 * b)
                for k in range(KT):
                    mm = pe.transpose(B[2 + k // 4][:, (k % 4) * P:(k % 4 + 1) * P], ST[:, k * P:(k + 1) * P], IDN[:, :])
                    if k % 4 == 3:
                        mm.then_inc(xt_full, 1)

            for c in range(2):
                for b in range(NB):
                    j = DVE_F + 8 * c + b
                    pe.wait_ge(d_free, j - 1)
                    if c == 0:
                        pe.wait_ge(mg_rdy, 12 if b < 4 else 16)
                    for k in range(KT):
                        mm = step("M", B[6 + j % 2], k, 0, tokens(MG, b), SLAB_F + c, b == 0, b == NB - 1)
                        if k == 3 and c == 1 and b >= 2:
                            transpose_h(b - 2)
                    mm.then_inc(d_full, 1)
            transpose_h(NB - 2)
            transpose_h(NB - 1)
            pe.wait_ge(hn_lo, 2 * (NB + 1) + 2 * NB)

            with pe.Fori(0, FF_GROUPS) as g:
                for c in range(2):
                    for gi in range(8):
                        dense_a("S", ACT_H + 16 * g + 8 * c + gi, B[gi % 2], gi % 4, halves(HN2, gi // 4),
                                SLAB_H + 4 * g + c, gi == 0, gi == 7)
                for c in range(2):
                    for b in range(NB):
                        j = DVE_H + 16 * g + 8 * c + b
                        pe.wait_ge(d_free, j - 1)
                        if c == 0:
                            pe.wait_ge(u_rdy, 16 * g + (12 if b < 4 else 16) + START)
                        for k in range(KT):
                            mm = step("M", B[6 + b % 2], k, 0, tokens(U, b), SLAB_H + 4 * g + 2 + c, b == 0, b == NB - 1)
                        mm.then_inc(d_full, 1)

        @block.scalar
        def _(act):
            for one in (meta_free, ptv_rdy):
                act.sem_inc(one, START)
            def split_hi(slab, k, first=False):
                act.wait_ge(raw_full[k % 4], 16 * (2 * slab + k // 4 + 1))
                if not first:
                    act.wait_ge(w_free, 8 * slab + k - 7)
                act.copy(WH[:, k, :], RAW[:, k % 4, :]).then_inc(w_hi, 1)

            def next_hi(slab):
                for k in range(KT - 1):
                    split_hi(slab, k)

            def square_x(b):
                rows = P if b < NB else META
                act.wait_ge(x_full[b % 4], 16 * (b // 4 + 1))
                act.activation(JUNK[0:rows, :], XR[0:rows, b % 4, :], ACT.Square,
                               accum_out=SS[0:rows, b:b + 1]).then_inc(ss_rdy, 1)
                act.wait_ge(ss_rdy, b + 1)
                act.activation(STD[0:rows, b:b + 1], SS[0:rows, b:b + 1], ACT.Sqrt, scale=1.0 / D,
                               bias=EPSC[0:rows, 0:1]).then_inc(std_rdy, 1)

            def hi_x(b):
                for u in range(2):
                    act.wait_ge(xt_full, 2 * b + u + 1)
                    if b < NB:
                        lo, w = META + b * P, P
                    else:
                        lo, w = 0, META
                    act.copy(HN[:, 0, 4 * u:4 * u + 4, lo:lo + w],
                             B[2 + u][:, 0:4 * w].rearrange("p (k t) -> p k t", k=4)).then_inc(hn_hi, 1)

            act.wait_ge(eps_set, 1)
            square_x(0)
            for k in range(4):
                split_hi(0, k, first=True)
            hi_x(0)
            for k in range(4, KT):
                split_hi(0, k, first=True)
            square_x(1)
            for b in range(NB):
                hi_x(b + 1)
                if b + 2 <= NB:
                    square_x(b + 2)
                if b == NB - 1:
                    next_hi(1)
                act.wait_ge(a_full, b + 1)
                act.copy(RT[:, 0, b, :], B[b % 2][:, :]).then_inc(a_free, 1)
            with act.Fori(1, 4) as c:
                split_hi(c, KT - 1)
                for b in range(NB):
                    act.wait_ge(a_full, 8 * c + b + 1)
                    act.copy(RT[:, c, b, :], B[b % 2][:, :]).then_inc(a_free, 1)
                next_hi(c + 1)
                act.wait_ge(meta_full, c)
                act.copy(MRK[0:META, c - 1, :], B[6][0:META, :]).then_inc(meta_free, 1)

            def tanh_gate(j, gi, uses):
                act.wait_ge(a_full, j + 1)
                act.wait_ge(gst_done[gi % 2], 16 * (uses + START))
                return act.activation(TB[:, gi % 2, :], B[gi % 2][:, :], ACT.Tanh, scale=0.5)

            with act.Fori(0, 2) as it:
                for r in range(4):
                    n = 4 * it + r
                    if r == 0:
                        split_hi(SLAB_B + it, KT - 1)
                    act.wait_ge(qt_full, n + START)
                    act.copy(QS[:, :], RT[:, 0, n, :]).then_inc(qs_rdy, 1)
                    act.wait_ge(qt_full, n + 1 + START)
                    act.wait_ge(o_full, n + START)
                    act.copy(QTR[:, :], B[2][:, :]).then_inc(qT_rdy, 1)
                    tanh_gate(ACT_B + 8 * it + 2 * r, 2 * r, 4 * it + r).then_inc(a_free, 1)
                    if r == 3:
                        for k in range(4):
                            split_hi(SLAB_B + it + 1, k)
                    act.wait_ge(oraw_rdy, n + 1 + START)
                    for h in range(HR):
                        sq = act.activation(JUNK[:, h * RV:(h + 1) * RV],
                                            RT[:, 2 + h // 2, n, (h % 2) * RV:(h % 2 + 1) * RV],
                                            ACT.Square, accum_out=SSR[:, n, h:h + 1])
                    sq.then_inc(sqr_rdy, 1)
                    if r == 3:
                        for k in range(4, KT - 1):
                            split_hi(SLAB_B + it + 1, k)
                    tanh_gate(ACT_B + 8 * it + 2 * r + 1, 2 * r + 1, 4 * it + r).then_inc(a_free, 1)

            act.wait_ge(st_rdy, NB + 1)
            split_hi(SLAB_C, KT - 1)
            for b in range(NB):
                act.wait_ge(a_full, ACT_C + b + 1)
                act.copy(KV[:, b + 1, :], B[b % 2][:, :])
                if b >= 2:
                    act.wait_ge(c_red, b - 1)
                act.activation(ST[:, (b % 2) * SL:(b % 2) * SL + 256], B[b % 2][:, 0:256], ACT.Square)\
                   .then_inc(a_free, 1)
            next_hi(SLAB_C + 1)
            act.wait_ge(meta_full, 4)
            act.copy(MKV[0:META, :], B[6][0:META, :]).then_inc(meta_free, 1)
            act.wait_ge(c_red, NB - 1)
            act.activation(ST[0:META, 0:256], B[6][0:META, 0:256], ACT.Square).then_inc(c_sq, 1)
            with act.Fori(0, 2) as c:
                split_hi(SLAB_C + 1 + c, KT - 1)
                for b in range(NB):
                    if b == NB - 1:
                        next_hi(SLAB_C + 2 + c)
                    act.wait_ge(a_full, ACT_C + 8 + 8 * c + b + 1)
                    act.copy(RT[:, c, b, :], B[b % 2][:, :])
                    act.wait_ge(c_red, 8 * c + b + 8)
                    act.activation(ST[:, ((b + 1) % 2) * SL:((b + 1) % 2 + 1) * SL], B[b % 2][:, :], ACT.Square)\
                       .then_inc(a_free, 1)
            act.wait_ge(c_red, 25)
            act.activation(RSW[:, :, :], RSW[:, :, :], ACT.Sqrt, scale=1.0 / HD, bias=EPSC[:, 0:1]).then_inc(c_std, 1)
            act.activation(SSM[0:META, 0:4], SSM[0:META, 0:4], ACT.Sqrt, scale=1.0 / HD,
                           bias=EPSC[0:META, 0:1]).then_inc(c_std, 1)
            act.wait_ge(scr_step, 1)
            act.activation(SCR[:, :, :], SCR[:, :, :], ACT.Sqrt, bias=EPSC[:, 0:1]).then_inc(c_std, 1)

            act.wait_ge(d_set, 1)
            for kind in range(2):
                with act.Fori(2 * kind, 2 * kind + 2) as pr:
                    for s in range(2):
                        n = 2 * pr + s
                        for t in range(12):
                            if t == 0 and s == 0:
                                split_hi(SLAB_D + pr, KT - 1)
                            if t == 0:
                                act.wait_ge(sc_full, HS * n + START)
                                for u in range(2):
                                    act.wait_ge(aq_full, 2 * n + u + 1 + START)
                                    act.activation(QT[:, 4 * u:4 * u + 4, :],
                                                   B[4 + u][:, :].rearrange("p (k t) -> p k t", k=4), ACT.Copy,
                                                   scale=GQK[:, 2:3]).then_inc(aqT_rdy, 1)
                            if 3 <= t <= 10:
                                p = t - 3
                                act.wait_ge(pt_full, 8 * n + p + 1)
                                act.wait_ge(pv_full, 8 * n + max(p - 1, 0) + START)
                                act.copy(PTS[:, p % 2, :, :],
                                         B[4 + p % 2][:, :].rearrange("p (k t) -> p k t", k=4)).then_inc(ptv_rdy, 1)
                            if 2 <= t <= 9:
                                p = t - 2
                                act.wait_ge(nm_rdy, 8 * n + p + 1)
                                act.wait_ge(se_rdy, 8 * n + p + 1)
                                act.activation(ES[:, s, 2 * p:2 * p + 2], SE[:, s, 2 * p:2 * p + 2], ACT.Exp)
                                for hl in range(2):
                                    hh = 2 * p + hl
                                    e = act.activation(PR[:, p % 2, hl, :], PR[:, p % 2, hl, :], ACT.Exp,
                                                       bias=NM[:, s, hh:hh + 1], accum_out=RS[:, s, hh:hh + 1])
                                e.then_inc(e_rdy, 1)
                            if s == 1 and t >= 9:
                                for k in KS_D[t - 9]:
                                    if k < KT - 1:
                                        split_hi(SLAB_D + pr + 1, k)
                            if t % 3 == 2:
                                q = t // 3
                                g = tanh_gate(ACT_D + 8 * pr + 4 * s + q, 4 * s + q, 8 + 4 * pr + 2 * s + q // 2)
                                g.then_inc(a_free if kind == 0 else th_rdy, 1)

            def hi_yr(b):
                for u in range(2):
                    act.wait_ge(yt_rdy, 2 * b + u + 1)
                    act.copy(YR[b // 4][:, 0, 4 * u:4 * u + 4, (b % 4) * P:(b % 4 + 1) * P],
                             TB[:, u, :].rearrange("p (k t) -> p k t", k=4)).then_inc(yh_rdy, 1)

            def hi_ys(b):
                if b == 4:
                    act.wait_ge(d_full, 12)
                if b == 0:
                    act.wait_ge(ysc_rdy, NB)
                for u in range(2):
                    act.wait_ge(st_full, 2 * b + u + 1)
                    act.copy(YS[b // 4][:, 0, 4 * u:4 * u + 4, (b % 4) * P:(b % 4 + 1) * P],
                             B[4 + u][:, :].rearrange("p (k t) -> p k t", k=4)).then_inc(sh_rdy, 1)

            for b in range(4):
                hi_yr(b)
            for j in range(32):
                if j % 8 == 0:
                    split_hi(SLAB_E + j // 8, KT - 1)
                if j < 4:
                    hi_yr(4 + j)
                elif j < 8:
                    hi_ys(j - 4)
                elif 12 <= j < 16:
                    hi_ys(j - 8)
                if j % 8 == 7:
                    next_hi(SLAB_E + j // 8 + 1)
                if j >= 16:
                    i = j - 16
                    f, half = 4 * (i // 8) + i % 4, (i // 4) % 2
                    act.wait_ge(e2_sum, i + 1)
                    act.copy(MG[0][:, f, half * SL:(half + 1) * SL], TB[:, 1, :]).then_inc(e2_hi, 1)

            def hi_h(b):
                for u in range(2):
                    act.wait_ge(xt_full, 2 * (NB + 1) + 2 * b + u + 1)
                    act.copy(HN2[b // 4][:, 0, 4 * u:4 * u + 4, (b % 4) * P:(b % 4 + 1) * P],
                             B[2 + u][:, :].rearrange("p (k t) -> p k t", k=4)).then_inc(hn_hi, 1)

            def square_h(b):
                act.wait_ge(d_free, DVE_F + 8 + b + 1)
                act.activation(JUNK2[:, :], H1[:, b, :], ACT.Square, accum_out=SS2[:, b:b + 1]).then_inc(ss_rdy, 1)
                act.wait_ge(ss_rdy, NB + 1 + b + 1)
                act.activation(STD2[:, b:b + 1], SS2[:, b:b + 1], ACT.Sqrt, scale=1.0 / D,
                               bias=EPSC[:, 0:1]).then_inc(std_rdy, 1)

            split_hi(SLAB_F, KT - 1)
            next_hi(SLAB_F + 1)
            split_hi(SLAB_F + 1, KT - 1)
            for b in range(NB):
                if b >= 2:
                    hi_h(b - 2)
                if b == NB - 1:
                    next_hi(SLAB_H)
                square_h(b)
            hi_h(NB - 2)
            hi_h(NB - 1)

            def mlp(g, last):
                for c in range(2):
                    split_hi(SLAB_H + 4 * g + c, KT - 1)
                    for gi in range(8):
                        if gi == 7:
                            next_hi(SLAB_H + 4 * g + c + 1)
                        i = 16 * g + 8 * c + gi
                        act.wait_ge(a_full, ACT_H + i + 1)
                        act.wait_ge(u_rdy, 16 * g + max(8 * c + gi - 1, 0) + START)
                        act.activation(TB[:, gi % 2, :], B[gi % 2][:, :], ACT.Relu).then_inc(a_free, 1)
                        act.wait_ge(sq_rdy, i + 1)
                        act.copy(U[0][:, 4 * c + gi % 4, (gi // 4) * SL:(gi // 4 + 1) * SL], TU[:, gi % 2, :])\
                           .then_inc(uh_rdy, 1)
                for c in range(2):
                    split_hi(SLAB_H + 4 * g + 2 + c, KT - 1)
                    if not (last and c == 1):
                        next_hi(SLAB_H + 4 * g + 3 + c)

            with act.Fori(0, FF_GROUPS - 1) as g:
                mlp(g, False)
            mlp(FF_GROUPS - 1, True)

        @block.vector
        def _(dve):
            for one in (sm_rdy, kT_rdy, oraw_rdy, ptm_rdy, y_rdy, sc_rdy, u_rdy):
                dve.sem_inc(one, START)
            def split_lo(slab, k):
                dve.wait_ge(w_hi, 8 * slab + k + 1)
                dve.tensor_tensor(WL[:, k, :], RAW[:, k % 4, :], WH[:, k, :].bitcast(F32), ALU.subtract)\
                   .then_inc(w_ready, 1)

            def next_lo(slab):
                for k in range(KT - 1):
                    split_lo(slab, k)

            dve.memset(EPSC[:, :], EPS).then_inc(eps_set, 1)

            def norm_x(b):
                rows = P if b < NB else META
                dve.wait_ge(std_rdy, b + 1)
                dve.reciprocal(RSTD[0:rows, b:b + 1], STD[0:rows, b:b + 1]).then_inc(rstd_rdy, 1)
                dve.wait_ge(rstd_rdy, b + 1)
                if b == 0:
                    dve.wait_ge(g_full, 16)
                if b >= 1:
                    dve.wait_ge(xt_full, 2 * b)
                dve.scalar_tensor_tensor(out=ST[0:rows, :], in0=XR[0:rows, b % 4, :], scalar=RSTD[0:rows, b:b + 1],
                                         in1=GBC[0:rows, :], op0=ALU.mult, op1=ALU.mult).then_inc(xn_rdy, 1)

            def lo_x(b):
                for u in range(2):
                    dve.wait_ge(hn_hi, 2 * b + u + 1)
                    if b < NB:
                        lo, w = META + b * P, P
                    else:
                        lo, w = 0, META
                    dve.tensor_tensor(HN[:, 1, 4 * u:4 * u + 4, lo:lo + w],
                                      B[2 + u][:, 0:4 * w].rearrange("p (k t) -> p k t", k=4),
                                      HN[:, 0, 4 * u:4 * u + 4, lo:lo + w].bitcast(F32), ALU.subtract)\
                       .then_inc(hn_lo, 1)

            norm_x(0)
            for k in range(4):
                split_lo(0, k)
            lo_x(0)
            for k in range(4, KT):
                split_lo(0, k)
            norm_x(1)
            for b in range(NB):
                lo_x(b + 1)
                if b + 2 <= NB:
                    norm_x(b + 2)
            next_lo(1)
            with dve.Fori(1, 4) as c:
                split_lo(c, KT - 1)
                next_lo(c + 1)

            def heads(ap, n=HR):
                return ap.rearrange("p (h d) -> p h d", h=n)

            dve.wait_ge(meta_free, 3 + START)
            dve.wait_ge(c_full, 16 * 5)
            dve.wait_ge(gst_done[0], 16)
            dve.wait_ge(gst_done[1], 16)
            dve.tensor_tensor(heads(KDM[0:META, :]), heads(MRK[0:META, 0, :]),
                              COLS[0:META, 1, :].unsqueeze(2).to_broadcast([META, HR, P]), ALU.mult)\
               .then_inc(kdm_rdy, 1)
            dve.wait_ge(u_full, 1)
            dve.tensor_copy(STA[:, 0:SL], B[6][:, :])
            dve.tensor_copy(STA[:, SL:2 * SL], B[7][:, :]).then_inc(st_rdy, 1)
            with dve.Fori(0, 2) as it:
                for r in range(4):
                    n = 4 * it + r
                    if r == 0:
                        split_lo(SLAB_B + it, KT - 1)
                    dve.wait_ge(kt_full, n + START)
                    dve.wait_ge(u_full, n + 1)
                    dve.tensor_tensor(heads(KD[:, :]), heads(RT[:, 1, n, :]),
                                      COLS[:, 0, :].unsqueeze(2).to_broadcast([P, HR, P]), ALU.mult)\
                       .then_inc(kd_rdy, 1)
                    dve.wait_ge(kt_full, n + 1 + START)
                    dve.wait_ge(s_full, n + START)
                    dve.tensor_copy(KTR[:, :], B[3][:, :]).then_inc(kT_rdy, 1)
                    dve.wait_ge(s_full, n + 1 + START)
                    dve.wait_ge(o_full, n + START)
                    dve.tensor_tensor(SMK[:, :], B[2][:, :], MASK[:, :], ALU.mult).then_inc(sm_rdy, 1)
                    if r == 3:
                        for k in range(4):
                            split_lo(SLAB_B + it + 1, k)
                    dve.wait_ge(o_full, n + 1 + START)
                    dve.wait_ge(u_full, n + 2)
                    for c in range(2):
                        cp = dve.tensor_copy(RT[:, 2 + c, n, :], B[4 + c][:, :])
                    cp.then_inc(oraw_rdy, 1)
                    for h in range(HR):
                        cp = dve.scalar_tensor_tensor(out=STA[:, h * RV:(h + 1) * RV], in0=STA[:, h * RV:(h + 1) * RV],
                                                      scalar=float(GAMMA[h] ** P),
                                                      in1=B[6 + h // 2][:, (h % 2) * RV:(h % 2 + 1) * RV],
                                                      op0=ALU.mult, op1=ALU.add)
                    cp.then_inc(st_rdy, 1)
                    if r == 3:
                        for k in range(4, KT - 1):
                            split_lo(SLAB_B + it + 1, k)

            def reduce_c(outap, inap):
                dve.tensor_reduce(outap, inap, AX_X, ALU.add).then_inc(c_red, 1)

            dve.memset(KV[:, 0, :], 0.0).then_inc(d_small, 1)
            split_lo(SLAB_C, KT - 1)
            for b in range(NB):
                dve.wait_ge(a_free, ACT_C + b + 1)
                reduce_c(RSW[:, b, 16:20], heads(ST[:, (b % 2) * SL:(b % 2) * SL + 256]))
            next_lo(SLAB_C + 1)
            dve.wait_ge(c_sq, 1)
            reduce_c(SSM[0:META, 0:4], heads(ST[0:META, 0:256]))
            with dve.Fori(0, 2) as c:
                split_lo(SLAB_C + 1 + c, KT - 1)
                for b in range(NB):
                    if b == NB - 1:
                        next_lo(SLAB_C + 2 + c)
                    dve.wait_ge(a_free, ACT_C + 8 + 8 * c + b + 1)
                    reduce_c(RSW[:, b, bass.ds(8 * c, 8)],
                             heads(ST[:, ((b + 1) % 2) * SL:((b + 1) % 2 + 1) * SL], 8))
            dve.wait_ge(sqr_rdy, NB)
            dve.tensor_tensor(SCR[:, :, :], SSR[:, :, :], COLS[:, 2, :].unsqueeze(1).to_broadcast([P, NB, HR]),
                              ALU.mult).then_inc(scr_step, 1)
            dve.wait_ge(c_std, 2)
            dve.reciprocal(RSW[:, :, :], RSW[:, :, :]).then_inc(c_rstd, 1)
            dve.reciprocal(SSM[0:META, 4:8], SSM[0:META, 0:4]).then_inc(c_rstd, 1)
            dve.wait_ge(c_std, 3)
            dve.reciprocal(SCR[:, :, :], SCR[:, :, :]).then_inc(c_rstd, 1)
            dve.wait_ge(c_rstd, 3)
            dve.tensor_tensor(SCR[:, :, :], SCR[:, :, :], COLS[:, 3, :].unsqueeze(1).to_broadcast([P, NB, HR]),
                              ALU.mult).then_inc(scr_step, 1)

            dve.tensor_tensor(heads(ST[0:META, 0:256]), heads(MKV[0:META, 0:256]),
                              SSM[0:META, 4:8].unsqueeze(2).to_broadcast([META, 4, HD]), ALU.mult)\
               .then_inc(mk_rdy, 1)
            dve.memset(KTT[:, :, META + P:NKEY], 0.0)
            dve.tensor_scalar(NSK[:, :], SK[:, :], -1.0, None, ALU.mult)
            dve.scalar_tensor_tensor(out=GQK[:, 2:3], in0=GQK[:, 0:1], scalar=float(HD ** -0.5), in1=GQK[:, 1:2],
                                     op0=ALU.mult, op1=ALU.mult).then_inc(d_set, 1)
            dve.wait_ge(mkt_full, 1)
            dve.tensor_copy(KTT[:, :, 0:META], B[6][:, 0:2 * META].rearrange("p (k t) -> p k t", k=2))\
               .then_inc(mkT_rdy, 1)
            dve.wait_ge(d_set, 1)
            for kind in range(2):
                with dve.Fori(2 * kind, 2 * kind + 2) as pr:
                    for s in range(2):
                        n = 2 * pr + s
                        for t in range(12):
                            if t == 0 and s == 0:
                                split_lo(SLAB_D + pr, KT - 1)
                            if t == 0:
                                dve.wait_ge(aq_full, 2 * n + START)
                                if s == 0:
                                    dve.wait_ge(mkt_full, 1)
                                for t2 in range(2):
                                    q = dve.tensor_tensor(
                                        ST[:, t2 * SL:(t2 + 1) * SL].rearrange("p (j q d) -> p q j d", j=4, q=2),
                                        RT[:, t2, n, :].rearrange("p (q j d) -> p q j d", q=2, j=4),
                                        RSW[:, n, 8 * t2:8 * t2 + 8].rearrange("p (q j) -> p q j", q=2).unsqueeze(3)
                                        .to_broadcast([P, 2, 4, HD]), ALU.mult)
                                q.then_inc(qn_rdy, 1)
                                dve.wait_ge(ak_full, n + START)
                                dve.tensor_tensor(heads(KN[:, :]), heads(KV[:, n + 1, 0:256]),
                                                  RSW[:, n, 16:20].unsqueeze(2).to_broadcast([P, 4, HD]), ALU.mult)\
                                   .then_inc(kn_rdy, 1)
                                dve.wait_ge(ak_full, n + 1 + START)
                                dve.wait_ge(sc_full, HS * n + START)
                                dve.tensor_copy(KTT[:, :, META + s * P:META + (s + 1) * P],
                                                B[6][:, 0:256].rearrange("p (k t) -> p k t", k=2)).then_inc(akT_rdy, 1)
                                dve.wait_ge(dt_full[s], 16 * (pr + 1))
                            if 3 <= t <= 10:
                                p = t - 3
                                dve.wait_ge(ptm_full, 8 * n + p + 1)
                                if p >= 2:
                                    dve.wait_ge(pv_full, 8 * n + p - 1 + START)
                                dve.tensor_copy(PTM[0:META, p % 2, :, :],
                                                B[6][0:META, 0:256].rearrange("p (k t) -> p k t", k=2))\
                                   .then_inc(ptm_rdy, 1)
                            if 1 <= t <= 8:
                                p = t - 1
                                if p >= 2:
                                    dve.wait_ge(ptm_full, 8 * n + p - 1)
                                for hl in range(2):
                                    hh = 2 * p + hl
                                    dve.wait_ge(sc_full, HS * n + hh + 1 + START)
                                    dve.scalar_tensor_tensor(out=PR[:, p % 2, hl, :], in0=DT[:, s, :],
                                                             scalar=SLOPES[hh], in1=B[2 + hh % 2][:, 0:NKEY],
                                                             op0=ALU.mult, op1=ALU.add).then_inc(sc_rdy, 1)
                                dve.wait_ge(sc_rdy, HS * n + 2 * p + 2 + START)
                                dve.tensor_reduce(MX[:, s, 2 * p:2 * p + 2], PR[:, p % 2, :, :], AX_X, ALU.max)\
                                   .then_inc(mx_rdy, 1)
                                dve.wait_ge(mx_rdy, 8 * n + p + 1)
                                cs = slice(2 * p, 2 * p + 2)
                                dve.scalar_tensor_tensor(out=NM[:, s, cs], in0=MX[:, s, cs], scalar=-1.0,
                                                         in1=NSK[:, cs], op0=ALU.mult, op1=ALU.min).then_inc(nm_rdy, 1)
                                dve.wait_ge(nm_rdy, 8 * n + p + 1)
                                dve.tensor_tensor(SE[:, s, cs], SK[:, cs], NM[:, s, cs], ALU.add).then_inc(se_rdy, 1)
                            if t >= 4:
                                p = t - 4
                                cs = slice(2 * p, 2 * p + 2)
                                dve.wait_ge(e_rdy, 8 * n + p + 1)
                                dve.tensor_tensor(RS[:, s, cs], RS[:, s, cs], ES[:, s, cs], ALU.add).then_inc(den_rdy, 1)
                                dve.wait_ge(den_rdy, 16 * n + 2 * p + 1)
                                dve.reciprocal(ES[:, s, cs], RS[:, s, cs]).then_inc(den_rdy, 1)
                                dve.wait_ge(den_rdy, 16 * n + 2 * p + 2)
                                dve.wait_ge(pv_full, 8 * n + p + 1 + START)
                                dve.tensor_tensor(RT[:, p // 4, n, (p % 4) * P:(p % 4 + 1) * P]
                                                  .rearrange("p (h d) -> p h d", h=2),
                                                  B[7][:, 0:P].rearrange("p (h d) -> p h d", h=2),
                                                  ES[:, s, cs].unsqueeze(2).to_broadcast([P, 2, HD]), ALU.mult)\
                                   .then_inc(y_rdy, 1)
                            if s == 1 and t >= 9:
                                for k in KS_D[t - 9]:
                                    if k < KT - 1:
                                        split_lo(SLAB_D + pr + 1, k)
                            if t % 3 == 2 and kind == 1:
                                q = t // 3
                                dve.wait_ge(th_rdy, 8 * (pr - 2) + 4 * s + q + 1)
                                dve.scalar_tensor_tensor(out=TB[:, q % 2, :], in0=TB[:, q % 2, :], scalar=1.0,
                                                         in1=B[q % 2][:, :], op0=ALU.add, op1=ALU.mult)\
                                   .then_inc(a_free, 1)

            def scale_yr(b):
                if b == 0:
                    dve.wait_ge(gm_full, 16)
                    dve.wait_ge(scr_step, 2)
                if b >= 1:
                    dve.wait_ge(yt_full, 2 * b)
                for h in range(HR):
                    y = dve.scalar_tensor_tensor(out=ST[:, h * RV:(h + 1) * RV],
                                                 in0=RT[:, 2 + h // 2, b, (h % 2) * RV:(h % 2 + 1) * RV],
                                                 scalar=SCR[:, b, h:h + 1], in1=GBR[:, h * RV:(h + 1) * RV],
                                                 op0=ALU.mult, op1=ALU.mult)
                y.then_inc(ysc_rdy, 1)

            def gate_yr(b):
                for u in range(2):
                    dve.wait_ge(yt_full, 2 * b + u + 1)
                    if u == 0:
                        dve.wait_ge(gb_full[b % 2], 32 * (b // 2 + 1))
                        if b == 0:
                            dve.wait_ge(gst_done[0], 16 * (24 + START))
                            dve.wait_ge(gst_done[1], 16 * (24 + START))
                    dve.tensor_tensor(TB[:, u, :].rearrange("p (k t) -> p k t", k=4),
                                      B[2 + u][:, :].rearrange("p (k t) -> p k t", k=4),
                                      GB[:, b % 2, 4 * u:4 * u + 4, :], ALU.mult).then_inc(yt_rdy, 1)
                for u in range(2):
                    cols = slice((b % 4) * P, (b % 4 + 1) * P)
                    dve.wait_ge(yh_rdy, 2 * b + u + 1)
                    dve.tensor_tensor(YR[b // 4][:, 1, 4 * u:4 * u + 4, cols],
                                      TB[:, u, :].rearrange("p (k t) -> p k t", k=4),
                                      YR[b // 4][:, 0, 4 * u:4 * u + 4, cols].bitcast(F32), ALU.subtract)\
                       .then_inc(yl_rdy, 1)

            def lo_ys(b):
                cols = slice((b % 4) * P, (b % 4 + 1) * P)
                for u in range(2):
                    dve.wait_ge(sh_rdy, 2 * b + u + 1)
                    dve.tensor_tensor(YS[b // 4][:, 1, 4 * u:4 * u + 4, cols],
                                      B[4 + u][:, :].rearrange("p (k t) -> p k t", k=4),
                                      YS[b // 4][:, 0, 4 * u:4 * u + 4, cols].bitcast(F32), ALU.subtract)\
                       .then_inc(ysl_rdy, 1)

            scale_yr(0)
            for b in range(4):
                gate_yr(b)
                scale_yr(b + 1)
            for j in range(32):
                if j % 8 == 0:
                    split_lo(SLAB_E + j // 8, KT - 1)
                if j < 4:
                    gate_yr(4 + j)
                    if j < 3:
                        scale_yr(5 + j)
                elif j < 8:
                    lo_ys(j - 4)
                elif 12 <= j < 16:
                    lo_ys(j - 8)
                if j % 8 == 7:
                    next_lo(SLAB_E + j // 8 + 1)
                i = j % 16
                f, half = 4 * (i // 8) + i % 4, (i // 4) % 2
                hs = slice(half * SL, (half + 1) * SL)
                dve.wait_ge(d_full, j + 1)
                dve.wait_ge(tg_full[j % 4], 16 * (j // 4 + 1))
                if j < 16:
                    dve.scalar_tensor_tensor(out=MR[:, f, hs], in0=TH[:, j % 4, :], scalar=1.0, in1=B[6 + j % 2][:, :],
                                             op0=ALU.add, op1=ALU.mult).then_inc(d_free, 1)
                else:
                    dve.scalar_tensor_tensor(out=TB[:, 0, :], in0=TH[:, j % 4, :], scalar=1.0, in1=B[6 + j % 2][:, :],
                                             op0=ALU.add, op1=ALU.mult).then_inc(d_free, 1)
                    dve.wait_ge(d_free, j + 1)
                    dve.tensor_tensor(TB[:, 1, :], TB[:, 0, :], MR[:, f, hs], ALU.add).then_inc(e2_sum, 1)
                    dve.wait_ge(e2_hi, i + 1)
                    dve.tensor_tensor(MG[1][:, f, hs], TB[:, 1, :], MG[0][:, f, hs].bitcast(F32), ALU.subtract)\
                       .then_inc(mg_rdy, 1)

            def norm_h(b):
                dve.wait_ge(std_rdy, NB + 1 + b + 1)
                dve.reciprocal(RSTD2[:, b:b + 1], STD2[:, b:b + 1]).then_inc(rstd_rdy, 1)
                dve.wait_ge(rstd_rdy, NB + 1 + b + 1)
                if b == 0:
                    dve.wait_ge(gm_full, 32)
                else:
                    dve.wait_ge(xt_full, 2 * (NB + 1) + 2 * b)
                dve.scalar_tensor_tensor(out=ST[:, :], in0=H1[:, b, :], scalar=RSTD2[:, b:b + 1],
                                         in1=GBM[:, :], op0=ALU.mult, op1=ALU.mult).then_inc(xn_rdy, 1)

            def lo_h(b):
                cols = slice((b % 4) * P, (b % 4 + 1) * P)
                for u in range(2):
                    dve.wait_ge(hn_hi, 2 * (NB + 1) + 2 * b + u + 1)
                    dve.tensor_tensor(HN2[b // 4][:, 1, 4 * u:4 * u + 4, cols],
                                      B[2 + u][:, :].rearrange("p (k t) -> p k t", k=4),
                                      HN2[b // 4][:, 0, 4 * u:4 * u + 4, cols].bitcast(F32), ALU.subtract)\
                       .then_inc(hn_lo, 1)

            for c in range(2):
                split_lo(SLAB_F + c, KT - 1)
                for b in range(NB):
                    j = DVE_F + 8 * c + b
                    if c == 1 and b >= 2:
                        lo_h(b - 2)
                    if b == NB - 1:
                        next_lo(SLAB_F + c + 1)
                    if c == 0:
                        dve.wait_ge(xres_full[b], 16)
                    dve.wait_ge(d_full, j + 1)
                    dve.scalar_tensor_tensor(out=H1[:, b, c * SL:(c + 1) * SL], in0=B[6 + j % 2][:, :], scalar=0.5,
                                             in1=H1[:, b, c * SL:(c + 1) * SL], op0=ALU.mult, op1=ALU.add)\
                       .then_inc(d_free, 1)
                    if c == 1:
                        norm_h(b)
            lo_h(NB - 2)
            lo_h(NB - 1)

            def mlp(g, last):
                for c in range(2):
                    split_lo(SLAB_H + 4 * g + c, KT - 1)
                    for gi in range(8):
                        if gi == 7:
                            next_lo(SLAB_H + 4 * g + c + 1)
                        i = 16 * g + 8 * c + gi
                        fs, hs = 4 * c + gi % 4, slice((gi // 4) * SL, (gi // 4 + 1) * SL)
                        dve.wait_ge(a_free, ACT_H + i + 1)
                        dve.tensor_tensor(TU[:, gi % 2, :], TB[:, gi % 2, :], TB[:, gi % 2, :], ALU.mult)\
                           .then_inc(sq_rdy, 1)
                        dve.wait_ge(uh_rdy, i + 1)
                        dve.tensor_tensor(U[1][:, fs, hs], TU[:, gi % 2, :], U[0][:, fs, hs].bitcast(F32),
                                          ALU.subtract).then_inc(u_rdy, 1)
                for c in range(2):
                    split_lo(SLAB_H + 4 * g + 2 + c, KT - 1)
                    for b in range(NB):
                        if b == NB - 1 and not (last and c == 1):
                            next_lo(SLAB_H + 4 * g + 3 + c)
                        dve.wait_ge(d_full, DVE_H + 16 * g + 8 * c + b + 1)
                        dve.tensor_tensor(H1[:, b, c * SL:(c + 1) * SL], B[6 + b % 2][:, :],
                                          H1[:, b, c * SL:(c + 1) * SL], ALU.add).then_inc(d_free, 1)

            with dve.Fori(0, FF_GROUPS - 1) as g:
                mlp(g, False)
            mlp(FF_GROUPS - 1, True)


_INS = ["x", "meta_tokens", "mix_norm_g", "w_in", "ret_norm_g", "q_norm_g", "k_norm_g", "sinks",
        "w_ret_branch", "w_swa_branch", "w_out", "mlp_norm_g", "w_up", "w_down"]


def kernel(**inputs):
    import concourse.bacc as bacc
    from concourse.bass_utils import run_bass_kernel_spmd

    nc = bacc.Bacc("TRN2", target_bir_lowering=False, num_devices=1, dynamic_dma_scratch_size=4096)
    shapes = {"x": (T, D), "q_norm_g": (HD, 1), "k_norm_g": (HD, 1), "mix_norm_g": (D,), "mlp_norm_g": (D,),
              "ret_norm_g": (HR * RV,), "sinks": (HS,)}
    arrays, args = {}, []
    for name in _INS:
        a = np.ascontiguousarray(inputs[name])
        a = a.reshape(shapes.get(name, a.shape[-2:]))
        arrays[f"in_{name}"] = a
    arrays.update(shape_constants())
    for name, a in arrays.items():
        args.append(nc.dram_tensor(name, a.shape, mybir.dt.from_np(a.dtype), kind="ExternalInput").ap())
    args.append(nc.dram_tensor("h_out", (T, D), F32, kind="ExternalOutput").ap())
    build(nc, *args)
    r = run_bass_kernel_spmd(nc, [arrays], core_ids=[0])
    return r.results[0]["h_out"].reshape(1, T, D)
```

```python
from contextlib import ExitStack

import numpy as np

import concourse.bass as bass
import concourse.mybir as mybir

F32 = mybir.dt.float32
F32R = mybir.dt.float32r
ALU = mybir.AluOpType
ACT = mybir.ActivationFunctionType
AX_X = mybir.AxisListType.X

P = 128
D = 1024
KT = D // P
T = 1024
NB = T // P
META = 16
SL = 512
HR, RV = 4, 256
HS, HD = 16, 64
NKEY = META + 2 * P
WKEY = NKEY + META
KEYS_OF = [slice(META, WKEY), slice(0, NKEY)]
EPS = 1e-6
FF_GROUPS = 4
COL_GR, COL_GS, COL_RG, COL_SQ, COL_KV = 4608, 5632, 2048, 3072, 4096

SLAB_B, SLAB_C, SLAB_D, SLAB_E, SLAB_F, SLAB_H = 4, 6, 9, 13, 17, 19
ACT_B, ACT_C, ACT_D, ACT_H = 32, 48, 72, 104
DVE_F, DVE_H = 32, 48
START = 1
KS_D = [[0, 1, 2], [3, 4, 5], [6, 7]]
SLOPES = [float(2.0 ** (-8.0 * (h + 1) / HS)) for h in range(HS)]
GAMMA = [1.0 - 2.0 ** (-5.0 - h) for h in range(HR)]


def shape_constants():
    ident = np.eye(P, dtype=np.float32)
    i = np.arange(P, dtype=np.float64)
    lg = np.log1p(-(2.0 ** (-5.0 - np.arange(HR, dtype=np.float64))))
    kscale = 128.0 ** -0.5
    mask = (i[:, None] <= i[None, :])[:, None, :] * np.exp(-P * lg)[None, :, None]
    kdec = np.exp(lg[None, :] * (P - 1 - i)[:, None]) * kscale
    kdec_meta = np.zeros((P, HR))
    kdec_meta[:META] = kdec[P - META:]
    qsq = np.exp(2 * lg[None, :] * (i + 1)[:, None]) / RV
    qhalf = 0.5 * np.exp(lg[None, :] * (i + 1)[:, None])
    cols = np.concatenate([kdec, kdec_meta, qsq, qhalf], axis=1)
    dist = np.full((NB + 1, P, WKEY), -1e30)
    for n in range(NB):
        dist[n, :, :META] = -((n + 1) * P + i[:, None] - (P - META + np.arange(META))[None, :])
        dist[n, :, NKEY:] = dist[n, :, :META]
        own = META + P * (n % 2)
        other = META + P * (1 - n % 2)
        d = i[:, None] - i[None, :]
        dist[n, :, own:own + P] = np.where(d >= 0, -d, -1e30)
        if n > 0:
            d = d + P
            dist[n, :, other:other + P] = np.where(d < P, -d, -1e30)
    f = lambda a: np.ascontiguousarray(a, dtype=np.float32)
    return {"c_ident": f(ident), "c_mask": f(mask.reshape(P, HR * P)), "c_cols": f(cols), "c_dist": f(dist)}


def build(nc, x, meta, g_mix, w_in, g_ret, g_q, g_k, sinks, w_ret, w_swa, w_out, g_mlp, w_up, w_down,
          c_ident, c_mask, c_cols, c_dist, out):
    with ExitStack() as ctx:
        base = (nc.sbuf_base + 63) // 64 * 64
        O_R0, O_R1 = 0, 32768
        O_Q = 2 * KT * (T + META) * 4
        O_V = O_Q + 32768
        O_M = O_V + 32768
        O_WH = O_M + 32768
        O_WL = O_WH + KT * SL * 4
        O_RAW = O_WL + KT * SL * 4
        O_ST = O_RAW + 4 * SL * 4
        O_TB = O_ST + D * 4
        O_ID = O_TB + 2 * SL * 4
        O_SM = O_ID + P * 4
        O_X = O_SM + 1088

        def at(name, off, shape, dt=F32):
            return nc.alloc_sbuf_tensor_at(name, [P, *shape], dt, offset=base + off)

        HN = at("HN", 0, [2, KT, META + T], F32R)
        RT = at("RT", O_Q, [4, NB, SL])
        YS = [at("YS0", O_R0, [2, KT, SL], F32R), at("YS1", O_R1, [2, KT, SL], F32R)]
        YR = [at("YR0", O_Q, [2, KT, SL], F32R), at("YR1", O_R0, [2, KT, SL], F32R)]
        HN2 = [at("HN20", O_Q, [2, KT, SL], F32R), at("HN21", O_R0, [2, KT, SL], F32R)]
        H1 = at("H1", O_R1, [NB, D])
        MR = at("MR", O_M, [KT, T])
        MG = [at("MGH", O_M, [KT, T], F32R), at("MGL", O_V, [KT, T], F32R)]
        U = [at("UH", O_M, [KT, T], F32R), at("UL", O_V, [KT, T], F32R)]
        WH = at("WH", O_WH, [KT, SL], F32R)
        WL = at("WL", O_WL, [KT, SL], F32R)
        RAW = at("RAW", O_RAW, [4, SL])
        ST = at("ST", O_ST, [D])
        TB = at("TB", O_TB, [2, SL])
        IDN = at("IDN", O_ID, [P])
        SS = at("SS", O_SM, [16])
        STD = at("STD", O_SM + 64, [16])
        RSTD = at("RSTD", O_SM + 128, [16])
        SS2 = at("SS2", O_SM + 192, [NB])
        STD2 = at("STD2", O_SM + 224, [NB])
        RSTD2 = at("RSTD2", O_SM + 256, [NB])
        COLS = at("COLS", O_SM + 288, [4, HR])
        SSR = at("SSR", O_SM + 352, [NB, HR])
        SCR = at("SCR", O_SM + 480, [NB, HR])
        EPSC = at("EPSC", O_SM + 608, [1])
        SK = at("SK", O_SM + 672, [HS])
        NSK = at("NSK", O_SM + 736, [HS])
        SSM = at("SSM", O_SM + 800, [8])
        GBC = at("GBC", O_M, [D])
        XR = at("XR", O_M + 4096, [4, D])
        MRK = at("MRK", O_M + 24576, [3, SL])
        JUNK = at("JUNK", O_X, [D])
        QS = at("QS", O_M, [SL])
        KD = at("KD", O_M + 2048, [SL])
        QTR = at("QTR", O_M + 4096, [SL])
        KTR = at("KTR", O_M + 6144, [SL])
        SMK = at("SMK", O_M + 8192, [SL])
        STA = at("STA", O_M + 10240, [HR * RV])
        KDM = at("KDM", O_M + 14336, [SL])
        MASK = at("MASK", O_X + 4096, [SL])
        KV = at("KV", O_M, [NB + 1, SL])
        MKV = at("MKV", O_M + 18432, [SL])
        KST = at("KST", O_M + 21504, [2, 4, P], F32R)
        GQ = at("GQ", O_M + 30720, [HD])
        GK = at("GK", O_M + 30976, [HD])
        GQK = at("GQK", O_M + 25600, [HD])
        KNF = at("KNF", O_M + 25856, [256])
        PTS = at("PTS", O_M + 27776, [2, 4, P])
        RSW = at("RSW", O_M + 31872, [NB, 20])
        PR = at("PR", O_X, [2, 2 * NKEY])
        PTM = at("PTM", O_X + 4352, [2, P])
        DT = at("DT", O_X + 6144, [2, WKEY])
        MX = at("MX", O_X + 8576, [2, HS])
        NM = at("NM", O_X + 8704, [2, HS])
        SE = at("SE", O_X + 8832, [2, HS])
        RS = at("RS", O_X + 8960, [2, HS])
        ES = at("ES", O_X + 9088, [2, HS])
        QNF = at("QNF", O_V, [D])
        QST = at("QST", O_V + 4096, [HS, 2, HD], F32R)
        QT = at("QT", O_V + 12288, [HS, P], F32R)
        KTS = [at("KTH", O_V + 20480, [4, WKEY], F32R), at("KTL", O_V + 25088, [4, WKEY], F32R)]
        IDR = at("IDR", O_V + 29696, [P], F32R)
        MVB = at("MVB", O_V + 30720, [4, 2, HD])
        YB = at("YB", O_V, [2, D])
        GB = at("GB", O_V + 8192, [2, KT, P])
        GBR = at("GBR", O_V + 16384, [D])
        TH = at("TH", O_X, [4, SL])
        GBM = at("GBM", O_X, [D])
        TU = at("TU", O_X + 4096, [2, SL])
        JUNK2 = at("JUNK2", O_X + 4096, [D])

        B = [ctx.enter_context(nc.psum_tensor(f"bank{i}", [P, SL], F32)) for i in range(8)]

        y_raw = nc.dram_tensor("y_raw", [NB, P, 2, SL], F32, kind="Internal").ap()
        gates = nc.dram_tensor("gates", [6, 2, 4, P, SL], F32, kind="Internal").ap()

        def sem(name):
            return ctx.enter_context(nc.semaphore(name))

        raw_full = [sem(f"raw_full{i}") for i in range(4)]
        w_hi, w_ready, w_free = sem("w_hi"), sem("w_ready"), sem("w_free")
        a_full, a_free, d_full, d_free = sem("a_full"), sem("a_free"), sem("d_full"), sem("d_free")
        id_full, c_full = sem("id_full"), sem("c_full")
        g_full = sem("g_full")
        x0_full = sem("x0_full")
        x_full = [sem(f"x_full{i}") for i in range(4)]
        ss_rdy, std_rdy, rstd_rdy, xn_rdy = sem("ss_rdy"), sem("std_rdy"), sem("rstd_rdy"), sem("xn_rdy")
        xt_full, hn_hi, hn_lo = sem("xt_full"), sem("hn_hi"), sem("hn_lo")
        meta_full, meta_free = sem("meta_full"), sem("meta_free")
        eps_set = sem("eps_set")
        kdm_rdy, kd_rdy, qs_rdy = sem("kdm_rdy"), sem("kd_rdy"), sem("qs_rdy")
        qt_full, kt_full, qT_rdy, kT_rdy = sem("qt_full"), sem("kt_full"), sem("qT_rdy"), sem("kT_rdy")
        s_full, sm_rdy, o_full, u_full = sem("s_full"), sem("sm_rdy"), sem("o_full"), sem("u_full")
        st_rdy, oraw_rdy, sqr_rdy = sem("st_rdy"), sem("oraw_rdy"), sem("sqr_rdy")
        gst_done = [sem("gst_done0"), sem("gst_done1")]
        c_sq, c_red, c_std, c_rstd, scr_step = sem("c_sq"), sem("c_red"), sem("c_std"), sem("c_rstd"), sem("scr_step")
        d_small, d_set = sem("d_small"), sem("d_set")
        qf_rdy, qh_rdy, ql_rdy = sem("qf_rdy"), sem("qh_rdy"), sem("ql_rdy")
        aq_full, ak_full, aqT_rdy, akT_rdy = sem("aq_full"), sem("ak_full"), sem("aqT_rdy"), sem("akT_rdy")
        kf_step, kv_zero = sem("kf_step"), sem("kv_zero")
        yraw_done, mvb_done = sem("yraw_done"), sem("mvb_done")
        yb_full = [sem("yb_full0"), sem("yb_full1")]
        sc_full, sc_rdy, mx_rdy, nm_rdy, se_rdy, e_rdy = (sem("sc_full"), sem("sc_rdy"), sem("mx_rdy"), sem("nm_rdy"),
                                                         sem("se_rdy"), sem("e_rdy"))
        pt_full, ptm_full, ptv_rdy, ptm_rdy = sem("pt_full"), sem("ptm_full"), sem("ptv_rdy"), sem("ptm_rdy")
        pv_full, y_rdy, den_rdy = sem("pv_full"), sem("y_rdy"), sem("den_rdy")
        dt_full = [sem("dt_full0"), sem("dt_full1")]
        th_rdy = sem("th_rdy")
        gb_full = [sem("gb_full0"), sem("gb_full1")]
        ysc_rdy, yt_full, yt_rdy, yh_rdy, yl_rdy = sem("ysc_rdy"), sem("yt_full"), sem("yt_rdy"), sem("yh_rdy"), sem("yl_rdy")
        st_full, sh_rdy, ysl_rdy = sem("st_full"), sem("sh_rdy"), sem("ysl_rdy")
        tg_full = [sem(f"tg_full{i}") for i in range(4)]
        e2_sum, e2_hi, e2_step, mg_rdy = sem("e2_sum"), sem("e2_hi"), sem("e2_step"), sem("mg_rdy")
        xres_full = [sem(f"xres_full{i}") for i in range(NB)]
        gm_full = sem("gm_full")
        sq_rdy, uh_rdy, u_rdy = sem("sq_rdy"), sem("uh_rdy"), sem("u_rdy")
        out_done = sem("out_done")

        block = ctx.enter_context(nc.Block())

        @block.sync
        def _(sp):
            def load_slab(slab, source, first=False):
                for k in range(KT):
                    if not (first and k < 4):
                        sp.wait_ge(w_ready, 8 * slab + k - 3)
                    sp.dma_start(RAW[:, k % 4, :], source(k)).then_inc(raw_full[k % 4], 16)

            def w_cols(w, col):
                return lambda k: w[k * P:(k + 1) * P, col:col + SL] if isinstance(col, int) else \
                    w[k * P:(k + 1) * P, bass.ds(col, SL)]

            sp.dma_start(XR[:, 0, :], x[0:P, :]).then_inc(x0_full, 16)
            load_slab(0, w_cols(w_in, 0), first=True)
            with sp.Fori(1, 4) as c:
                load_slab(c, w_cols(w_in, c * SL))
            with sp.Fori(0, 2) as c:
                load_slab(SLAB_B + c, w_cols(w_in, COL_GR + c * SL))
            load_slab(SLAB_C, w_cols(w_in, COL_KV))
            with sp.Fori(0, 2) as c:
                load_slab(SLAB_C + 1 + c, w_cols(w_in, COL_SQ + c * SL))
            with sp.Fori(0, 2) as c:
                load_slab(SLAB_D + c, w_cols(w_in, COL_GS + c * SL))
            with sp.Fori(0, 2) as c:
                load_slab(SLAB_D + 2 + c, w_cols(w_in, COL_RG + c * SL))
            for i, w in enumerate((w_swa, w_ret, w_out)):
                with sp.Fori(0, 2) as c:
                    load_slab(SLAB_E + 2 * i + c, w_cols(w, c * SL))
            with sp.Fori(0, FF_GROUPS) as g:
                for c in range(2):
                    load_slab(SLAB_H + 4 * g + c, w_cols(w_up, g * D + c * SL))
                for c in range(2):
                    load_slab(SLAB_H + 4 * g + 2 + c,
                              lambda k: w_down[bass.ds(g * D + k * P, P), c * SL:(c + 1) * SL])
            for c in range(2):
                for b in range(NB):
                    sp.wait_ge(d_free, DVE_H + 16 * (FF_GROUPS - 1) + 8 * c + b + 1)
                    sp.dma_start(out[b * P:(b + 1) * P, c * SL:(c + 1) * SL],
                                 H1[:, b, c * SL:(c + 1) * SL]).then_inc(out_done, 16)
            sp.wait_ge(out_done, 16 * 2 * NB)

        @block.gpsimd
        def _(pool):
            pool.dma_start(IDN[:, :], c_ident).then_inc(id_full, 16)
            pool.dma_start(GBC[:, :], g_mix.partition_broadcast(P)).then_inc(g_full, 16)

            def load_x(b):
                if b >= 4:
                    pool.wait_ge(xn_rdy, b - 3)
                if b < NB:
                    pool.dma_start(XR[:, b % 4, :], x[b * P:(b + 1) * P, :]).then_inc(x_full[b % 4], 16)
                else:
                    pool.dma_start(XR[0:META, b % 4, :], meta).then_inc(x_full[b % 4], 16)

            load_x(1)
            pool.wait_ge(w_ready, 5)
            load_x(2)
            load_x(3)
            pool.dma_start(MASK[:, :], c_mask).then_inc(gst_done[0], 16)
            pool.dma_start(COLS[:, :, :], c_cols.rearrange("p (a h) -> p a h", a=4)).then_inc(gst_done[1], 16)
            pool.dma_start(SK[:, :], sinks.partition_broadcast(P)).then_inc(c_full, 16)
            pool.dma_start(GQ[:, :], g_q.partition_broadcast(P)).then_inc(c_full, 16)
            pool.dma_start(GK[:, :], g_k.partition_broadcast(P)).then_inc(c_full, 16)
            for b in range(4, NB + 1):
                load_x(b)

            def store_gate(a_index, slab6, gi):
                pool.wait_ge(a_free, a_index + 1)
                pool.dma_start(gates[slab6, gi // 4, gi % 4], TB[:, gi % 2, :]).then_inc(gst_done[gi % 2], 16)

            with pool.Fori(0, 2) as it:
                for gi in range(8):
                    store_gate(ACT_B + 8 * it + gi, it, gi)
                    if gi % 2 == 1:
                        r = gi // 2
                        pool.wait_ge(oraw_rdy, 4 * it + r + 1 + START)
                        pool.dma_start(y_raw[4 * it + r], RT[:, 2:4, 4 * it + r, :]).then_inc(yraw_done, 16)
            pool.wait_ge(st_rdy, NB + 1)
            pool.wait_ge(sqr_rdy, NB)
            pool.dma_start(DT[:, 0, :], c_dist[0]).then_inc(dt_full[0], 16)
            pool.wait_ge(meta_free, 4 + START)
            pool.wait_ge(d_small, 1)
            for hl in range(2):
                pool.dma_start(MVB[hl * META:(hl + 1) * META, :, hl, :],
                               MKV[0:META, 256:512].rearrange("p (g d) -> p g d", g=4)).then_inc(mvb_done, 16)
            with pool.Fori(0, 4) as pr:
                for s in range(2):
                    pool.wait_ge(sc_rdy, HS * (2 * pr + s) + START)
                    pool.dma_start(DT[:, 1 - s, :], c_dist[2 * pr + s + 1]).then_inc(dt_full[1 - s], 16)
                    for q in range(4):
                        store_gate(ACT_D + 8 * pr + 4 * s + q, 2 + pr, 4 * s + q)
            pool.wait_ge(gst_done[0], 16 * (24 + START))
            pool.wait_ge(gst_done[1], 16 * (24 + START))
            pool.wait_ge(y_rdy, 8 * NB + START)
            pool.wait_ge(dt_full[0], 16 * 5)
            pool.dma_start(GBR[:, :], g_ret.partition_broadcast(P)).then_inc(gm_full, 16)

            def load_tg(i):
                if i >= 4:
                    pool.wait_ge(d_free, i - 3)
                slab6 = 2 + i // 8 if i < 16 else i // 8 - 2
                pool.dma_start(TH[:, i % 4, :], gates[slab6, (i // 4) % 2, i % 4]).then_inc(tg_full[i % 4], 16)

            def load_yr(b):
                if b >= 2:
                    pool.wait_ge(ysc_rdy, b - 1)
                pool.dma_start(YB[:, b % 2, :].rearrange("p (c s) -> p c s", c=2), y_raw[b])\
                    .then_inc(yb_full[b % 2], 16)
                if b >= 2:
                    pool.wait_ge(yt_rdy, 2 * (b - 1))
                for c in range(2):
                    pool.dma_start(GB[:, b % 2, 4 * c:4 * c + 4, :],
                                   gates[4 + c, b // 4, :, :, (b % 4) * P:(b % 4 + 1) * P].rearrange(
                                       "f p t -> p f t")).then_inc(gb_full[b % 2], 16)

            for i in range(4):
                load_tg(i)
            load_yr(0)
            load_yr(1)
            for i in range(4, 8):
                load_tg(i)
            for b in range(2, 6):
                load_yr(b)
                load_tg(b + 6)
            for i in range(12, 16):
                load_tg(i)
            load_yr(6)
            load_yr(7)
            load_tg(16)
            load_tg(17)
            pool.wait_ge(d_full, 16)
            for i in range(18, 32):
                load_tg(i)
                if i - 18 < NB:
                    b = i - 18
                    pool.dma_start(H1[:, b, :], x[b * P:(b + 1) * P, :]).then_inc(xres_full[b], 16)
            pool.wait_ge(d_free, DVE_F)
            pool.dma_start(GBM[:, :], g_mlp.partition_broadcast(P)).then_inc(gm_full, 16)

        @block.tensor
        def _(pe):
            for one in (qt_full, kt_full, s_full, o_full, sc_full, pv_full):
                pe.sem_inc(one, START)
            def three(bank, ahi, alo, bhi, blo, first, last, frees):
                mm = pe.matmul(bank, ahi, bhi, start=first, stop=False)
                if frees:
                    mm.then_inc(w_free, 1)
                pe.matmul(bank, alo, bhi, start=False, stop=False)
                return pe.matmul(bank, ahi, blo, start=False, stop=last)

            def step(form, bank, k, f, act, slab, opening, closing):
                if opening:
                    pe.wait_ge(w_ready, 8 * slab + k + 1)
                frees = opening and k == 0 and not (isinstance(slab, int) and slab == 0)
                hi, lo = act(k)
                if form == "S":
                    fs = slice(f * P, (f + 1) * P)
                    mm = three(bank[:, :], WH[:, k, fs], WL[:, k, fs], hi, lo, k == 0, k == KT - 1, frees)
                else:
                    mm = three(bank[:, :], hi, lo, WH[:, k, :], WL[:, k, :], k == 0, k == KT - 1, frees)
                if closing and k < KT - 1:
                    mm.then_inc(w_free, 1)
                return mm

            def hn_block(b):
                lo = META + b * P
                return lambda k: (HN[:, 0, k, lo:lo + P], HN[:, 1, k, lo:lo + P])

            def hn_meta(k):
                return HN[:, 0, k, 0:P], HN[:, 1, k, 0:P]

            def hn_half(half):
                lo = META + half * SL
                return lambda k: (HN[:, 0, k, lo:lo + SL], HN[:, 1, k, lo:lo + SL])

            def halves(pair, half):
                return lambda k: (pair[half][:, 0, k, :], pair[half][:, 1, k, :])

            def tokens(pair, b):
                return lambda k: (pair[0][:, k, b * P:(b + 1) * P], pair[1][:, k, b * P:(b + 1) * P])

            def bank_wait(j, loop=False):
                if loop or j >= 2:
                    pe.wait_ge(a_free, j - 1)

            def dense_a(form, j, bank, f, act, slab, opening, closing, loop=True, middle=None):
                bank_wait(j, loop)
                for k in range(KT):
                    mm = step(form, bank, k, f, act, slab, opening, closing)
                    if middle and k == 3:
                        middle()
                mm.then_inc(a_full, 1)

            pe.wait_ge(id_full, 16)

            def transpose_x(b):
                pe.wait_ge(xn_rdy, b + 1)
                if b >= 1:
                    pe.wait_ge(hn_lo, 2 * b)
                rows, w = (P, P) if b < NB else (META, META)
                for k in range(KT):
                    bank = B[2 + k // 4]
                    mm = pe.transpose(bank[:, (k % 4) * w:(k % 4) * w + w], ST[0:rows, k * P:(k + 1) * P],
                                      IDN[0:rows, 0:rows])
                    if k % 4 == 3:
                        mm.then_inc(xt_full, 1)

            transpose_x(0)
            for b in range(NB):
                pe.wait_ge(hn_lo, 2 * (b + 1))
                dense_a("M", b, B[b % 2], 0, hn_block(b), 0, b == 0, b == NB - 1, loop=False,
                        middle=lambda b=b: transpose_x(b + 1))
            pe.wait_ge(hn_lo, 2 * (NB + 1))
            with pe.Fori(1, 4) as c:
                pe.wait_ge(meta_free, c - 1 + START)
                for k in range(KT):
                    mm = step("M", B[6], k, 0, hn_meta, c, True, False)
                mm.then_inc(meta_full, 1)
                for b in range(NB):
                    dense_a("M", 8 * c + b, B[b % 2], 0, hn_block(b), c, False, b == NB - 1)

            pe.wait_ge(kdm_rdy, 1)
            pe.wait_ge(meta_free, 3 + START)
            for h in range(HR):
                mm = pe.matmul(B[6 + h // 2][:, (h % 2) * RV:(h % 2 + 1) * RV], KDM[0:META, h * P:(h + 1) * P],
                               MRK[0:META, 1 + h // 2, (h % 2) * RV:(h % 2 + 1) * RV], start=True, stop=True)
            mm.then_inc(u_full, 1)
            with pe.Fori(0, 2) as it:
                for r in range(4):
                    n = 4 * it + r

                    def weave(slot):
                        gi = 2 * r + slot // 2
                        j = ACT_B + 8 * it + gi
                        if slot % 2 == 0:
                            pe.wait_ge(a_free, j - 1)
                        for k in range(4 * (slot % 2), 4 * (slot % 2) + 4):
                            mm = step("S", B[gi % 2], k, gi % 4, hn_half(gi // 4), SLAB_B + it, gi == 0, gi == 7)
                        if slot % 2 == 1:
                            mm.then_inc(a_full, 1)

                    weave(0)
                    pe.wait_ge(qs_rdy, n + 1)
                    pe.wait_ge(sm_rdy, n + START)
                    for h in range(HR):
                        mm = pe.transpose(B[2][:, h * P:(h + 1) * P], QS[:, h * P:(h + 1) * P], IDN[:, :])
                    mm.then_inc(qt_full, 1)
                    pe.wait_ge(kd_rdy, n + 1)
                    pe.wait_ge(kT_rdy, n + START)
                    for h in range(HR):
                        mm = pe.transpose(B[3][:, h * P:(h + 1) * P], KD[:, h * P:(h + 1) * P], IDN[:, :])
                    mm.then_inc(kt_full, 1)
                    weave(1)
                    pe.wait_ge(qT_rdy, n + 1)
                    pe.wait_ge(kT_rdy, n + 1 + START)
                    for h in range(HR):
                        mm = pe.matmul(B[2][:, h * P:(h + 1) * P], KTR[:, h * P:(h + 1) * P],
                                       QTR[:, h * P:(h + 1) * P], start=True, stop=True)
                    mm.then_inc(s_full, 1)
                    pe.wait_ge(st_rdy, n + 1)
                    for h in range(HR):
                        mm = pe.matmul(B[6 + h // 2][:, (h % 2) * RV:(h % 2 + 1) * RV], KD[:, h * P:(h + 1) * P],
                                       RT[:, 2 + h // 2, n, (h % 2) * RV:(h % 2 + 1) * RV], start=True, stop=True)
                    mm.then_inc(u_full, 1)
                    weave(2)
                    pe.wait_ge(sm_rdy, n + 1 + START)
                    pe.wait_ge(oraw_rdy, n + START)
                    for h in range(HR):
                        o = B[4 + h // 2][:, (h % 2) * RV:(h % 2 + 1) * RV]
                        pe.matmul(o, SMK[:, h * P:(h + 1) * P],
                                  RT[:, 2 + h // 2, n, (h % 2) * RV:(h % 2 + 1) * RV], start=True, stop=False)
                        mm = pe.matmul(o, QTR[:, h * P:(h + 1) * P], STA[:, h * RV:(h + 1) * RV],
                                       start=False, stop=True)
                    mm.then_inc(o_full, 1)
                    weave(3)

            pe.wait_ge(st_rdy, NB + 1)
            for k in range(KT):
                mm = step("M", B[6], k, 0, hn_meta, SLAB_C, True, False)
            mm.then_inc(meta_full, 1)
            for b in range(NB):
                dense_a("M", ACT_C + b, B[b % 2], 0, hn_block(b), SLAB_C, False, b == NB - 1)

            def transpose_k(rows):
                for part in range(2):
                    for g in range(4):
                        mm = pe.transpose(B[6 + part][:, g * rows:(g + 1) * rows].bitcast(F32R),
                                          KST[0:rows, part, g, :], IDR[0:rows, 0:rows])
                    mm.then_inc(ak_full, 1)

            def transpose_meta_k():
                pe.wait_ge(ql_rdy, 1)
                pe.wait_ge(c_sq, 1)
                transpose_k(META)

            for c in range(2):
                for b in range(NB):
                    dense_a("M", ACT_C + 8 + 8 * c + b, B[b % 2], 0, hn_block(b), SLAB_C + 1 + c, b == 0, b == NB - 1,
                            middle=transpose_meta_k if c == 1 and b == 6 else None)

            def attention_block(pr, s):
                n = 2 * pr + s

                def weave(t):
                    q = t // 3
                    j = ACT_D + 8 * pr + 4 * s + q
                    if t % 3 == 0:
                        pe.wait_ge(a_free, j - 1)
                    for k in KS_D[t % 3]:
                        mm = step("S", B[q % 2], k, q, hn_half(s), SLAB_D + pr, s == 0 and q == 0,
                                  s == 1 and q == 3)
                    if t % 3 == 2:
                        mm.then_inc(a_full, 1)

                for t in range(12):
                    weave(t)
                    if t == 0:
                        pe.wait_ge(ql_rdy, n + 2)
                        pe.wait_ge(sc_rdy, HS * n + START)
                        pe.wait_ge(ptv_rdy, 8 * n + START)
                        for hh in range(HS):
                            mm = pe.transpose(B[2 + hh // 4][:, (hh % 4) * P:(hh % 4 + 1) * P].bitcast(F32R),
                                              QST[:, hh, :, :].rearrange("p a d -> p (a d)"), IDR[:, :])
                            if hh % 4 == 3:
                                mm.then_inc(aq_full, 1)
                        pe.wait_ge(akT_rdy, 2 * n + 2)
                        pe.wait_ge(ptm_rdy, 8 * n + START)
                        pe.wait_ge(y_rdy, 8 * n + START)
                        transpose_k(P)
                    if 3 <= t <= 10:
                        p = t - 3
                        pe.wait_ge(e_rdy, 8 * n + p + 1)
                        if p == 0:
                            pe.wait_ge(aqT_rdy, 4 * n + 4)
                        if p >= 2:
                            pe.wait_ge(ptv_rdy, 8 * n + p - 1 + START)
                        for hl in range(2):
                            for sl in range(2):
                                c = 2 * hl + sl
                                mm = pe.transpose(B[4 + p % 2][:, c * P:(c + 1) * P],
                                                  PR[:, p % 2, hl * (NKEY + META) + sl * P:hl * (NKEY + META) + (sl + 1) * P], IDN[:, :])
                        mm.then_inc(pt_full, 1)
                        if p >= 1:
                            pe.wait_ge(ptm_rdy, 8 * n + p + START)
                        pe.transpose(B[6][0:2 * META, 0:P], PR[:, p % 2, 2 * P:2 * P + 2 * META], IDN[:, :]).then_inc(ptm_full, 1)
                    if 1 <= t <= 8:
                        p = t - 1
                        for hh in (2 * p, 2 * p + 1):
                            g = hh // 4
                            if hh % 4 == 0 or hh == 1:
                                pe.wait_ge(aqT_rdy, 4 * n + max(hh // 4, hh % 4) + 1)
                            if hh == 0:
                                pe.wait_ge(akT_rdy, 2 * n + 4)
                            if hh >= 2:
                                pe.wait_ge(sc_rdy, HS * n + hh - 1 + START)
                            pe.matmul(B[2 + hh % 2][:, 0:NKEY], QT[:, hh, :], KTS[0][:, g, KEYS_OF[hh % 2]], start=True,
                                      stop=False)
                            pe.matmul(B[2 + hh % 2][:, 0:NKEY], QT[:, hh, :], KTS[1][:, g, KEYS_OF[hh % 2]], start=False,
                                      stop=True).then_inc(sc_full, 1)
                    if t >= 4:
                        p = t - 4
                        g = p // 2
                        vs = slice(256 + g * HD, 256 + (g + 1) * HD)
                        if p == 0:
                            pe.wait_ge(mvb_done, 32)
                        pe.wait_ge(ptv_rdy, 8 * n + p + 1 + START)
                        pe.wait_ge(ptm_rdy, 8 * n + p + 1 + START)
                        pe.wait_ge(y_rdy, 8 * n + p + START)
                        pe.matmul(B[7][:, 0:P], PTM[0:2 * META, p % 2, :],
                                  MVB[0:2 * META, g, :, :].rearrange("p a d -> p (a d)"), start=True, stop=False)
                        for hl in range(2):
                            for sl in range(2):
                                blk = n + 1 if sl == s else n
                                mm = pe.matmul(B[7][:, hl * HD:(hl + 1) * HD], PTS[:, p % 2, 2 * hl + sl, :],
                                               KV[:, blk, vs], start=False, stop=hl == 1 and sl == 1)
                        mm.then_inc(pv_full, 1)

            with pe.Fori(0, 2) as pr:
                for s in range(2):
                    attention_block(pr, s)
            for pr in (2, 3):
                for s in range(2):
                    attention_block(pr, s)

            def transpose_yr(b):
                pe.wait_ge(ysc_rdy, b + 1)
                if b >= 1:
                    pe.wait_ge(yt_rdy, 2 * b)
                for k in range(KT):
                    mm = pe.transpose(B[2 + k // 4][:, (k % 4) * P:(k % 4 + 1) * P], ST[:, k * P:(k + 1) * P],
                                      IDN[:, :])
                    if k % 4 == 3:
                        mm.then_inc(yt_full, 1)

            def transpose_ys(b, u, bank):
                for k in range(4):
                    mm = pe.transpose(bank[:, k * P:(k + 1) * P], RT[:, u, b, k * P:(k + 1) * P], IDN[:, :])
                mm.then_inc(st_full, 1)

            pe.wait_ge(y_rdy, 8 * NB + START)
            for u in range(2):
                for b in range(4):
                    if u == 1:
                        pe.wait_ge(ysl_rdy, b + 1)
                    transpose_ys(b, u, B[2 + b])
            for j in range(32):
                branch, c, half, f = j // 16, (j // 8) % 2, (j // 4) % 2, j % 4
                slab = SLAB_E + 2 * branch + c
                if j >= 2:
                    pe.wait_ge(d_free, j - 1)
                if j == 0:
                    pe.wait_ge(ysl_rdy, 4)
                if j == 4:
                    pe.wait_ge(ysl_rdy, 16)
                if branch == 1 and c == 0 and f == 0:
                    pe.wait_ge(yl_rdy, 8 * (half + 1))
                act = halves(YS if branch == 0 else YR, half)
                for k in range(KT):
                    if j == 0 and k == 4:
                        pe.wait_ge(ysl_rdy, 8)
                    mm = step("S", B[6 + j % 2], k, f, act, slab, half == 0 and f == 0, half == 1 and f == 3)
                    if k == 3:
                        if j < 4:
                            b = 4 + j
                            pe.wait_ge(ysl_rdy, 2 * b)
                            for u in range(2):
                                transpose_ys(b, u, B[4 + u])
                        elif j < 8:
                            transpose_yr(j - 4)
                        elif 12 <= j < 16:
                            transpose_yr(j - 8)
                mm.then_inc(d_full, 1)

            def transpose_h(b):
                pe.wait_ge(xn_rdy, NB + 1 + b + 1)
                pe.wait_ge(hn_lo, 2 * (NB + 1) + 2 * b)
                for k in range(KT):
                    mm = pe.transpose(B[2 + k // 4][:, (k % 4) * P:(k % 4 + 1) * P], ST[:, k * P:(k + 1) * P], IDN[:, :])
                    if k % 4 == 3:
                        mm.then_inc(xt_full, 1)

            for c in range(2):
                for b in range(NB):
                    j = DVE_F + 8 * c + b
                    pe.wait_ge(d_free, j - 1)
                    if c == 0:
                        pe.wait_ge(mg_rdy, 12 if b < 4 else 16)
                    for k in range(KT):
                        mm = step("M", B[6 + j % 2], k, 0, tokens(MG, b), SLAB_F + c, b == 0, b == NB - 1)
                        if k == 3 and c == 1 and b >= 2:
                            transpose_h(b - 2)
                    mm.then_inc(d_full, 1)

            def mlp(g):
                for c in range(2):
                    for gi in range(8):
                        middle = None
                        if isinstance(g, int) and g == c == 0:
                            if gi in (0, 2):
                                middle = lambda gi=gi: transpose_h(NB - 2 + gi // 2)
                            if gi == 4:
                                pe.wait_ge(hn_lo, 2 * (NB + 1) + 2 * NB)
                        dense_a("S", ACT_H + 16 * g + 8 * c + gi, B[gi % 2], gi % 4, halves(HN2, gi // 4),
                                SLAB_H + 4 * g + c, gi == 0, gi == 7, middle=middle)
                for c in range(2):
                    for b in range(NB):
                        j = DVE_H + 16 * g + 8 * c + b
                        pe.wait_ge(d_free, j - 1)
                        if c == 0:
                            pe.wait_ge(u_rdy, 16 * g + (12 if b < 4 else 16) + START)
                        for k in range(KT):
                            mm = step("M", B[6 + b % 2], k, 0, tokens(U, b), SLAB_H + 4 * g + 2 + c, b == 0, b == NB - 1)
                        mm.then_inc(d_full, 1)

            mlp(0)
            with pe.Fori(1, FF_GROUPS) as g:
                mlp(g)

        @block.scalar
        def _(act):
            for one in (meta_free, ptv_rdy):
                act.sem_inc(one, START)
            def split_hi(slab, k, first=False):
                act.wait_ge(raw_full[k % 4], 16 * (2 * slab + k // 4 + 1))
                if not first:
                    act.wait_ge(w_free, 8 * slab + k - 7)
                act.copy(WH[:, k, :], RAW[:, k % 4, :]).then_inc(w_hi, 1)

            def next_hi(slab, tiles=KT - 1):
                for k in range(tiles):
                    split_hi(slab, k)

            def square_x(b):
                rows = P if b < NB else META
                if b == 0:
                    act.wait_ge(x0_full, 16)
                else:
                    act.wait_ge(x_full[b % 4], 16 * (b // 4 + (b % 4 > 0)))
                act.activation(JUNK[0:rows, :], XR[0:rows, b % 4, :], ACT.Square,
                               accum_out=SS[0:rows, b:b + 1]).then_inc(ss_rdy, 1)
                act.wait_ge(ss_rdy, b + 1)
                act.activation(STD[0:rows, b:b + 1], SS[0:rows, b:b + 1], ACT.Sqrt, scale=1.0 / D,
                               bias=EPSC[0:rows, 0:1]).then_inc(std_rdy, 1)

            def hi_x(b):
                for u in range(2):
                    act.wait_ge(xt_full, 2 * b + u + 1)
                    if b < NB:
                        lo, w = META + b * P, P
                    else:
                        lo, w = 0, META
                    act.copy(HN[:, 0, 4 * u:4 * u + 4, lo:lo + w],
                             B[2 + u][:, 0:4 * w].rearrange("p (k t) -> p k t", k=4)).then_inc(hn_hi, 1)

            act.wait_ge(eps_set, 1)
            square_x(0)
            for k in range(4):
                split_hi(0, k, first=True)
            hi_x(0)
            square_x(1)
            for k in range(4, KT):
                split_hi(0, k, first=True)
            for b in range(NB):
                hi_x(b + 1)
                if b + 2 <= NB:
                    square_x(b + 2)
                if b == NB - 1:
                    next_hi(1)
                act.wait_ge(a_full, b + 1)
                act.copy(RT[:, 0, b, :], B[b % 2][:, :]).then_inc(a_free, 1)
            with act.Fori(1, 4) as c:
                split_hi(c, KT - 1)
                act.wait_ge(meta_full, c)
                act.copy(MRK[0:META, c - 1, :], B[6][0:META, :]).then_inc(meta_free, 1)
                for b in range(NB):
                    if b == NB - 1:
                        next_hi(c + 1)
                    act.wait_ge(a_full, 8 * c + b + 1)
                    act.copy(RT[:, c, b, :], B[b % 2][:, :]).then_inc(a_free, 1)

            def tanh_gate(j, gi, uses):
                act.wait_ge(a_full, j + 1)
                act.wait_ge(gst_done[gi % 2], 16 * (uses + START))
                return act.activation(TB[:, gi % 2, :], B[gi % 2][:, :], ACT.Tanh, scale=0.5)

            with act.Fori(0, 2) as it:
                for r in range(4):
                    n = 4 * it + r
                    act.wait_ge(qt_full, n + START)
                    act.copy(QS[:, :], RT[:, 0, n, :]).then_inc(qs_rdy, 1)
                    if r == 0:
                        split_hi(SLAB_B + it, KT - 1)
                    act.wait_ge(qt_full, n + 1 + START)
                    act.wait_ge(o_full, n + START)
                    act.copy(QTR[:, :], B[2][:, :]).then_inc(qT_rdy, 1)
                    tanh_gate(ACT_B + 8 * it + 2 * r, 2 * r, 4 * it + r).then_inc(a_free, 1)
                    if r == 3:
                        for k in range(4):
                            split_hi(SLAB_B + it + 1, k)
                    act.wait_ge(oraw_rdy, n + 1 + START)
                    for h in range(HR):
                        sq = act.activation(JUNK[:, h * RV:(h + 1) * RV],
                                            RT[:, 2 + h // 2, n, (h % 2) * RV:(h % 2 + 1) * RV],
                                            ACT.Square, accum_out=SSR[:, n, h:h + 1])
                    sq.then_inc(sqr_rdy, 1)
                    if r == 3:
                        for k in range(4, KT - 1):
                            split_hi(SLAB_B + it + 1, k)
                    tanh_gate(ACT_B + 8 * it + 2 * r + 1, 2 * r + 1, 4 * it + r).then_inc(a_free, 1)

            split_hi(SLAB_C, KT - 1)
            act.wait_ge(st_rdy, NB + 1)
            act.wait_ge(meta_full, 4)
            act.copy(MKV[0:META, :], B[6][0:META, :]).then_inc(meta_free, 1)
            act.activation(ST[0:META, SL:SL + 256], B[6][0:META, 0:256], ACT.Square).then_inc(c_sq, 1)
            for b in range(NB):
                if b == NB - 1:
                    next_hi(SLAB_C + 1)
                act.wait_ge(a_full, ACT_C + b + 1)
                act.copy(KV[:, b + 1, :], B[b % 2][:, :])
                if b >= 1:
                    act.wait_ge(c_red, b)
                act.activation(ST[:, (b % 2) * SL:(b % 2) * SL + 256], B[b % 2][:, 0:256], ACT.Square)\
                   .then_inc(a_free, 1)
            def root(first_red, stats, scale=1.0 / HD):
                act.wait_ge(c_red, first_red)
                act.activation(stats, stats, ACT.Sqrt, scale=scale,
                               bias=EPSC[0:stats.shape[0], 0:1]).then_inc(c_std, 1)

            def hi_k(rows):
                return act.copy(KST[0:rows, 0, :, :].rearrange("p g (a d) -> p g a d", a=2),
                                KNF[0:rows, :].rearrange("p (g d) -> p g d", g=4).unsqueeze(2)
                                .to_broadcast([rows, 4, 2, HD]))

            def hi_qk(n):
                act.wait_ge(qf_rdy, n + 2)
                act.wait_ge(ak_full, 2 * (n + 1))
                if not (isinstance(n, int) and n == 0):
                    act.wait_ge(aq_full, 4 * n)
                act.copy(QST[:, :, 0, :], QNF[:, :].rearrange("p (h d) -> p h d", h=HS))
                hi_k(P).then_inc(qh_rdy, 1)

            for c in range(2):
                split_hi(SLAB_C + 1 + c, KT - 1)
                for b in range(NB):
                    if c == 1 and b == NB - 1:
                        hi_qk(0)
                    if b == NB - 1:
                        next_hi(SLAB_C + 2 + c)
                    act.wait_ge(a_full, ACT_C + 8 + 8 * c + b + 1)
                    act.copy(RT[:, c, b, :], B[b % 2][:, :])
                    act.wait_ge(c_red, 8 * c + b + 8)
                    act.activation(ST[:, (b % 2) * SL:(b % 2 + 1) * SL], B[b % 2][:, :], ACT.Square)\
                       .then_inc(a_free, 1)
                    if c == 1 and b == 4:
                        root(21, RSW[:, 0:4, :])
                        root(1, SSM[0:META, 0:4])
                    if c == 1 and b == 5:
                        act.wait_ge(qf_rdy, 1)
                        hi_k(META).then_inc(qh_rdy, 1)
            root(25, RSW[:, 4:NB, :])
            act.wait_ge(scr_step, 1)
            act.activation(SCR[:, :, :], SCR[:, :, :], ACT.Sqrt, bias=EPSC[:, 0:1]).then_inc(c_std, 1)

            def attention_block(pr, s, kind, last):
                n = 2 * pr + s
                for t in range(12):
                    if t == 0:
                        act.wait_ge(sc_full, HS * n + START)
                        for u in range(4):
                            act.wait_ge(aq_full, 4 * n + u + 1)
                            act.copy(QT[:, 4 * u:4 * u + 4, :],
                                     B[2 + u][:, :].rearrange("p (k t) -> p k t", k=4)).then_inc(aqT_rdy, 1)
                    if t == 0 and s == 0:
                        split_hi(SLAB_D + pr, KT - 1)
                    if 3 <= t <= 10:
                        p = t - 3
                        act.wait_ge(pt_full, 8 * n + p + 1)
                        act.wait_ge(pv_full, 8 * n + max(p - 1, 0) + START)
                        act.copy(PTS[:, p % 2, :, :],
                                 B[4 + p % 2][:, :].rearrange("p (k t) -> p k t", k=4)).then_inc(ptv_rdy, 1)
                    if 2 <= t <= 9:
                        p = t - 2
                        act.wait_ge(nm_rdy, 8 * n + p + 1)
                        act.wait_ge(se_rdy, 8 * n + p + 1)
                        act.activation(ES[:, s, 2 * p:2 * p + 2], SE[:, s, 2 * p:2 * p + 2], ACT.Exp)
                        for hl in range(2):
                            hh = 2 * p + hl
                            e = act.activation(PR[:, p % 2, hl * NKEY:(hl + 1) * NKEY],
                                               PR[:, p % 2, hl * NKEY:(hl + 1) * NKEY], ACT.Exp,
                                               bias=NM[:, s, hh:hh + 1], accum_out=RS[:, s, hh:hh + 1])
                        e.then_inc(e_rdy, 1)
                    if t == 10 and not last:
                        hi_qk(n + 1)
                    if s == 1 and t >= 9:
                        for k in KS_D[t - 9]:
                            if k < KT - 1:
                                split_hi(SLAB_D + pr + 1, k)
                    if t % 3 == 2:
                        q = t // 3
                        g = tanh_gate(ACT_D + 8 * pr + 4 * s + q, 4 * s + q, 8 + 4 * pr + 2 * s + q // 2)
                        g.then_inc(a_free if kind == 0 else th_rdy, 1)

            with act.Fori(0, 2) as pr:
                for s in range(2):
                    attention_block(pr, s, 0, False)
            for pr in (2, 3):
                for s in range(2):
                    attention_block(pr, s, 1, pr == 3 and s == 1)

            def hi_yr(b):
                for u in range(2):
                    act.wait_ge(yt_rdy, 2 * b + u + 1)
                    act.copy(YR[b // 4][:, 0, 4 * u:4 * u + 4, (b % 4) * P:(b % 4 + 1) * P],
                             TB[:, u, :].rearrange("p (k t) -> p k t", k=4)).then_inc(yh_rdy, 1)

            def hi_ys(i, b, u, bank):
                act.wait_ge(st_full, i + 1)
                act.copy(YS[b // 4][:, 0, 4 * u:4 * u + 4, (b % 4) * P:(b % 4 + 1) * P],
                         bank[:, :].rearrange("p (k t) -> p k t", k=4)).then_inc(sh_rdy, 1)

            for u in range(2):
                for b in range(4):
                    hi_ys(4 * u + b, b, u, B[2 + b])
            for j in range(32):
                if j == 0:
                    split_hi(SLAB_E, KT - 1)
                if j < 4:
                    for u in range(2):
                        hi_ys(8 + 2 * j + u, 4 + j, u, B[4 + u])
                if j % 8 == 7:
                    next_hi(SLAB_E + j // 8 + 1, KT)
                if 4 <= j < 8:
                    hi_yr(j - 4)
                elif 12 <= j < 16:
                    act.wait_ge(d_full, 12)
                    hi_yr(j - 8)
                if j >= 16:
                    i = j - 16
                    f, half = 4 * (i // 8) + i % 4, (i // 4) % 2
                    act.wait_ge(e2_sum, i + 1)
                    act.copy(MG[0][:, f, half * SL:(half + 1) * SL], TB[:, 1, :]).then_inc(e2_hi, 1)

            def hi_h(b):
                for u in range(2):
                    act.wait_ge(xt_full, 2 * (NB + 1) + 2 * b + u + 1)
                    act.copy(HN2[b // 4][:, 0, 4 * u:4 * u + 4, (b % 4) * P:(b % 4 + 1) * P],
                             B[2 + u][:, :].rearrange("p (k t) -> p k t", k=4)).then_inc(hn_hi, 1)

            def square_h(b):
                act.wait_ge(d_free, DVE_F + 8 + b + 1)
                act.activation(JUNK2[:, :], H1[:, b, :], ACT.Square, accum_out=SS2[:, b:b + 1]).then_inc(ss_rdy, 1)
                act.wait_ge(ss_rdy, NB + 1 + b + 1)
                act.activation(STD2[:, b:b + 1], SS2[:, b:b + 1], ACT.Sqrt, scale=1.0 / D,
                               bias=EPSC[:, 0:1]).then_inc(std_rdy, 1)

            next_hi(SLAB_F + 1, KT)
            for b in range(NB):
                if b >= 2:
                    hi_h(b - 2)
                if b == NB - 1:
                    next_hi(SLAB_H, KT)
                square_h(b)

            def mlp(g, last):
                for c in range(2):
                    for gi in range(8):
                        if isinstance(g, int) and g == c == 0 and gi in (0, 2):
                            hi_h(NB - 2 + gi // 2)
                        if gi == 7:
                            next_hi(SLAB_H + 4 * g + c + 1, KT)
                        i = 16 * g + 8 * c + gi
                        act.wait_ge(a_full, ACT_H + i + 1)
                        act.wait_ge(u_rdy, 16 * g + max(8 * c + gi - 1, 0) + START)
                        act.activation(TB[:, gi % 2, :], B[gi % 2][:, :], ACT.Relu).then_inc(a_free, 1)
                        act.wait_ge(sq_rdy, i + 1)
                        act.copy(U[0][:, 4 * c + gi % 4, (gi // 4) * SL:(gi // 4 + 1) * SL], TU[:, gi % 2, :])\
                           .then_inc(uh_rdy, 1)
                for c in range(2):
                    if not (last and c == 1):
                        next_hi(SLAB_H + 4 * g + 3 + c, KT)

            mlp(0, False)
            with act.Fori(1, FF_GROUPS - 1) as g:
                mlp(g, False)
            mlp(FF_GROUPS - 1, True)

        @block.vector
        def _(dve):
            for one in (sm_rdy, kT_rdy, oraw_rdy, ptm_rdy, y_rdy, sc_rdy, u_rdy):
                dve.sem_inc(one, START)
            def split_lo(slab, k):
                dve.wait_ge(w_hi, 8 * slab + k + 1)
                dve.tensor_tensor(WL[:, k, :], RAW[:, k % 4, :], WH[:, k, :].bitcast(F32), ALU.subtract)\
                   .then_inc(w_ready, 1)

            def next_lo(slab, tiles=KT - 1):
                for k in range(tiles):
                    split_lo(slab, k)

            dve.memset(EPSC[:, :], EPS).then_inc(eps_set, 1)

            def norm_x(b):
                rows = P if b < NB else META
                dve.wait_ge(std_rdy, b + 1)
                dve.reciprocal(RSTD[0:rows, b:b + 1], STD[0:rows, b:b + 1]).then_inc(rstd_rdy, 1)
                dve.wait_ge(rstd_rdy, b + 1)
                if b == 0:
                    dve.wait_ge(g_full, 16)
                if b >= 1:
                    dve.wait_ge(xt_full, 2 * b)
                dve.scalar_tensor_tensor(out=ST[0:rows, :], in0=XR[0:rows, b % 4, :], scalar=RSTD[0:rows, b:b + 1],
                                         in1=GBC[0:rows, :], op0=ALU.mult, op1=ALU.mult).then_inc(xn_rdy, 1)

            def lo_x(b):
                for u in range(2):
                    dve.wait_ge(hn_hi, 2 * b + u + 1)
                    if b < NB:
                        lo, w = META + b * P, P
                    else:
                        lo, w = 0, META
                    dve.tensor_tensor(HN[:, 1, 4 * u:4 * u + 4, lo:lo + w],
                                      B[2 + u][:, 0:4 * w].rearrange("p (k t) -> p k t", k=4),
                                      HN[:, 0, 4 * u:4 * u + 4, lo:lo + w].bitcast(F32), ALU.subtract)\
                       .then_inc(hn_lo, 1)

            norm_x(0)
            for k in range(4):
                split_lo(0, k)
            lo_x(0)
            for k in range(4, KT):
                split_lo(0, k)
            norm_x(1)
            for b in range(NB):
                lo_x(b + 1)
                if b + 2 <= NB:
                    norm_x(b + 2)
            next_lo(1)
            def heads(ap, n=HR):
                return ap.rearrange("p (h d) -> p h d", h=n)

            split_lo(1, KT - 1)
            dve.wait_ge(meta_free, 1 + START)
            dve.wait_ge(gst_done[0], 16)
            dve.wait_ge(gst_done[1], 16)
            dve.tensor_tensor(heads(KDM[0:META, :]), heads(MRK[0:META, 0, :]),
                              COLS[0:META, 1, :].unsqueeze(2).to_broadcast([META, HR, P]), ALU.mult)\
               .then_inc(kdm_rdy, 1)
            next_lo(2)
            with dve.Fori(2, 4) as c:
                split_lo(c, KT - 1)
                next_lo(c + 1)

            dve.wait_ge(c_full, 16 * 3)
            dve.wait_ge(u_full, 1)
            dve.tensor_copy(STA[:, 0:SL], B[6][:, :])
            dve.tensor_copy(STA[:, SL:2 * SL], B[7][:, :]).then_inc(st_rdy, 1)
            with dve.Fori(0, 2) as it:
                for r in range(4):
                    n = 4 * it + r
                    dve.wait_ge(kt_full, n + START)
                    dve.wait_ge(u_full, n + 1)
                    dve.tensor_tensor(heads(KD[:, :]), heads(RT[:, 1, n, :]),
                                      COLS[:, 0, :].unsqueeze(2).to_broadcast([P, HR, P]), ALU.mult)\
                       .then_inc(kd_rdy, 1)
                    if r == 0:
                        split_lo(SLAB_B + it, KT - 1)
                    dve.wait_ge(kt_full, n + 1 + START)
                    dve.wait_ge(s_full, n + START)
                    dve.tensor_copy(KTR[:, :], B[3][:, :]).then_inc(kT_rdy, 1)
                    dve.wait_ge(s_full, n + 1 + START)
                    dve.wait_ge(o_full, n + START)
                    dve.tensor_tensor(SMK[:, :], B[2][:, :], MASK[:, :], ALU.mult).then_inc(sm_rdy, 1)
                    if r == 3:
                        for k in range(4):
                            split_lo(SLAB_B + it + 1, k)
                    dve.wait_ge(o_full, n + 1 + START)
                    dve.wait_ge(u_full, n + 2)
                    for c in range(2):
                        cp = dve.tensor_copy(RT[:, 2 + c, n, :], B[4 + c][:, :])
                    cp.then_inc(oraw_rdy, 1)
                    for h in range(HR):
                        cp = dve.scalar_tensor_tensor(out=STA[:, h * RV:(h + 1) * RV], in0=STA[:, h * RV:(h + 1) * RV],
                                                      scalar=float(GAMMA[h] ** P),
                                                      in1=B[6 + h // 2][:, (h % 2) * RV:(h % 2 + 1) * RV],
                                                      op0=ALU.mult, op1=ALU.add)
                    cp.then_inc(st_rdy, 1)
                    if r == 3:
                        for k in range(4, KT - 1):
                            split_lo(SLAB_B + it + 1, k)

            def reduce_c(outap, inap):
                dve.tensor_reduce(outap, inap, AX_X, ALU.add).then_inc(c_red, 1)

            split_lo(SLAB_C, KT - 1)
            dve.memset(KV[:, 0, :], 0.0).then_inc(kv_zero, 1)
            dve.wait_ge(yraw_done, 16 * NB)
            dve.wait_ge(sqr_rdy, NB)
            dve.memset(MVB[:, :, :, :], 0.0).then_inc(d_small, 1)
            dve.wait_ge(kv_zero, 1)
            for part in range(2):
                dve.tensor_copy(KTS[part][:, :, META + P:NKEY], heads(KV[:, 0, :]))
            dve.tensor_copy(IDR[:, :], IDN[:, :])
            dve.tensor_scalar(NSK[:, :], SK[:, :], -1.0, None, ALU.mult)
            dve.scalar_tensor_tensor(out=GQK[:, :], in0=GQ[:, :], scalar=float(HD ** -0.5), in1=GK[:, :],
                                     op0=ALU.mult, op1=ALU.mult).then_inc(d_set, 1)
            dve.wait_ge(c_sq, 1)
            reduce_c(SSM[0:META, 0:4], heads(ST[0:META, SL:SL + 256]))
            for b in range(NB):
                if b == NB - 1:
                    next_lo(SLAB_C + 1)
                dve.wait_ge(a_free, ACT_C + b + 1)
                reduce_c(RSW[:, b, 16:20], heads(ST[:, (b % 2) * SL:(b % 2) * SL + 256]))
            def normed_k(index, rows, k, rstd):
                dve.tensor_tensor(heads(KNF[0:rows, :]), heads(k), rstd.unsqueeze(2).to_broadcast([rows, 4, HD]),
                                  ALU.mult).then_inc(kf_step, 1)
                dve.wait_ge(kf_step, index)
                return dve.tensor_tensor(heads(KNF[0:rows, :]), heads(KNF[0:rows, :]),
                                         GQK[0:rows, :].unsqueeze(1).to_broadcast([rows, 4, HD]), ALU.mult)

            def normed_qk(n):
                for t2 in range(2):
                    dve.tensor_tensor(heads(QNF[:, t2 * SL:(t2 + 1) * SL], 8), heads(RT[:, t2, n, :], 8),
                                      RSW[:, n, 8 * t2:8 * t2 + 8].unsqueeze(2).to_broadcast([P, 8, HD]), ALU.mult)
                dve.wait_ge(ql_rdy, n + 1)
                normed_k(n + 2, P, KV[:, n + 1, 0:256], RSW[:, n, 16:20]).then_inc(qf_rdy, 1)

            def lo_k(rows):
                return dve.tensor_tensor(KST[0:rows, 1, :, :].rearrange("p g (a d) -> p g a d", a=2),
                                         heads(KNF[0:rows, :]).unsqueeze(2).to_broadcast([rows, 4, 2, HD]),
                                         KST[0:rows, 0, :, :].rearrange("p g (a d) -> p g a d", a=2).bitcast(F32),
                                         ALU.subtract)

            def lo_qk(n):
                dve.wait_ge(qh_rdy, n + 2)
                dve.tensor_tensor(QST[:, :, 1, :], heads(QNF[:, :], HS), QST[:, :, 0, :].bitcast(F32), ALU.subtract)
                lo_k(P).then_inc(ql_rdy, 1)

            def take_k(index, w, *places):
                for part in range(2):
                    dve.wait_ge(ak_full, index + part)
                    for lo in places:
                        cp = dve.tensor_copy(KTS[part][:, :, lo:lo + w],
                                             B[6 + part][:, 0:4 * w].rearrange("p (k t) -> p k t", k=4))
                    cp.then_inc(akT_rdy, 1)

            def root_inverse(index, out_stats, stats):
                dve.wait_ge(c_std, index)
                dve.reciprocal(out_stats, stats).then_inc(c_rstd, 1)
                dve.wait_ge(c_rstd, index)

            for c in range(2):
                split_lo(SLAB_C + 1 + c, KT - 1)
                for b in range(NB):
                    if c == 1 and b == NB - 1:
                        lo_qk(0)
                    if b == NB - 1:
                        next_lo(SLAB_C + 2 + c)
                    dve.wait_ge(a_free, ACT_C + 8 + 8 * c + b + 1)
                    reduce_c(RSW[:, b, 8 * c:8 * c + 8],
                             heads(ST[:, (b % 2) * SL:(b % 2 + 1) * SL], 8))
                    if c == 1 and b == 4:
                        root_inverse(1, RSW[:, 0:4, :], RSW[:, 0:4, :])
                        root_inverse(2, SSM[0:META, 4:8], SSM[0:META, 0:4])
                        dve.wait_ge(d_set, 1)
                        normed_k(1, META, MKV[0:META, 0:256], SSM[0:META, 4:8]).then_inc(qf_rdy, 1)
                    if c == 1 and b == 5:
                        dve.wait_ge(qh_rdy, 1)
                        lo_k(META).then_inc(ql_rdy, 1)
                        normed_qk(0)
                    if c == 1 and b == 6:
                        take_k(1, META, 0, NKEY)
            dve.tensor_tensor(SCR[:, :, :], SSR[:, :, :], COLS[:, 2, :].unsqueeze(1).to_broadcast([P, NB, HR]),
                              ALU.mult).then_inc(scr_step, 1)
            root_inverse(3, RSW[:, 4:NB, :], RSW[:, 4:NB, :])
            root_inverse(4, SCR[:, :, :], SCR[:, :, :])
            dve.tensor_tensor(SCR[:, :, :], SCR[:, :, :], COLS[:, 3, :].unsqueeze(1).to_broadcast([P, NB, HR]),
                              ALU.mult).then_inc(scr_step, 1)


            def attention_block(pr, s, kind, last):
                n = 2 * pr + s
                for t in range(12):
                    if t == 0:
                        dve.wait_ge(sc_full, HS * n + START)
                        take_k(2 * n + 3, P, META + s * P)
                        if s == 0:
                            split_lo(SLAB_D + pr, KT - 1)
                        dve.wait_ge(dt_full[s], 16 * (pr + 1))
                    if 3 <= t <= 10:
                        p = t - 3
                        dve.wait_ge(ptm_full, 8 * n + p + 1)
                        if p >= 2:
                            dve.wait_ge(pv_full, 8 * n + p - 1 + START)
                        dve.tensor_copy(PTM[0:2 * META, p % 2, :], B[6][0:2 * META, 0:P]).then_inc(ptm_rdy, 1)
                    if 1 <= t <= 8:
                        p = t - 1
                        if p >= 2:
                            dve.wait_ge(ptm_full, 8 * n + p - 1)
                        for hl in range(2):
                            hh = 2 * p + hl
                            dve.wait_ge(sc_full, HS * n + hh + 1 + START)
                            dve.scalar_tensor_tensor(out=PR[:, p % 2, hl * NKEY:(hl + 1) * NKEY],
                                                     in0=DT[:, s, KEYS_OF[hl]],
                                                     scalar=SLOPES[hh], in1=B[2 + hh % 2][:, 0:NKEY],
                                                     op0=ALU.mult, op1=ALU.add).then_inc(sc_rdy, 1)
                        dve.wait_ge(sc_rdy, HS * n + 2 * p + 2 + START)
                        dve.tensor_reduce(MX[:, s, 2 * p:2 * p + 2], heads(PR[:, p % 2, :], 2), AX_X, ALU.max)\
                           .then_inc(mx_rdy, 1)
                        dve.wait_ge(mx_rdy, 8 * n + p + 1)
                        cs = slice(2 * p, 2 * p + 2)
                        dve.scalar_tensor_tensor(out=NM[:, s, cs], in0=MX[:, s, cs], scalar=-1.0,
                                                 in1=NSK[:, cs], op0=ALU.mult, op1=ALU.min).then_inc(nm_rdy, 1)
                        dve.wait_ge(nm_rdy, 8 * n + p + 1)
                        dve.tensor_tensor(SE[:, s, cs], SK[:, cs], NM[:, s, cs], ALU.add).then_inc(se_rdy, 1)
                    if t >= 4:
                        p = t - 4
                        cs = slice(2 * p, 2 * p + 2)
                        dve.wait_ge(e_rdy, 8 * n + p + 1)
                        dve.tensor_tensor(RS[:, s, cs], RS[:, s, cs], ES[:, s, cs], ALU.add).then_inc(den_rdy, 1)
                        dve.wait_ge(den_rdy, 16 * n + 2 * p + 1)
                        dve.reciprocal(ES[:, s, cs], RS[:, s, cs]).then_inc(den_rdy, 1)
                        dve.wait_ge(den_rdy, 16 * n + 2 * p + 2)
                        dve.wait_ge(pv_full, 8 * n + p + 1 + START)
                        dve.tensor_tensor(RT[:, p // 4, n, (p % 4) * P:(p % 4 + 1) * P]
                                          .rearrange("p (h d) -> p h d", h=2),
                                          B[7][:, 0:P].rearrange("p (h d) -> p h d", h=2),
                                          ES[:, s, cs].unsqueeze(2).to_broadcast([P, 2, HD]), ALU.mult)\
                           .then_inc(y_rdy, 1)
                    if t == 9 and not last:
                        normed_qk(n + 1)
                    if t == 10 and not last:
                        lo_qk(n + 1)
                    if s == 1 and t >= 9:
                        for k in KS_D[t - 9]:
                            if k < KT - 1:
                                split_lo(SLAB_D + pr + 1, k)
                    if t % 3 == 2 and kind == 1:
                        q = t // 3
                        dve.wait_ge(th_rdy, 8 * (pr - 2) + 4 * s + q + 1)
                        dve.scalar_tensor_tensor(out=TB[:, q % 2, :], in0=TB[:, q % 2, :], scalar=1.0,
                                                 in1=B[q % 2][:, :], op0=ALU.add, op1=ALU.mult)\
                           .then_inc(a_free, 1)

            with dve.Fori(0, 2) as pr:
                for s in range(2):
                    attention_block(pr, s, 0, False)
            for pr in (2, 3):
                for s in range(2):
                    attention_block(pr, s, 1, pr == 3 and s == 1)

            def scale_yr(b):
                dve.wait_ge(yb_full[b % 2], 16 * (b // 2 + 1))
                if b == 0:
                    dve.wait_ge(gm_full, 16)
                    dve.wait_ge(scr_step, 2)
                if b >= 1:
                    dve.wait_ge(yt_full, 2 * b)
                for h in range(HR):
                    y = dve.scalar_tensor_tensor(out=ST[:, h * RV:(h + 1) * RV],
                                                 in0=YB[:, b % 2, h * RV:(h + 1) * RV],
                                                 scalar=SCR[:, b, h:h + 1], in1=GBR[:, h * RV:(h + 1) * RV],
                                                 op0=ALU.mult, op1=ALU.mult)
                y.then_inc(ysc_rdy, 1)

            def gate_yr(b):
                for u in range(2):
                    dve.wait_ge(yt_full, 2 * b + u + 1)
                    if u == 0:
                        dve.wait_ge(gb_full[b % 2], 32 * (b // 2 + 1))
                        if b == 0:
                            dve.wait_ge(gst_done[0], 16 * (24 + START))
                            dve.wait_ge(gst_done[1], 16 * (24 + START))
                    dve.tensor_tensor(TB[:, u, :].rearrange("p (k t) -> p k t", k=4),
                                      B[2 + u][:, :].rearrange("p (k t) -> p k t", k=4),
                                      GB[:, b % 2, 4 * u:4 * u + 4, :], ALU.mult).then_inc(yt_rdy, 1)
                for u in range(2):
                    cols = slice((b % 4) * P, (b % 4 + 1) * P)
                    dve.wait_ge(yh_rdy, 2 * b + u + 1)
                    dve.tensor_tensor(YR[b // 4][:, 1, 4 * u:4 * u + 4, cols],
                                      TB[:, u, :].rearrange("p (k t) -> p k t", k=4),
                                      YR[b // 4][:, 0, 4 * u:4 * u + 4, cols].bitcast(F32), ALU.subtract)\
                       .then_inc(yl_rdy, 1)

            def lo_ys(i, b, u, bank):
                cols = slice((b % 4) * P, (b % 4 + 1) * P)
                dve.wait_ge(sh_rdy, i + 1)
                dve.tensor_tensor(YS[b // 4][:, 1, 4 * u:4 * u + 4, cols],
                                  bank[:, :].rearrange("p (k t) -> p k t", k=4),
                                  YS[b // 4][:, 0, 4 * u:4 * u + 4, cols].bitcast(F32), ALU.subtract)\
                   .then_inc(ysl_rdy, 1)

            for u in range(2):
                for b in range(4):
                    lo_ys(4 * u + b, b, u, B[2 + b])
            for j in range(32):
                if j == 0:
                    split_lo(SLAB_E, KT - 1)
                if j < 4:
                    for u in range(2):
                        lo_ys(8 + 2 * j + u, 4 + j, u, B[4 + u])
                if j % 8 == 7:
                    next_lo(SLAB_E + j // 8 + 1, KT)
                if 4 <= j < 8:
                    gate_yr(j - 4)
                elif 12 <= j < 16:
                    gate_yr(j - 8)
                i = j % 16
                f, half = 4 * (i // 8) + i % 4, (i // 4) % 2
                hs = slice(half * SL, (half + 1) * SL)
                dve.wait_ge(d_full, j + 1)
                dve.wait_ge(tg_full[j % 4], 16 * (j // 4 + 1))
                if j < 16:
                    dve.scalar_tensor_tensor(out=MR[:, f, hs], in0=TH[:, j % 4, :], scalar=1.0, in1=B[6 + j % 2][:, :],
                                             op0=ALU.add, op1=ALU.mult).then_inc(d_free, 1)
                    if 3 <= j < 7:
                        scale_yr(j - 3)
                    if 11 <= j < 15:
                        scale_yr(j - 7)
                else:
                    if j == 16:
                        dve.wait_ge(yl_rdy, 2 * NB)
                    dve.scalar_tensor_tensor(out=TB[:, 0, :], in0=TH[:, j % 4, :], scalar=1.0, in1=B[6 + j % 2][:, :],
                                             op0=ALU.add, op1=ALU.mult).then_inc(d_free, 1)
                    dve.wait_ge(d_free, j + 1)
                    dve.tensor_tensor(TB[:, 1, :], TB[:, 0, :], MR[:, f, hs], ALU.add).then_inc(e2_sum, 1)
                    dve.wait_ge(e2_hi, i + 1)
                    dve.tensor_tensor(MG[1][:, f, hs], TB[:, 1, :], MG[0][:, f, hs].bitcast(F32), ALU.subtract)\
                       .then_inc(mg_rdy, 1)

            def norm_h(b):
                dve.wait_ge(std_rdy, NB + 1 + b + 1)
                dve.reciprocal(RSTD2[:, b:b + 1], STD2[:, b:b + 1]).then_inc(rstd_rdy, 1)
                dve.wait_ge(rstd_rdy, NB + 1 + b + 1)
                if b == 0:
                    dve.wait_ge(gm_full, 32)
                else:
                    dve.wait_ge(xt_full, 2 * (NB + 1) + 2 * b)
                dve.scalar_tensor_tensor(out=ST[:, :], in0=H1[:, b, :], scalar=RSTD2[:, b:b + 1],
                                         in1=GBM[:, :], op0=ALU.mult, op1=ALU.mult).then_inc(xn_rdy, 1)

            def lo_h(b):
                cols = slice((b % 4) * P, (b % 4 + 1) * P)
                for u in range(2):
                    dve.wait_ge(hn_hi, 2 * (NB + 1) + 2 * b + u + 1)
                    dve.tensor_tensor(HN2[b // 4][:, 1, 4 * u:4 * u + 4, cols],
                                      B[2 + u][:, :].rearrange("p (k t) -> p k t", k=4),
                                      HN2[b // 4][:, 0, 4 * u:4 * u + 4, cols].bitcast(F32), ALU.subtract)\
                       .then_inc(hn_lo, 1)

            for c in range(2):
                for b in range(NB):
                    j = DVE_F + 8 * c + b
                    if c == 1 and b >= 2:
                        lo_h(b - 2)
                    if b == NB - 1:
                        next_lo(SLAB_F + c + 1, KT)
                    if c == 0:
                        dve.wait_ge(xres_full[b], 16)
                    dve.wait_ge(d_full, j + 1)
                    dve.scalar_tensor_tensor(out=H1[:, b, c * SL:(c + 1) * SL], in0=B[6 + j % 2][:, :], scalar=0.5,
                                             in1=H1[:, b, c * SL:(c + 1) * SL], op0=ALU.mult, op1=ALU.add)\
                       .then_inc(d_free, 1)
                    if c == 1:
                        norm_h(b)
            def mlp(g, last):
                for c in range(2):
                    for gi in range(8):
                        if isinstance(g, int) and g == c == 0 and gi in (0, 2):
                            lo_h(NB - 2 + gi // 2)
                        if gi == 7:
                            next_lo(SLAB_H + 4 * g + c + 1, KT)
                        i = 16 * g + 8 * c + gi
                        fs, hs = 4 * c + gi % 4, slice((gi // 4) * SL, (gi // 4 + 1) * SL)
                        dve.wait_ge(a_free, ACT_H + i + 1)
                        dve.tensor_tensor(TU[:, gi % 2, :], TB[:, gi % 2, :], TB[:, gi % 2, :], ALU.mult)\
                           .then_inc(sq_rdy, 1)
                        dve.wait_ge(uh_rdy, i + 1)
                        dve.tensor_tensor(U[1][:, fs, hs], TU[:, gi % 2, :], U[0][:, fs, hs].bitcast(F32),
                                          ALU.subtract).then_inc(u_rdy, 1)
                for c in range(2):
                    for b in range(NB):
                        if b == NB - 1 and not (last and c == 1):
                            next_lo(SLAB_H + 4 * g + 3 + c, KT)
                        dve.wait_ge(d_full, DVE_H + 16 * g + 8 * c + b + 1)
                        dve.tensor_tensor(H1[:, b, c * SL:(c + 1) * SL], B[6 + b % 2][:, :],
                                          H1[:, b, c * SL:(c + 1) * SL], ALU.add).then_inc(d_free, 1)

            mlp(0, False)
            with dve.Fori(1, FF_GROUPS - 1) as g:
                mlp(g, False)
            mlp(FF_GROUPS - 1, True)


_INS = ["x", "meta_tokens", "mix_norm_g", "w_in", "ret_norm_g", "q_norm_g", "k_norm_g", "sinks",
        "w_ret_branch", "w_swa_branch", "w_out", "mlp_norm_g", "w_up", "w_down"]


def kernel(**inputs):
    import concourse.bacc as bacc
    from concourse.bass_utils import run_bass_kernel_spmd

    nc = bacc.Bacc("TRN2", target_bir_lowering=False, num_devices=1, dynamic_dma_scratch_size=4096)
    shapes = {"x": (T, D), "q_norm_g": (HD,), "k_norm_g": (HD,), "mix_norm_g": (D,), "mlp_norm_g": (D,),
              "ret_norm_g": (HR * RV,), "sinks": (HS,)}
    arrays, args = {}, []
    for name in _INS:
        a = np.ascontiguousarray(inputs[name])
        a = a.reshape(shapes.get(name, a.shape[-2:]))
        arrays[f"in_{name}"] = a
    arrays.update(shape_constants())
    for name, a in arrays.items():
        args.append(nc.dram_tensor(name, a.shape, mybir.dt.from_np(a.dtype), kind="ExternalInput").ap())
    args.append(nc.dram_tensor("h_out", (T, D), F32, kind="ExternalOutput").ap())
    build(nc, *args)
    r = run_bass_kernel_spmd(nc, [arrays], core_ids=[0])
    return r.results[0]["h_out"].reshape(1, T, D)
```

```python
from contextlib import ExitStack

import numpy as np

import concourse.bass as bass
import concourse.mybir as mybir

F32 = mybir.dt.float32
F32R = mybir.dt.float32r
ALU = mybir.AluOpType
ACT = mybir.ActivationFunctionType
AX_X = mybir.AxisListType.X

P = 128
D = 1024
KT = D // P
T = 1024
NB = T // P
META = 16
SL = 512
HR, RV = 4, 256
HS, HD = 16, 64
NKEY = META + 2 * P
WKEY = NKEY + META
KEYS_OF = [slice(META, WKEY), slice(0, NKEY)]
EPS = 1e-6
FF_GROUPS = 4
COL_GR, COL_GS, COL_RG, COL_SQ, COL_KV = 4608, 5632, 2048, 3072, 4096

SLAB_B, SLAB_C, SLAB_D, SLAB_E, SLAB_F, SLAB_H = 4, 6, 9, 13, 17, 19
ACT_B, ACT_C, ACT_D, ACT_H = 32, 48, 72, 104
DVE_F, DVE_H = 32, 48
START = 1
KS_D = [[0, 1, 2], [3, 4, 5], [6, 7]]
SLOPES = [float(2.0 ** (-8.0 * (h + 1) / HS)) for h in range(HS)]
GAMMA = [1.0 - 2.0 ** (-5.0 - h) for h in range(HR)]


def shape_constants():
    ident = np.eye(P, dtype=np.float32)
    i = np.arange(P, dtype=np.float64)
    lg = np.log1p(-(2.0 ** (-5.0 - np.arange(HR, dtype=np.float64))))
    kscale = 128.0 ** -0.5
    mask = (i[:, None] <= i[None, :])[:, None, :] * np.exp(-P * lg)[None, :, None]
    kdec = np.exp(lg[None, :] * (P - 1 - i)[:, None]) * kscale
    kdec_meta = np.zeros((P, HR))
    kdec_meta[:META] = kdec[P - META:]
    qsq = np.exp(2 * lg[None, :] * (i + 1)[:, None]) / RV
    qhalf = 0.5 * np.exp(lg[None, :] * (i + 1)[:, None])
    cols = np.concatenate([kdec, kdec_meta, qsq, qhalf], axis=1)
    dist = np.full((NB + 1, P, WKEY), -1e30)
    for n in range(NB):
        dist[n, :, :META] = -((n + 1) * P + i[:, None] - (P - META + np.arange(META))[None, :])
        dist[n, :, NKEY:] = dist[n, :, :META]
        own = META + P * (n % 2)
        other = META + P * (1 - n % 2)
        d = i[:, None] - i[None, :]
        dist[n, :, own:own + P] = np.where(d >= 0, -d, -1e30)
        if n > 0:
            d = d + P
            dist[n, :, other:other + P] = np.where(d < P, -d, -1e30)
    f = lambda a: np.ascontiguousarray(a, dtype=np.float32)
    return {"c_ident": f(ident), "c_mask": f(mask.reshape(P, HR * P)), "c_cols": f(cols), "c_dist": f(dist)}


def build(nc, x, meta, g_mix, w_in, g_ret, g_q, g_k, sinks, w_ret, w_swa, w_out, g_mlp, w_up, w_down,
          c_ident, c_mask, c_cols, c_dist, out):
    with ExitStack() as ctx:
        base = (nc.sbuf_base + 63) // 64 * 64
        O_R0, O_R1 = 0, 32768
        O_HM = 2 * KT * T * 4
        O_Q = O_HM + KT * 2 * META * 4
        O_V = O_Q + 32768
        O_M = O_V + 32768
        O_WH = O_M + 32768
        O_WL = O_WH + KT * SL * 4
        O_RAW = O_WL + KT * SL * 4
        O_ST = O_RAW + 4 * SL * 4
        O_TB = O_ST + D * 4
        O_ID = O_TB + 2 * SL * 4
        O_SM = O_ID + P * 4
        O_X = O_SM + 1088

        def at(name, off, shape, dt=F32):
            return nc.alloc_sbuf_tensor_at(name, [P, *shape], dt, offset=base + off)

        HN = at("HN", 0, [2, KT, T], F32R)
        HM = at("HM", O_HM, [KT, 2 * META], F32R)
        RT = at("RT", O_Q, [4, NB, SL])
        YS = [at("YS0", O_R0, [2, KT, SL], F32R), at("YS1", O_R1, [2, KT, SL], F32R)]
        YR = [at("YR0", O_Q, [2, KT, SL], F32R), at("YR1", O_R0, [2, KT, SL], F32R)]
        HN2 = [at("HN20", O_Q, [2, KT, SL], F32R), at("HN21", O_R0, [2, KT, SL], F32R)]
        H1 = at("H1", O_R1, [NB, D])
        MR = at("MR", O_M, [KT, T])
        MG = [at("MGH", O_M, [KT, T], F32R), at("MGL", O_V, [KT, T], F32R)]
        U = [at("UH", O_M, [KT, T], F32R), at("UL", O_V, [KT, T], F32R)]
        WH = at("WH", O_WH, [KT, SL], F32R)
        WL = at("WL", O_WL, [KT, SL], F32R)
        RAW = at("RAW", O_RAW, [4, SL])
        ST = at("ST", O_ST, [D])
        TB = at("TB", O_TB, [2, SL])
        IDN = at("IDN", O_ID, [P])
        SS = at("SS", O_SM, [16])
        STD = at("STD", O_SM + 64, [16])
        RSTD = at("RSTD", O_SM + 128, [16])
        SS2 = at("SS2", O_SM + 192, [NB])
        STD2 = at("STD2", O_SM + 224, [NB])
        RSTD2 = at("RSTD2", O_SM + 256, [NB])
        COLS = at("COLS", O_SM + 288, [4, HR])
        SSR = at("SSR", O_SM + 352, [NB, HR])
        SCR = at("SCR", O_SM + 480, [NB, HR])
        EPSC = at("EPSC", O_SM + 608, [1])
        SK = at("SK", O_SM + 672, [HS])
        NSK = at("NSK", O_SM + 736, [HS])
        SSM = at("SSM", O_SM + 800, [8])
        GBC = at("GBC", O_M, [D])
        XR = at("XR", O_M + 4096, [4, D])
        MRK = at("MRK", O_M + 24576, [3, SL])
        MU = at("MU", O_M + 18432, [3, SL])
        JUNK = at("JUNK", O_X, [D])
        QS = at("QS", O_M, [SL])
        KD = at("KD", O_M + 2048, [SL])
        QTR = at("QTR", O_M + 4096, [SL])
        KTR = at("KTR", O_M + 6144, [SL])
        SMK = at("SMK", O_M + 8192, [SL])
        STA = at("STA", O_M + 10240, [HR * RV])
        KDM = at("KDM", O_M + 14336, [SL])
        MASK = at("MASK", O_X + 4096, [SL])
        JUNKB = at("JUNKB", O_M + 4096, [HR * RV])
        SMH, SML = at("SMH", O_X + 1024, [SL], F32R), at("SML", O_M + 8192, [SL], F32R)
        KDH, KDL = at("KDH", O_M + 14336, [SL], F32R), at("KDL", O_M + 2048, [SL], F32R)
        QTH, QTL = at("QTH", O_M + 28672, [SL], F32R), at("QTL", O_X + 6144, [SL], F32R)
        VH, VL = at("VH", O_M + 16384, [2, SL], F32R), at("VL", O_M + 20480, [2, SL], F32R)
        STH, STL = at("STH", O_ST, [HR * RV], F32R), at("STL", O_M + 24576, [HR * RV], F32R)
        KV = at("KV", O_M, [NB + 1, SL])
        MKV = at("MKV", O_M + 18432, [SL])
        MU2 = at("MU2", O_M + 28672, [SL])
        KST = at("KST", O_M + 21504, [2, 4, P], F32R)
        GQ = at("GQ", O_M + 30720, [HD])
        GK = at("GK", O_M + 30976, [HD])
        GQK = at("GQK", O_M + 25600, [HD])
        KNF = at("KNF", O_M + 25856, [256])
        PTS = at("PTS", O_M + 27776, [2, 4, P])
        RSW = at("RSW", O_M + 31872, [NB, 20])
        PR = at("PR", O_X, [2, 2 * NKEY])
        PTM = at("PTM", O_X + 4352, [2, P])
        DT = at("DT", O_X + 6144, [2, WKEY])
        MX = at("MX", O_X + 8576, [2, HS])
        NM = at("NM", O_X + 8704, [2, HS])
        SE = at("SE", O_X + 8832, [2, HS])
        RS = at("RS", O_X + 8960, [2, HS])
        ES = at("ES", O_X + 9088, [2, HS])
        QNF = at("QNF", O_V, [D])
        QST = at("QST", O_V + 4096, [HS, 2, HD], F32R)
        QT = at("QT", O_V + 12288, [HS, P], F32R)
        KTS = [at("KTH", O_V + 20480, [4, WKEY], F32R), at("KTL", O_V + 25088, [4, WKEY], F32R)]
        IDR = at("IDR", O_V + 29696, [P], F32R)
        MVB = at("MVB", O_V + 30720, [4, 2, HD])
        YB = at("YB", O_V, [2, D])
        GB = at("GB", O_V + 8192, [2, KT, P])
        GBR = at("GBR", O_V + 16384, [D])
        TH = at("TH", O_X, [4, SL])
        GBM = at("GBM", O_X, [D])
        TU = at("TU", O_X + 4096, [2, SL])
        JUNK2 = at("JUNK2", O_X + 4096, [D])

        B = [ctx.enter_context(nc.psum_tensor(f"bank{i}", [P, SL], F32)) for i in range(8)]

        y_raw = nc.dram_tensor("y_raw", [NB, P, 2, SL], F32, kind="Internal").ap()
        gates = nc.dram_tensor("gates", [6, 2, 4, P, SL], F32, kind="Internal").ap()

        def x_part(b, u, part):
            ks = slice(4 * u, 4 * u + 4)
            return HN[:, part, ks, b * P:(b + 1) * P] if b < NB else HM[:, ks, part * META:(part + 1) * META]

        def ys_bank(b, u):
            return B[2 + b] if u == 0 else B[b]

        def sem(name):
            return ctx.enter_context(nc.semaphore(name))

        raw_full = [sem(f"raw_full{i}") for i in range(4)]
        w_hi, w_ready, w_free = sem("w_hi"), sem("w_ready"), sem("w_free")
        a_full, a_free, d_full, d_free = sem("a_full"), sem("a_free"), sem("d_full"), sem("d_free")
        id_full, c_full = sem("id_full"), sem("c_full")
        g_full = sem("g_full")
        x0_full = sem("x0_full")
        x_full = [sem(f"x_full{i}") for i in range(4)]
        ss_rdy, std_rdy, rstd_rdy, xn_rdy = sem("ss_rdy"), sem("std_rdy"), sem("rstd_rdy"), sem("xn_rdy")
        xt_full, hn_hi, hn_lo = sem("xt_full"), sem("hn_hi"), sem("hn_lo")
        meta_full, meta_free = sem("meta_full"), sem("meta_free")
        mu_full, meta_sum = sem("mu_full"), sem("meta_sum")
        eps_set = sem("eps_set")
        kdm_rdy, kd_rdy, qs_rdy = sem("kdm_rdy"), sem("kd_rdy"), sem("qs_rdy")
        qt_full, kt_full, qT_rdy, kT_rdy = sem("qt_full"), sem("kt_full"), sem("qT_rdy"), sem("kT_rdy")
        s_full, sm_rdy, o_full, u_full = sem("s_full"), sem("sm_rdy"), sem("o_full"), sem("u_full")
        kdh_rdy, kdl_rdy, vh_rdy, vl_rdy = sem("kdh_rdy"), sem("kdl_rdy"), sem("vh_rdy"), sem("vl_rdy")
        qth_rdy, sth_rdy, smh_rdy, sml_rdy = sem("qth_rdy"), sem("sth_rdy"), sem("smh_rdy"), sem("sml_rdy")
        st_rdy, oraw_rdy, sqr_rdy = sem("st_rdy"), sem("oraw_rdy"), sem("sqr_rdy")
        gst_done = [sem("gst_done0"), sem("gst_done1")]
        c_sq, c_red, c_std, c_rstd, scr_step = sem("c_sq"), sem("c_red"), sem("c_std"), sem("c_rstd"), sem("scr_step")
        d_small, d_set = sem("d_small"), sem("d_set")
        qf_rdy, qh_rdy, ql_rdy = sem("qf_rdy"), sem("qh_rdy"), sem("ql_rdy")
        aq_full, ak_full, aqT_rdy, akT_rdy = sem("aq_full"), sem("ak_full"), sem("aqT_rdy"), sem("akT_rdy")
        kf_step, kv_zero = sem("kf_step"), sem("kv_zero")
        yraw_done, mvb_done = sem("yraw_done"), sem("mvb_done")
        yb_full = [sem("yb_full0"), sem("yb_full1")]
        sc_full, sc_rdy, mx_rdy, nm_rdy, se_rdy, e_rdy = (sem("sc_full"), sem("sc_rdy"), sem("mx_rdy"), sem("nm_rdy"),
                                                         sem("se_rdy"), sem("e_rdy"))
        pt_full, ptm_full, ptv_rdy, ptm_rdy = sem("pt_full"), sem("ptm_full"), sem("ptv_rdy"), sem("ptm_rdy")
        pv_full, y_rdy, den_rdy = sem("pv_full"), sem("y_rdy"), sem("den_rdy")
        dt_full = [sem("dt_full0"), sem("dt_full1")]
        th_rdy = sem("th_rdy")
        gb_full = [sem("gb_full0"), sem("gb_full1")]
        ysc_rdy, yt_full = sem("ysc_rdy"), sem("yt_full")
        yt_rdy, yh_rdy, yl_rdy = sem("yt_rdy"), sem("yh_rdy"), sem("yl_rdy")
        st_full, sh_rdy, ysl_rdy = sem("st_full"), sem("sh_rdy"), sem("ysl_rdy")
        tg_full = [sem(f"tg_full{i}") for i in range(4)]
        e2_sum, e2_hi, mg_rdy = sem("e2_sum"), sem("e2_hi"), sem("mg_rdy")
        xres_full = [sem(f"xres_full{i}") for i in range(NB)]
        gm_full = sem("gm_full")
        sq_rdy, uh_rdy, u_rdy = sem("sq_rdy"), sem("uh_rdy"), sem("u_rdy")
        out_done = sem("out_done")

        block = ctx.enter_context(nc.Block())

        @block.sync
        def _(sp):
            def load_slab(slab, source, first=False):
                for k in range(KT):
                    if not (first and k < 4):
                        sp.wait_ge(w_ready, 8 * slab + k - 3)
                    sp.dma_start(RAW[:, k % 4, :], source(k)).then_inc(raw_full[k % 4], 16)

            def w_cols(w, col):
                return lambda k: w[k * P:(k + 1) * P, col:col + SL] if isinstance(col, int) else \
                    w[k * P:(k + 1) * P, bass.ds(col, SL)]

            sp.dma_start(XR[:, 0, :], x[0:P, :]).then_inc(x0_full, 16)
            sp.dma_start(GBC[:, :], g_mix.partition_broadcast(P)).then_inc(g_full, 16)
            load_slab(0, w_cols(w_in, 0), first=True)
            with sp.Fori(1, 4) as c:
                load_slab(c, w_cols(w_in, c * SL))
            with sp.Fori(0, 2) as c:
                load_slab(SLAB_B + c, w_cols(w_in, COL_GR + c * SL))
            load_slab(SLAB_C, w_cols(w_in, COL_KV))
            with sp.Fori(0, 2) as c:
                load_slab(SLAB_C + 1 + c, w_cols(w_in, COL_SQ + c * SL))
            with sp.Fori(0, 2) as c:
                load_slab(SLAB_D + c, w_cols(w_in, COL_GS + c * SL))
            with sp.Fori(0, 2) as c:
                load_slab(SLAB_D + 2 + c, w_cols(w_in, COL_RG + c * SL))
            for i, w in enumerate((w_swa, w_ret, w_out)):
                with sp.Fori(0, 2) as c:
                    load_slab(SLAB_E + 2 * i + c, w_cols(w, c * SL))
            with sp.Fori(0, FF_GROUPS) as g:
                for c in range(2):
                    load_slab(SLAB_H + 4 * g + c, w_cols(w_up, g * D + c * SL))
                for c in range(2):
                    load_slab(SLAB_H + 4 * g + 2 + c,
                              lambda k: w_down[bass.ds(g * D + k * P, P), c * SL:(c + 1) * SL])
            for c in range(2):
                for b in range(NB):
                    sp.wait_ge(d_free, DVE_H + 16 * (FF_GROUPS - 1) + 8 * c + b + 1)
                    sp.dma_start(out[b * P:(b + 1) * P, c * SL:(c + 1) * SL],
                                 H1[:, b, c * SL:(c + 1) * SL]).then_inc(out_done, 16)
            sp.wait_ge(out_done, 16 * 2 * NB)

        @block.gpsimd
        def _(pool):
            pool.dma_start(IDN[:, :], c_ident).then_inc(id_full, 16)

            def load_x(b):
                if b >= 4:
                    pool.wait_ge(xn_rdy, b - 3)
                if b < NB:
                    pool.dma_start(XR[:, b % 4, :], x[b * P:(b + 1) * P, :]).then_inc(x_full[b % 4], 16)
                else:
                    pool.dma_start(XR[0:META, b % 4, :], meta).then_inc(x_full[b % 4], 16)

            load_x(1)
            pool.wait_ge(w_ready, 4)
            load_x(2)
            load_x(3)
            pool.dma_start(MASK[:, :], c_mask).then_inc(gst_done[0], 16)
            pool.dma_start(COLS[:, :, :], c_cols.rearrange("p (a h) -> p a h", a=4)).then_inc(gst_done[1], 16)
            pool.dma_start(SK[:, :], sinks.partition_broadcast(P)).then_inc(c_full, 16)
            pool.dma_start(GQ[:, :], g_q.partition_broadcast(P)).then_inc(c_full, 16)
            pool.dma_start(GK[:, :], g_k.partition_broadcast(P)).then_inc(c_full, 16)
            for b in range(4, NB + 1):
                load_x(b)

            pool.wait_ge(meta_free, 3 + START)
            pool.wait_ge(xn_rdy, NB + 1)
            pool.dma_start(MU[0:META, :, :], MRK[META:2 * META, :, :]).then_inc(mu_full, 16)

            def store_gate(a_index, slab6, gi):
                pool.wait_ge(a_free, a_index + 1)
                pool.dma_start(gates[slab6, gi // 4, gi % 4], TB[:, gi % 2, :]).then_inc(gst_done[gi % 2], 16)

            with pool.Fori(0, 2) as it:
                for gi in range(8):
                    store_gate(ACT_B + 8 * it + gi, it, gi)
                    if gi % 2 == 1:
                        r = gi // 2
                        pool.wait_ge(oraw_rdy, 4 * it + r + 1 + START)
                        pool.dma_start(y_raw[4 * it + r], RT[:, 2:4, 4 * it + r, :]).then_inc(yraw_done, 16)
            pool.wait_ge(st_rdy, NB + 1)
            pool.wait_ge(sqr_rdy, NB + START)
            pool.dma_start(DT[:, 0, :], c_dist[0]).then_inc(dt_full[0], 16)
            pool.wait_ge(meta_free, 4 + START)
            pool.dma_start(MU2[0:META, :], MKV[META:2 * META, :]).then_inc(mu_full, 16)
            pool.wait_ge(meta_sum, 2)
            pool.wait_ge(d_small, 1)
            for hl in range(2):
                pool.dma_start(MVB[hl * META:(hl + 1) * META, :, hl, :],
                               MKV[0:META, 256:512].rearrange("p (g d) -> p g d", g=4)).then_inc(mvb_done, 16)
            with pool.Fori(0, 4) as pr:
                for s in range(2):
                    pool.wait_ge(sc_rdy, HS * (2 * pr + s) + START)
                    pool.dma_start(DT[:, 1 - s, :], c_dist[2 * pr + s + 1]).then_inc(dt_full[1 - s], 16)
                    for q in range(4):
                        store_gate(ACT_D + 8 * pr + 4 * s + q, 2 + pr, 4 * s + q)
            pool.wait_ge(gst_done[0], 16 * (24 + START))
            pool.wait_ge(gst_done[1], 16 * (24 + START))
            pool.wait_ge(y_rdy, 8 * NB + START)
            pool.wait_ge(dt_full[0], 16 * 5)
            pool.dma_start(GBR[:, :], g_ret.partition_broadcast(P)).then_inc(gm_full, 16)

            def load_tg(i):
                if i >= 4:
                    pool.wait_ge(d_free, i - 3)
                slab6 = 2 + i // 8 if i < 16 else i // 8 - 2
                pool.dma_start(TH[:, i % 4, :], gates[slab6, (i // 4) % 2, i % 4]).then_inc(tg_full[i % 4], 16)

            def load_yr(b):
                if b >= 2:
                    pool.wait_ge(ysc_rdy, b - 1)
                pool.dma_start(YB[:, b % 2, :].rearrange("p (c s) -> p c s", c=2), y_raw[b])\
                    .then_inc(yb_full[b % 2], 16)
                if b >= 2:
                    pool.wait_ge(yt_rdy, 2 * (b - 1))
                for c in range(2):
                    pool.dma_start(GB[:, b % 2, 4 * c:4 * c + 4, :],
                                   gates[4 + c, b // 4, :, :, (b % 4) * P:(b % 4 + 1) * P].rearrange(
                                       "f p t -> p f t")).then_inc(gb_full[b % 2], 16)

            for i in range(4):
                load_tg(i)
            load_yr(0)
            load_yr(1)
            for i in range(4, 8):
                load_tg(i)
            for b in range(2, 6):
                load_yr(b)
                load_tg(b + 6)
            for i in range(12, 16):
                load_tg(i)
            load_yr(6)
            load_yr(7)
            load_tg(16)
            load_tg(17)
            pool.wait_ge(d_full, 16)
            for i in range(18, 32):
                load_tg(i)
                if i - 18 < NB:
                    b = i - 18
                    pool.dma_start(H1[:, b, :], x[b * P:(b + 1) * P, :]).then_inc(xres_full[b], 16)
            pool.wait_ge(d_free, DVE_F)
            pool.dma_start(GBM[:, :], g_mlp.partition_broadcast(P)).then_inc(gm_full, 16)

        @block.tensor
        def _(pe):
            for one in (qt_full, kt_full, s_full, o_full, sc_full, pv_full):
                pe.sem_inc(one, START)
            def three(bank, ahi, alo, bhi, blo, first, last, frees):
                mm = pe.matmul(bank, ahi, bhi, start=first, stop=False)
                if frees:
                    mm.then_inc(w_free, 1)
                pe.matmul(bank, alo, bhi, start=False, stop=False)
                return pe.matmul(bank, ahi, blo, start=False, stop=last)

            def step(form, bank, k, f, act, slab, opening, closing):
                if opening:
                    pe.wait_ge(w_ready, 8 * slab + k + 1)
                frees = opening and k == 0 and not (isinstance(slab, int) and slab == 0)
                hi, lo = act(k)
                if form == "S":
                    fs = slice(f * P, (f + 1) * P)
                    mm = three(bank[:, :], WH[:, k, fs], WL[:, k, fs], hi, lo, k == 0, k == KT - 1, frees)
                else:
                    mm = three(bank[:, :], hi, lo, WH[:, k, :], WL[:, k, :], k == 0, k == KT - 1, frees)
                if closing and k < KT - 1:
                    mm.then_inc(w_free, 1)
                return mm

            def hn_block(b):
                lo = b * P
                return lambda k: (HN[:, 0, k, lo:lo + P], HN[:, 1, k, lo:lo + P])

            def meta_group():
                def both_rows(k, last):
                    return pe.matmul(B[6][0:2 * META, :], HM[:, k, :], WH[:, k, :], start=k == 0, stop=last)

                for k in range(KT):
                    if k < KT - 1:
                        both_rows(k, False)
                    pe.matmul(B[6][0:META, :], HM[:, k, 0:META], WL[:, k, :], start=False, stop=False)
                both_rows(KT - 1, True).then_inc(meta_full, 1)

            def hn_half(half):
                lo = half * SL
                return lambda k: (HN[:, 0, k, lo:lo + SL], HN[:, 1, k, lo:lo + SL])

            def halves(pair, half):
                return lambda k: (pair[half][:, 0, k, :], pair[half][:, 1, k, :])

            def tokens(pair, b):
                return lambda k: (pair[0][:, k, b * P:(b + 1) * P], pair[1][:, k, b * P:(b + 1) * P])

            def bank_wait(j, loop=False):
                if loop or j >= 2:
                    pe.wait_ge(a_free, j - 1)

            def dense_a(form, j, bank, f, act, slab, opening, closing, loop=True, middle=None):
                bank_wait(j, loop)
                for k in range(KT):
                    mm = step(form, bank, k, f, act, slab, opening, closing)
                    if middle and k == 3:
                        middle()
                mm.then_inc(a_full, 1)

            pe.wait_ge(id_full, 16)

            def transpose_x(b):
                pe.wait_ge(xn_rdy, b + 1)
                if b >= 1:
                    pe.wait_ge(hn_lo, 2 * b)
                rows, w = (P, P) if b < NB else (META, META)
                for k in range(KT):
                    bank = B[2 + k // 4]
                    mm = pe.transpose(bank[:, (k % 4) * w:(k % 4) * w + w], ST[0:rows, k * P:(k + 1) * P],
                                      IDN[0:rows, 0:rows])
                    if k % 4 == 3:
                        mm.then_inc(xt_full, 1)

            transpose_x(0)
            for b in range(NB):
                pe.wait_ge(hn_lo, 2 * (b + 1))
                dense_a("M", b, B[b % 2], 0, hn_block(b), 0, b == 0, b == NB - 1, loop=False,
                        middle=lambda b=b: transpose_x(b + 1))
            pe.wait_ge(hn_lo, 2 * (NB + 1))
            with pe.Fori(1, 4) as c:
                for b in range(NB):
                    dense_a("M", 8 * c + b, B[b % 2], 0, hn_block(b), c, b == 0, b == NB - 1)
                    if b == 0:
                        pe.wait_ge(meta_free, c - 1 + START)
                        meta_group()

            pe.wait_ge(kdm_rdy, 1)
            pe.wait_ge(meta_free, 3 + START)
            for h in range(HR):
                mm = pe.matmul(B[6 + h // 2][:, (h % 2) * RV:(h % 2 + 1) * RV], KDM[0:META, h * P:(h + 1) * P],
                               MRK[0:META, 1 + h // 2, (h % 2) * RV:(h % 2 + 1) * RV], start=True, stop=True)
            mm.then_inc(u_full, 1)
            with pe.Fori(0, 2) as it:
                for r in range(4):
                    n = 4 * it + r

                    def weave(slot):
                        gi = 2 * r + slot // 2
                        j = ACT_B + 8 * it + gi
                        if slot % 2 == 0:
                            pe.wait_ge(a_free, j - 1)
                        for k in range(4 * (slot % 2), 4 * (slot % 2) + 4):
                            mm = step("S", B[gi % 2], k, gi % 4, hn_half(gi // 4), SLAB_B + it, gi == 0, gi == 7)
                        if slot % 2 == 1:
                            mm.then_inc(a_full, 1)

                    weave(0)
                    pe.wait_ge(qs_rdy, n + 1)
                    pe.wait_ge(sm_rdy, n + START)
                    for h in range(HR):
                        mm = pe.transpose(B[2][:, h * P:(h + 1) * P], QS[:, h * P:(h + 1) * P], IDN[:, :])
                    mm.then_inc(qt_full, 1)
                    pe.wait_ge(kd_rdy, n + 1)
                    pe.wait_ge(kT_rdy, n + START)
                    for h in range(HR):
                        mm = pe.transpose(B[3][:, h * P:(h + 1) * P], KD[:, h * P:(h + 1) * P], IDN[:, :])
                    mm.then_inc(kt_full, 1)
                    weave(1)
                    pe.wait_ge(qT_rdy, n + 1)
                    pe.wait_ge(kT_rdy, n + 1 + START)
                    for h in range(HR):
                        mm = pe.matmul(B[2][:, h * P:(h + 1) * P], KTR[:, h * P:(h + 1) * P],
                                       QTR[:, h * P:(h + 1) * P], start=True, stop=True)
                    mm.then_inc(s_full, 1)
                    weave(2)
                    pe.wait_ge(st_rdy, n + 1)
                    pe.wait_ge(vl_rdy, n + 1)
                    pe.wait_ge(kdl_rdy, n + 1)
                    for h in range(HR):
                        ps, vs = slice(h * P, (h + 1) * P), slice((h % 2) * RV, (h % 2 + 1) * RV)
                        mm = three(B[6 + h // 2][:, vs], KDH[:, ps], KDL[:, ps], VH[:, h // 2, vs], VL[:, h // 2, vs],
                                   True, True, False)
                    mm.then_inc(u_full, 1)
                    pe.wait_ge(sml_rdy, n + 1)
                    pe.wait_ge(oraw_rdy, n + START)
                    for h in range(HR):
                        ps, vs = slice(h * P, (h + 1) * P), slice((h % 2) * RV, (h % 2 + 1) * RV)
                        o = B[4 + h // 2][:, vs]
                        three(o, SMH[:, ps], SML[:, ps], VH[:, h // 2, vs], VL[:, h // 2, vs], True, False, False)
                        ss = slice(h * RV, (h + 1) * RV)
                        mm = three(o, QTH[:, ps], QTL[:, ps], STH[:, ss], STL[:, ss], False, True, False)
                    mm.then_inc(o_full, 1)
                    weave(3)

            for b in range(NB):
                dense_a("M", ACT_C + b, B[b % 2], 0, hn_block(b), SLAB_C, b == 0, b == NB - 1)
                if b == 0:
                    pe.wait_ge(st_rdy, NB + 1)
                    meta_group()

            def transpose_k(rows):
                for part in range(2):
                    for g in range(4):
                        mm = pe.transpose(B[2 + part][:, g * rows:(g + 1) * rows].bitcast(F32R),
                                          KST[0:rows, part, g, :], IDR[0:rows, 0:rows])
                    mm.then_inc(ak_full, 1)

            def transpose_new_k(n):
                pe.wait_ge(ql_rdy, n + 2)
                pe.wait_ge(sc_rdy, HS * n + START)
                pe.wait_ge(akT_rdy, 2 * n + 2)
                transpose_k(P)

            def transpose_q(n):
                pe.wait_ge(akT_rdy, 2 * n + 4)
                pe.wait_ge(ptv_rdy, 8 * n + START)
                for hh in range(HS):
                    mm = pe.transpose(B[2 + hh // 4][:, (hh % 4) * P:(hh % 4 + 1) * P].bitcast(F32R),
                                      QST[:, hh, :, :].rearrange("p a d -> p (a d)"), IDR[:, :])
                    if hh % 4 == 3:
                        mm.then_inc(aq_full, 1)

            def transpose_meta_k():
                pe.wait_ge(ql_rdy, 1)
                transpose_k(META)

            between = {4: transpose_meta_k, 6: lambda: transpose_new_k(0), 7: lambda: transpose_q(0)}
            for c in range(2):
                for b in range(NB):
                    dense_a("M", ACT_C + 8 + 8 * c + b, B[b % 2], 0, hn_block(b), SLAB_C + 1 + c, b == 0, b == NB - 1,
                            middle=between.get(b) if c == 1 else None)

            def attention_block(pr, s, last):
                n = 2 * pr + s

                def weave(t):
                    q = t // 3
                    j = ACT_D + 8 * pr + 4 * s + q
                    if t % 3 == 0:
                        pe.wait_ge(a_free, j - 1)
                    for k in KS_D[t % 3]:
                        mm = step("S", B[q % 2], k, q, hn_half(s), SLAB_D + pr, s == 0 and q == 0,
                                  s == 1 and q == 3)
                    if t % 3 == 2:
                        mm.then_inc(a_full, 1)

                for t in range(12):
                    weave(t)
                    if 3 <= t <= 10:
                        p = t - 3
                        pe.wait_ge(e_rdy, 8 * n + p + 1)
                        if p == 0:
                            pe.wait_ge(aqT_rdy, 4 * n + 4)
                        if p >= 2:
                            pe.wait_ge(ptv_rdy, 8 * n + p - 1 + START)
                        for hl in range(2):
                            for sl in range(2):
                                c, key = 2 * hl + sl, hl * (NKEY + META) + sl * P
                                mm = pe.transpose(B[4 + p % 2][:, c * P:(c + 1) * P],
                                                  PR[:, p % 2, key:key + P], IDN[:, :])
                        mm.then_inc(pt_full, 1)
                        if p >= 1:
                            pe.wait_ge(ptm_rdy, 8 * n + p + START)
                        pe.transpose(B[6][0:2 * META, 0:P], PR[:, p % 2, 2 * P:2 * P + 2 * META], IDN[:, :])\
                          .then_inc(ptm_full, 1)
                    if 1 <= t <= 8:
                        p = t - 1
                        for hh in (2 * p, 2 * p + 1):
                            g = hh // 4
                            if hh % 4 == 0 or hh == 1:
                                pe.wait_ge(aqT_rdy, 4 * n + max(hh // 4, hh % 4) + 1)
                            if hh == 0:
                                pe.wait_ge(akT_rdy, 2 * n + 4)
                            if hh >= 2:
                                pe.wait_ge(sc_rdy, HS * n + hh - 1 + START)
                            pe.matmul(B[2 + hh % 2][:, 0:NKEY], QT[:, hh, :], KTS[0][:, g, KEYS_OF[hh % 2]], start=True,
                                      stop=False)
                            pe.matmul(B[2 + hh % 2][:, 0:NKEY], QT[:, hh, :], KTS[1][:, g, KEYS_OF[hh % 2]], start=False,
                                      stop=True).then_inc(sc_full, 1)
                    if t >= 4:
                        p = t - 4
                        g = p // 2
                        vs = slice(256 + g * HD, 256 + (g + 1) * HD)
                        if p == 0:
                            pe.wait_ge(mvb_done, 32)
                        pe.wait_ge(ptv_rdy, 8 * n + p + 1 + START)
                        pe.wait_ge(ptm_rdy, 8 * n + p + 1 + START)
                        pe.wait_ge(y_rdy, 8 * n + p + START)
                        pe.matmul(B[7][:, 0:P], PTM[0:2 * META, p % 2, :],
                                  MVB[0:2 * META, g, :, :].rearrange("p a d -> p (a d)"), start=True, stop=False)
                        for hl in range(2):
                            for sl in range(2):
                                blk = n + 1 if sl == s else n
                                mm = pe.matmul(B[7][:, hl * HD:(hl + 1) * HD], PTS[:, p % 2, 2 * hl + sl, :],
                                               KV[:, blk, vs], start=False, stop=hl == 1 and sl == 1)
                        mm.then_inc(pv_full, 1)
                    if t == 9 and not last:
                        transpose_new_k(n + 1)
                    if t == 11 and not last:
                        transpose_q(n + 1)

            with pe.Fori(0, 3) as pr:
                for s in range(2):
                    attention_block(pr, s, False)
            for s in range(2):
                attention_block(3, s, s == 1)

            def transpose_yr(b):
                pe.wait_ge(ysc_rdy, b + 1)
                if b >= 1:
                    pe.wait_ge(yt_rdy, 2 * b)
                for k in range(KT):
                    mm = pe.transpose(B[2 + k // 4][:, (k % 4) * P:(k % 4 + 1) * P], ST[:, k * P:(k + 1) * P],
                                      IDN[:, :])
                    if k % 4 == 3:
                        mm.then_inc(yt_full, 1)

            def transpose_ys(b, u, bank):
                for k in range(4):
                    mm = pe.transpose(bank[:, k * P:(k + 1) * P], RT[:, u, b, k * P:(k + 1) * P], IDN[:, :])
                mm.then_inc(st_full, 1)

            pe.wait_ge(sc_rdy, HS * NB + START)
            pe.wait_ge(ptv_rdy, 8 * NB + START)
            for u in range(2):
                for b in range(4):
                    if u == 1 and b < 2:
                        pe.wait_ge(a_free, ACT_H - 1 + b)
                    elif u == 1:
                        pe.wait_ge(ysl_rdy, b - 1)
                    transpose_ys(b, u, ys_bank(b, u))
            for j in range(32):
                branch, c, half, f = j // 16, (j // 8) % 2, (j // 4) % 2, j % 4
                slab = SLAB_E + 2 * branch + c
                if j >= 2:
                    pe.wait_ge(d_free, j - 1)
                if j == 0:
                    pe.wait_ge(ysl_rdy, 4)
                if j == 4:
                    pe.wait_ge(ysl_rdy, 16)
                if branch == 1 and c == 0 and f == 0:
                    pe.wait_ge(yl_rdy, 8 * (half + 1))
                act = halves(YS if branch == 0 else YR, half)
                for k in range(KT):
                    if j == 0 and k == 4:
                        pe.wait_ge(ysl_rdy, 8)
                    mm = step("S", B[6 + j % 2], k, f, act, slab, half == 0 and f == 0, half == 1 and f == 3)
                    if k == 3:
                        if j < 4:
                            b = 4 + j
                            pe.wait_ge(y_rdy, 8 * NB + START)
                            pe.wait_ge(ysl_rdy, 2 * b)
                            for u in range(2):
                                transpose_ys(b, u, B[4 + u])
                        elif j < 8:
                            transpose_yr(j - 4)
                        elif 12 <= j < 16:
                            transpose_yr(j - 8)
                mm.then_inc(d_full, 1)

            def transpose_h(b):
                pe.wait_ge(xn_rdy, NB + 1 + b + 1)
                pe.wait_ge(hn_lo, 2 * (NB + 1) + 2 * b)
                for k in range(KT):
                    mm = pe.transpose(B[2 + k // 4][:, (k % 4) * P:(k % 4 + 1) * P], ST[:, k * P:(k + 1) * P], IDN[:, :])
                    if k % 4 == 3:
                        mm.then_inc(xt_full, 1)

            for c in range(2):
                for b in range(NB):
                    j = DVE_F + 8 * c + b
                    pe.wait_ge(d_free, j - 1)
                    if c == 0:
                        pe.wait_ge(mg_rdy, 12 if b < 4 else 16)
                    for k in range(KT):
                        mm = step("M", B[6 + j % 2], k, 0, tokens(MG, b), SLAB_F + c, b == 0, b == NB - 1)
                        if k == 3 and c == 1 and b >= 2:
                            transpose_h(b - 2)
                    mm.then_inc(d_full, 1)

            def mlp(g):
                for c in range(2):
                    for gi in range(8):
                        middle = None
                        if isinstance(g, int) and g == c == 0:
                            if gi in (0, 2):
                                middle = lambda gi=gi: transpose_h(NB - 2 + gi // 2)
                            if gi == 4:
                                pe.wait_ge(hn_lo, 2 * (NB + 1) + 2 * NB)
                        dense_a("S", ACT_H + 16 * g + 8 * c + gi, B[gi % 2], gi % 4, halves(HN2, gi // 4),
                                SLAB_H + 4 * g + c, gi == 0, gi == 7, middle=middle)
                for c in range(2):
                    for b in range(NB):
                        j = DVE_H + 16 * g + 8 * c + b
                        pe.wait_ge(d_free, j - 1)
                        if c == 0:
                            pe.wait_ge(u_rdy, 16 * g + (12 if b < 4 else 16) + START)
                        for k in range(KT):
                            mm = step("M", B[6 + b % 2], k, 0, tokens(U, b), SLAB_H + 4 * g + 2 + c, b == 0, b == NB - 1)
                        mm.then_inc(d_full, 1)

            mlp(0)
            with pe.Fori(1, FF_GROUPS) as g:
                mlp(g)

        @block.scalar
        def _(act):
            for one in (meta_free, ptv_rdy, sqr_rdy):
                act.sem_inc(one, START)
            def split_hi(slab, k, first=False):
                act.wait_ge(raw_full[k % 4], 16 * (2 * slab + k // 4 + 1))
                if not first:
                    act.wait_ge(w_free, 8 * slab + k - 7)
                act.copy(WH[:, k, :], RAW[:, k % 4, :]).then_inc(w_hi, 1)

            def next_hi(slab, tiles=KT - 1):
                for k in range(tiles):
                    split_hi(slab, k)

            def square_x(b):
                rows = P if b < NB else META
                if b == 0:
                    act.wait_ge(x0_full, 16)
                else:
                    act.wait_ge(x_full[b % 4], 16 * (b // 4 + (b % 4 > 0)))
                act.activation(JUNK[0:rows, :], XR[0:rows, b % 4, :], ACT.Square,
                               accum_out=SS[0:rows, b:b + 1]).then_inc(ss_rdy, 1)
                act.wait_ge(ss_rdy, b + 1)
                act.activation(STD[0:rows, b:b + 1], SS[0:rows, b:b + 1], ACT.Sqrt, scale=1.0 / D,
                               bias=EPSC[0:rows, 0:1]).then_inc(std_rdy, 1)

            def hi_x(b):
                for u in range(2):
                    act.wait_ge(xt_full, 2 * b + u + 1)
                    w = P if b < NB else META
                    act.copy(x_part(b, u, 0),
                             B[2 + u][:, 0:4 * w].rearrange("p (k t) -> p k t", k=4)).then_inc(hn_hi, 1)

            act.wait_ge(eps_set, 1)
            act.activation(STD[:, 15:16], EPSC[:, :], ACT.Sqrt)
            square_x(0)
            for k in range(2):
                split_hi(0, k, first=True)
            hi_x(0)
            for k in range(2, 4):
                split_hi(0, k, first=True)
            square_x(1)
            for k in range(4, KT):
                split_hi(0, k, first=True)
            for b in range(NB):
                hi_x(b + 1)
                if b + 2 <= NB:
                    square_x(b + 2)
                if b == NB - 1:
                    next_hi(1)
                act.wait_ge(a_full, b + 1)
                act.copy(RT[:, 0, b, :], B[b % 2][:, :]).then_inc(a_free, 1)
            with act.Fori(1, 4) as c:
                split_hi(c, KT - 1)
                for b in range(NB):
                    if b == 1:
                        act.wait_ge(meta_full, c)
                        act.copy(MRK[0:2 * META, c - 1, :], B[6][0:2 * META, :]).then_inc(meta_free, 1)
                    if b == NB - 1:
                        next_hi(c + 1)
                    act.wait_ge(a_full, 8 * c + b + 1)
                    act.copy(RT[:, c, b, :], B[b % 2][:, :]).then_inc(a_free, 1)

            def tanh_gate(j, gi, uses):
                act.wait_ge(a_full, j + 1)
                act.wait_ge(gst_done[gi % 2], 16 * (uses + START))
                return act.activation(TB[:, gi % 2, :], B[gi % 2][:, :], ACT.Tanh, scale=0.5)

            for it in range(2):
                for r in range(4):
                    n = 4 * it + r
                    act.wait_ge(qt_full, n + START)
                    act.copy(QS[:, :], RT[:, 0, n, :]).then_inc(qs_rdy, 1)
                    if r == 0:
                        split_hi(SLAB_B + it, KT - 1)
                    act.wait_ge(qt_full, n + 1 + START)
                    act.wait_ge(o_full, n + START)
                    act.wait_ge(sqr_rdy, n + START)
                    act.copy(QTR[:, :], B[2][:, :]).then_inc(qT_rdy, 1)
                    act.wait_ge(qT_rdy, n + 1)
                    act.copy(QTH[:, :], QTR[:, :]).then_inc(qth_rdy, 1)
                    act.wait_ge(kd_rdy, n + 1)
                    act.copy(KDH[:, :], KD[:, :]).then_inc(kdh_rdy, 1)
                    act.copy(VH[:, :, :], RT[:, 2:4, n, :]).then_inc(vh_rdy, 1)
                    act.wait_ge(st_rdy, n + 1)
                    act.copy(STH[:, :], STA[:, :]).then_inc(sth_rdy, 1)
                    act.wait_ge(sm_rdy, n + 1 + START)
                    act.copy(SMH[:, :], SMK[:, :]).then_inc(smh_rdy, 1)
                    tanh_gate(ACT_B + 8 * it + 2 * r, 2 * r, 4 * it + r).then_inc(a_free, 1)
                    if r == 3:
                        for k in range(4):
                            split_hi(SLAB_B + it + 1, k)
                    act.wait_ge(oraw_rdy, n + 1 + START)
                    for h in range(HR):
                        sq = act.activation(JUNKB[:, h * RV:(h + 1) * RV],
                                            RT[:, 2 + h // 2, n, (h % 2) * RV:(h % 2 + 1) * RV],
                                            ACT.Square, accum_out=SSR[:, n, h:h + 1])
                    sq.then_inc(sqr_rdy, 1)
                    if r == 3:
                        for k in range(4, KT - 1):
                            split_hi(SLAB_B + it + 1, k)
                    tanh_gate(ACT_B + 8 * it + 2 * r + 1, 2 * r + 1, 4 * it + r).then_inc(a_free, 1)

            split_hi(SLAB_C, KT - 1)
            act.wait_ge(st_rdy, NB + 1)
            for b in range(NB):
                if b == NB - 1:
                    next_hi(SLAB_C + 1)
                act.wait_ge(a_full, ACT_C + b + 1)
                act.copy(KV[:, b + 1, :], B[b % 2][:, :])
                if b >= 2:
                    act.wait_ge(c_red, b - 1 if b == 2 else b)
                act.activation(ST[:, (b % 2) * SL:(b % 2) * SL + 256], B[b % 2][:, 0:256], ACT.Square)\
                   .then_inc(a_free, 1)
                if b == 0:
                    act.wait_ge(meta_full, 4)
                    act.copy(MKV[0:2 * META, :], B[6][0:2 * META, :]).then_inc(meta_free, 1)
                if b == 1:
                    act.wait_ge(meta_sum, 2)
                    act.activation(ST[0:META, SL + 256:2 * SL], MKV[0:META, 0:256], ACT.Square).then_inc(c_sq, 1)
            def root(first_red, stats, scale=1.0 / HD):
                act.wait_ge(c_red, first_red)
                act.activation(stats, stats, ACT.Sqrt, scale=scale,
                               bias=EPSC[0:stats.shape[0], 0:1]).then_inc(c_std, 1)

            def hi_k(rows):
                return act.copy(KST[0:rows, 0, :, :].rearrange("p g (a d) -> p g a d", a=2),
                                KNF[0:rows, :].rearrange("p (g d) -> p g d", g=4).unsqueeze(2)
                                .to_broadcast([rows, 4, 2, HD]))

            def hi_qk(n):
                act.wait_ge(qf_rdy, n + 2)
                act.wait_ge(ak_full, 2 * (n + 1))
                if not (isinstance(n, int) and n == 0):
                    act.wait_ge(aq_full, 4 * n)
                act.copy(QST[:, :, 0, :], QNF[:, :].rearrange("p (h d) -> p h d", h=HS))
                hi_k(P).then_inc(qh_rdy, 1)

            def take_q(n):
                act.wait_ge(sc_full, HS * n + START)
                for u in range(4):
                    act.wait_ge(aq_full, 4 * n + u + 1)
                    act.copy(QT[:, 4 * u:4 * u + 4, :],
                             B[2 + u][:, :].rearrange("p (k t) -> p k t", k=4)).then_inc(aqT_rdy, 1)

            for c in range(2):
                split_hi(SLAB_C + 1 + c, KT - 1)
                for b in range(NB):
                    if c == 1 and b == 5:
                        hi_qk(0)
                    if b == NB - 1:
                        next_hi(SLAB_C + 2 + c)
                    if c == 1 and b == NB - 1:
                        take_q(0)
                    act.wait_ge(a_full, ACT_C + 8 + 8 * c + b + 1)
                    act.copy(RT[:, c, b, :], B[b % 2][:, :])
                    act.wait_ge(c_red, 8 * c + b + 8)
                    act.activation(ST[:, (b % 2) * SL:(b % 2 + 1) * SL], B[b % 2][:, :], ACT.Square)\
                       .then_inc(a_free, 1)
                    if c == 0 and b == 2:
                        act.wait_ge(scr_step, 1)
                        act.activation(SCR[:, :, :], SCR[:, :, :], ACT.Sqrt, bias=EPSC[:, 0:1]).then_inc(c_std, 1)
                    if c == 1 and b == 2:
                        root(19, RSW[:, 0:2, :])
                        root(1, SSM[0:META, 0:4])
                    if c == 1 and b == 6:
                        root(23, RSW[:, 2:6, :])
                    if c == 1 and b == 3:
                        act.wait_ge(qf_rdy, 1)
                        hi_k(META).then_inc(qh_rdy, 1)
            split_hi(SLAB_D, KT - 1)
            root(25, RSW[:, 6:NB, :])
            act.activation(STD[:, 15:16], EPSC[:, :], ACT.Exp)

            def attention_block(pr, s, kind, last):
                n = 2 * pr + s
                for t in range(12):
                    if 3 <= t <= 10:
                        p = t - 3
                        act.wait_ge(pt_full, 8 * n + p + 1)
                        act.wait_ge(pv_full, 8 * n + max(p - 1, 0) + START)
                        act.copy(PTS[:, p % 2, :, :],
                                 B[4 + p % 2][:, :].rearrange("p (k t) -> p k t", k=4)).then_inc(ptv_rdy, 1)
                    if 2 <= t <= 9:
                        p = t - 2
                        act.wait_ge(nm_rdy, 8 * n + p + 1)
                        act.wait_ge(se_rdy, 8 * n + p + 1)
                        act.activation(ES[:, s, 2 * p:2 * p + 2], SE[:, s, 2 * p:2 * p + 2], ACT.Exp)
                        for hl in range(2):
                            hh = 2 * p + hl
                            e = act.activation(PR[:, p % 2, hl * NKEY:(hl + 1) * NKEY],
                                               PR[:, p % 2, hl * NKEY:(hl + 1) * NKEY], ACT.Exp,
                                               bias=NM[:, s, hh:hh + 1], accum_out=RS[:, s, hh:hh + 1])
                        e.then_inc(e_rdy, 1)
                    if t == 7 and not last:
                        hi_qk(n + 1)
                    if s == 1 and t >= 9:
                        for k in KS_D[t - 9]:
                            if k < KT - 1:
                                split_hi(SLAB_D + pr + 1, k)
                    if t == 11 and not last:
                        take_q(n + 1)
                    if t % 3 == 2:
                        q = t // 3
                        g = tanh_gate(ACT_D + 8 * pr + 4 * s + q, 4 * s + q, 8 + 4 * pr + 2 * s + q // 2)
                        g.then_inc(a_free if kind == 0 else th_rdy, 1)
                    if t == 11 and s == 1 and not last:
                        split_hi(SLAB_D + pr + 1, KT - 1)

            with act.Fori(0, 2) as pr:
                for s in range(2):
                    attention_block(pr, s, 0, False)
            for pr in (2, 3):
                for s in range(2):
                    attention_block(pr, s, 1, pr == 3 and s == 1)

            def hi_yr(b):
                for u in range(2):
                    act.wait_ge(yt_rdy, 2 * b + u + 1)
                    act.copy(YR[b // 4][:, 0, 4 * u:4 * u + 4, (b % 4) * P:(b % 4 + 1) * P],
                             TB[:, u, :].rearrange("p (k t) -> p k t", k=4)).then_inc(yh_rdy, 1)

            def hi_ys(i, b, u, bank):
                act.wait_ge(st_full, i + 1)
                act.copy(YS[b // 4][:, 0, 4 * u:4 * u + 4, (b % 4) * P:(b % 4 + 1) * P],
                         bank[:, :].rearrange("p (k t) -> p k t", k=4)).then_inc(sh_rdy, 1)

            for u in range(2):
                for b in range(4):
                    hi_ys(4 * u + b, b, u, ys_bank(b, u))
            for j in range(32):
                if j == 0:
                    split_hi(SLAB_E, KT - 1)
                if j < 4:
                    for u in range(2):
                        hi_ys(8 + 2 * j + u, 4 + j, u, B[4 + u])
                if j % 8 == 7:
                    next_hi(SLAB_E + j // 8 + 1, KT)
                if 4 <= j < 8:
                    hi_yr(j - 4)
                elif 12 <= j < 16:
                    act.wait_ge(d_full, 12)
                    hi_yr(j - 8)
                if j >= 16:
                    i = j - 16
                    f, half = 4 * (i // 8) + i % 4, (i // 4) % 2
                    act.wait_ge(e2_sum, i + 1)
                    act.copy(MG[0][:, f, half * SL:(half + 1) * SL], TB[:, 1, :]).then_inc(e2_hi, 1)

            def hi_h(b):
                for u in range(2):
                    act.wait_ge(xt_full, 2 * (NB + 1) + 2 * b + u + 1)
                    act.copy(HN2[b // 4][:, 0, 4 * u:4 * u + 4, (b % 4) * P:(b % 4 + 1) * P],
                             B[2 + u][:, :].rearrange("p (k t) -> p k t", k=4)).then_inc(hn_hi, 1)

            def square_h(b):
                act.wait_ge(d_free, DVE_F + 8 + b + 1)
                act.activation(JUNK2[:, :], H1[:, b, :], ACT.Square, accum_out=SS2[:, b:b + 1]).then_inc(ss_rdy, 1)
                act.wait_ge(ss_rdy, NB + 1 + b + 1)
                act.activation(STD2[:, b:b + 1], SS2[:, b:b + 1], ACT.Sqrt, scale=1.0 / D,
                               bias=EPSC[:, 0:1]).then_inc(std_rdy, 1)

            next_hi(SLAB_F + 1, KT)
            for b in range(NB):
                if b >= 2:
                    hi_h(b - 2)
                if b == NB - 1:
                    next_hi(SLAB_H, KT)
                square_h(b)

            def mlp(g, last):
                for c in range(2):
                    for gi in range(8):
                        if isinstance(g, int) and g == c == 0 and gi in (0, 2):
                            hi_h(NB - 2 + gi // 2)
                        if gi == 7:
                            next_hi(SLAB_H + 4 * g + c + 1, KT)
                        i = 16 * g + 8 * c + gi
                        act.wait_ge(a_full, ACT_H + i + 1)
                        act.wait_ge(u_rdy, 16 * g + max(8 * c + gi - 1, 0) + START)
                        act.activation(TB[:, gi % 2, :], B[gi % 2][:, :], ACT.Relu).then_inc(a_free, 1)
                        act.wait_ge(sq_rdy, i + 1)
                        act.copy(U[0][:, 4 * c + gi % 4, (gi // 4) * SL:(gi // 4 + 1) * SL], TU[:, gi % 2, :])\
                           .then_inc(uh_rdy, 1)
                for c in range(2):
                    if not (last and c == 1):
                        next_hi(SLAB_H + 4 * g + 3 + c, KT)

            mlp(0, False)
            with act.Fori(1, FF_GROUPS - 1) as g:
                mlp(g, False)
            mlp(FF_GROUPS - 1, True)

        @block.vector
        def _(dve):
            for one in (sm_rdy, kT_rdy, oraw_rdy, ptm_rdy, y_rdy, sc_rdy, u_rdy):
                dve.sem_inc(one, START)
            def split_lo(slab, k):
                dve.wait_ge(w_hi, 8 * slab + k + 1)
                dve.tensor_tensor(WL[:, k, :], RAW[:, k % 4, :], WH[:, k, :].bitcast(F32), ALU.subtract)\
                   .then_inc(w_ready, 1)

            def next_lo(slab, tiles=KT - 1):
                for k in range(tiles):
                    split_lo(slab, k)

            dve.memset(EPSC[:, :], EPS).then_inc(eps_set, 1)

            def norm_x(b):
                rows = P if b < NB else META
                dve.wait_ge(std_rdy, b + 1)
                dve.reciprocal(RSTD[0:rows, b:b + 1], STD[0:rows, b:b + 1]).then_inc(rstd_rdy, 1)
                dve.wait_ge(rstd_rdy, b + 1)
                if b == 0:
                    dve.wait_ge(g_full, 16)
                if b >= 1:
                    dve.wait_ge(xt_full, 2 * b)
                dve.scalar_tensor_tensor(out=ST[0:rows, :], in0=XR[0:rows, b % 4, :], scalar=RSTD[0:rows, b:b + 1],
                                         in1=GBC[0:rows, :], op0=ALU.mult, op1=ALU.mult).then_inc(xn_rdy, 1)

            def lo_x(b):
                for u in range(2):
                    dve.wait_ge(hn_hi, 2 * b + u + 1)
                    w = P if b < NB else META
                    dve.tensor_tensor(x_part(b, u, 1),
                                      B[2 + u][:, 0:4 * w].rearrange("p (k t) -> p k t", k=4),
                                      x_part(b, u, 0).bitcast(F32), ALU.subtract).then_inc(hn_lo, 1)

            norm_x(0)
            for k in range(2):
                split_lo(0, k)
            lo_x(0)
            for k in range(2, 4):
                split_lo(0, k)
            norm_x(1)
            for k in range(4, KT):
                split_lo(0, k)
            for b in range(NB):
                lo_x(b + 1)
                if b + 2 <= NB:
                    norm_x(b + 2)
            next_lo(1)
            def heads(ap, n=HR):
                return ap.rearrange("p (h d) -> p h d", h=n)

            with dve.Fori(1, 3) as c:
                split_lo(c, KT - 1)
                next_lo(c + 1)
            split_lo(3, KT - 1)
            dve.wait_ge(mu_full, 16)
            dve.tensor_tensor(MRK[0:META, :, :], MRK[0:META, :, :], MU[0:META, :, :], ALU.add).then_inc(meta_sum, 1)
            dve.wait_ge(meta_sum, 1)
            dve.wait_ge(gst_done[0], 16)
            dve.wait_ge(gst_done[1], 16)
            dve.tensor_tensor(heads(KDM[0:META, :]), heads(MRK[0:META, 0, :]),
                              COLS[0:META, 1, :].unsqueeze(2).to_broadcast([META, HR, P]), ALU.mult)\
               .then_inc(kdm_rdy, 1)
            next_lo(4)

            dve.wait_ge(c_full, 16 * 3)
            dve.wait_ge(u_full, 1)
            dve.tensor_copy(STA[:, 0:SL], B[6][:, :])
            dve.tensor_copy(STA[:, SL:2 * SL], B[7][:, :]).then_inc(st_rdy, 1)
            with dve.Fori(0, 2) as it:
                for r in range(4):
                    n = 4 * it + r
                    dve.wait_ge(kt_full, n + START)
                    dve.wait_ge(u_full, n + 1)
                    dve.tensor_tensor(heads(KD[:, :]), heads(RT[:, 1, n, :]),
                                      COLS[:, 0, :].unsqueeze(2).to_broadcast([P, HR, P]), ALU.mult)\
                       .then_inc(kd_rdy, 1)
                    if r == 0:
                        split_lo(SLAB_B + it, KT - 1)
                    dve.wait_ge(kt_full, n + 1 + START)
                    dve.wait_ge(s_full, n + START)
                    dve.wait_ge(sqr_rdy, n + START)
                    dve.tensor_copy(KTR[:, :], B[3][:, :]).then_inc(kT_rdy, 1)
                    dve.wait_ge(kdh_rdy, n + 1)
                    dve.tensor_tensor(KDL[:, :], KD[:, :], KDH[:, :].bitcast(F32), ALU.subtract).then_inc(kdl_rdy, 1)
                    dve.wait_ge(vh_rdy, n + 1)
                    dve.wait_ge(o_full, n + START)
                    dve.tensor_tensor(VL[:, :, :], RT[:, 2:4, n, :], VH[:, :, :].bitcast(F32), ALU.subtract)\
                       .then_inc(vl_rdy, 1)
                    dve.wait_ge(s_full, n + 1 + START)
                    dve.tensor_tensor(SMK[:, :], B[2][:, :], MASK[:, :], ALU.mult).then_inc(sm_rdy, 1)
                    dve.wait_ge(qth_rdy, n + 1)
                    dve.tensor_tensor(QTL[:, :], QTR[:, :], QTH[:, :].bitcast(F32), ALU.subtract)
                    dve.wait_ge(sth_rdy, n + 1)
                    dve.tensor_tensor(STL[:, :], STA[:, :], STH[:, :].bitcast(F32), ALU.subtract)
                    dve.wait_ge(smh_rdy, n + 1)
                    dve.tensor_tensor(SML[:, :], SMK[:, :], SMH[:, :].bitcast(F32), ALU.subtract).then_inc(sml_rdy, 1)
                    if r == 3:
                        for k in range(4):
                            split_lo(SLAB_B + it + 1, k)
                    dve.wait_ge(o_full, n + 1 + START)
                    dve.wait_ge(u_full, n + 2)
                    for h in range(HR):
                        cp = dve.scalar_tensor_tensor(out=STA[:, h * RV:(h + 1) * RV], in0=STA[:, h * RV:(h + 1) * RV],
                                                      scalar=float(GAMMA[h] ** P),
                                                      in1=B[6 + h // 2][:, (h % 2) * RV:(h % 2 + 1) * RV],
                                                      op0=ALU.mult, op1=ALU.add)
                        if h == 0:
                            for c in range(2):
                                raw = dve.tensor_copy(RT[:, 2 + c, n, :], B[4 + c][:, :])
                            raw.then_inc(oraw_rdy, 1)
                    cp.then_inc(st_rdy, 1)
                    if r == 3:
                        for k in range(4, KT - 1):
                            split_lo(SLAB_B + it + 1, k)

            def reduce_c(outap, inap):
                dve.tensor_reduce(outap, inap, AX_X, ALU.add).then_inc(c_red, 1)

            split_lo(SLAB_C, KT - 1)
            dve.memset(KV[:, 0, :], 0.0).then_inc(kv_zero, 1)
            dve.wait_ge(yraw_done, 16 * NB)
            dve.wait_ge(sqr_rdy, NB + START)
            dve.memset(MVB[:, :, :, :], 0.0).then_inc(d_small, 1)
            dve.wait_ge(kv_zero, 1)
            for part in range(2):
                dve.tensor_copy(KTS[part][:, :, META + P:NKEY], heads(KV[:, 0, :]))
            dve.tensor_copy(IDR[:, :], IDN[:, :])
            dve.tensor_scalar(NSK[:, :], SK[:, :], -1.0, None, ALU.mult)
            dve.scalar_tensor_tensor(out=GQK[:, :], in0=GQ[:, :], scalar=float(HD ** -0.5), in1=GK[:, :],
                                     op0=ALU.mult, op1=ALU.mult).then_inc(d_set, 1)
            for b in range(NB):
                if b == 1:
                    dve.wait_ge(mu_full, 32)
                    dve.tensor_tensor(MKV[0:META, :], MKV[0:META, :], MU2[0:META, :], ALU.add).then_inc(meta_sum, 1)
                if b == NB - 1:
                    next_lo(SLAB_C + 1)
                dve.wait_ge(a_free, ACT_C + b + 1)
                reduce_c(RSW[:, b, 16:20], heads(ST[:, (b % 2) * SL:(b % 2) * SL + 256]))
                if b == 1:
                    dve.wait_ge(c_sq, 1)
                    reduce_c(SSM[0:META, 0:4], heads(ST[0:META, SL + 256:2 * SL]))
            def normed_k(index, rows, k, rstd):
                dve.tensor_tensor(heads(KNF[0:rows, :]), heads(k), rstd.unsqueeze(2).to_broadcast([rows, 4, HD]),
                                  ALU.mult).then_inc(kf_step, 1)
                dve.wait_ge(kf_step, index)
                return dve.tensor_tensor(heads(KNF[0:rows, :]), heads(KNF[0:rows, :]),
                                         GQK[0:rows, :].unsqueeze(1).to_broadcast([rows, 4, HD]), ALU.mult)

            def normed_qk(n):
                for t2 in range(2):
                    dve.tensor_tensor(heads(QNF[:, t2 * SL:(t2 + 1) * SL], 8), heads(RT[:, t2, n, :], 8),
                                      RSW[:, n, 8 * t2:8 * t2 + 8].unsqueeze(2).to_broadcast([P, 8, HD]), ALU.mult)
                dve.wait_ge(ql_rdy, n + 1)
                normed_k(n + 2, P, KV[:, n + 1, 0:256], RSW[:, n, 16:20]).then_inc(qf_rdy, 1)

            def lo_k(rows):
                return dve.tensor_tensor(KST[0:rows, 1, :, :].rearrange("p g (a d) -> p g a d", a=2),
                                         heads(KNF[0:rows, :]).unsqueeze(2).to_broadcast([rows, 4, 2, HD]),
                                         KST[0:rows, 0, :, :].rearrange("p g (a d) -> p g a d", a=2).bitcast(F32),
                                         ALU.subtract)

            def lo_qk(n):
                dve.wait_ge(qh_rdy, n + 2)
                dve.tensor_tensor(QST[:, :, 1, :], heads(QNF[:, :], HS), QST[:, :, 0, :].bitcast(F32), ALU.subtract)
                lo_k(P).then_inc(ql_rdy, 1)

            def take_k(index, w, *places):
                for part in range(2):
                    dve.wait_ge(ak_full, index + part)
                    for lo in places:
                        cp = dve.tensor_copy(KTS[part][:, :, lo:lo + w],
                                             B[2 + part][:, 0:4 * w].rearrange("p (k t) -> p k t", k=4))
                    cp.then_inc(akT_rdy, 1)

            def take_new_k(n, s):
                dve.wait_ge(sc_full, HS * n + START)
                take_k(2 * n + 3, P, META + s * P)

            def root_inverse(index, out_stats, stats):
                dve.wait_ge(c_std, index)
                dve.reciprocal(out_stats, stats).then_inc(c_rstd, 1)
                dve.wait_ge(c_rstd, index)

            for c in range(2):
                split_lo(SLAB_C + 1 + c, KT - 1)
                for b in range(NB):
                    if c == 1 and b == 5:
                        lo_qk(0)
                    if c == 1 and b == 7:
                        take_new_k(0, 0)
                    if b == NB - 1:
                        next_lo(SLAB_C + 2 + c)
                    dve.wait_ge(a_free, ACT_C + 8 + 8 * c + b + 1)
                    reduce_c(RSW[:, b, 8 * c:8 * c + 8],
                             heads(ST[:, (b % 2) * SL:(b % 2 + 1) * SL], 8))
                    if c == 0 and b == 1:
                        dve.tensor_tensor(SCR[:, :, :], SSR[:, :, :],
                                          COLS[:, 2, :].unsqueeze(1).to_broadcast([P, NB, HR]),
                                          ALU.mult).then_inc(scr_step, 1)
                    if c == 0 and b == 3:
                        root_inverse(1, SCR[:, :, :], SCR[:, :, :])
                        dve.tensor_tensor(SCR[:, :, :], SCR[:, :, :],
                                          COLS[:, 3, :].unsqueeze(1).to_broadcast([P, NB, HR]),
                                          ALU.mult).then_inc(scr_step, 1)
                    if c == 1 and b == 2:
                        root_inverse(2, RSW[:, 0:2, :], RSW[:, 0:2, :])
                        root_inverse(3, SSM[0:META, 4:8], SSM[0:META, 0:4])
                        dve.wait_ge(d_set, 1)
                        normed_k(1, META, MKV[0:META, 0:256], SSM[0:META, 4:8]).then_inc(qf_rdy, 1)
                    if c == 1 and b == 6:
                        root_inverse(4, RSW[:, 2:6, :], RSW[:, 2:6, :])
                    if c == 1 and b == 3:
                        dve.wait_ge(qh_rdy, 1)
                        lo_k(META).then_inc(ql_rdy, 1)
                        normed_qk(0)
                    if c == 1 and b == 4:
                        take_k(1, META, 0, NKEY)
            split_lo(SLAB_D, KT - 1)
            root_inverse(5, RSW[:, 6:NB, :], RSW[:, 6:NB, :])


            def attention_block(pr, s, kind, last):
                n = 2 * pr + s
                for t in range(12):
                    if t == 10 and not last:
                        take_new_k(n + 1, 1 - s)
                    if t == 0:
                        dve.wait_ge(dt_full[s], 16 * (pr + 1))
                    if 3 <= t <= 10:
                        p = t - 3
                        dve.wait_ge(ptm_full, 8 * n + p + 1)
                        if p >= 2:
                            dve.wait_ge(pv_full, 8 * n + p - 1 + START)
                        dve.tensor_copy(PTM[0:2 * META, p % 2, :], B[6][0:2 * META, 0:P]).then_inc(ptm_rdy, 1)
                    if 1 <= t <= 8:
                        p = t - 1
                        if p >= 2:
                            dve.wait_ge(ptm_full, 8 * n + p - 1)
                        for hl in range(2):
                            hh = 2 * p + hl
                            dve.wait_ge(sc_full, HS * n + hh + 1 + START)
                            dve.scalar_tensor_tensor(out=PR[:, p % 2, hl * NKEY:(hl + 1) * NKEY],
                                                     in0=DT[:, s, KEYS_OF[hl]],
                                                     scalar=SLOPES[hh], in1=B[2 + hh % 2][:, 0:NKEY],
                                                     op0=ALU.mult, op1=ALU.add).then_inc(sc_rdy, 1)
                        dve.wait_ge(sc_rdy, HS * n + 2 * p + 2 + START)
                        dve.tensor_reduce(MX[:, s, 2 * p:2 * p + 2], heads(PR[:, p % 2, :], 2), AX_X, ALU.max)\
                           .then_inc(mx_rdy, 1)
                        dve.wait_ge(mx_rdy, 8 * n + p + 1)
                        cs = slice(2 * p, 2 * p + 2)
                        dve.scalar_tensor_tensor(out=NM[:, s, cs], in0=MX[:, s, cs], scalar=-1.0,
                                                 in1=NSK[:, cs], op0=ALU.mult, op1=ALU.min).then_inc(nm_rdy, 1)
                        dve.wait_ge(nm_rdy, 8 * n + p + 1)
                        dve.tensor_tensor(SE[:, s, cs], SK[:, cs], NM[:, s, cs], ALU.add).then_inc(se_rdy, 1)
                    if t >= 4:
                        p = t - 4
                        cs = slice(2 * p, 2 * p + 2)
                        dve.wait_ge(e_rdy, 8 * n + p + 1)
                        dve.tensor_tensor(RS[:, s, cs], RS[:, s, cs], ES[:, s, cs], ALU.add).then_inc(den_rdy, 1)
                        dve.wait_ge(den_rdy, 16 * n + 2 * p + 1)
                        dve.reciprocal(ES[:, s, cs], RS[:, s, cs]).then_inc(den_rdy, 1)
                        dve.wait_ge(den_rdy, 16 * n + 2 * p + 2)
                        dve.wait_ge(pv_full, 8 * n + p + 1 + START)
                        dve.tensor_tensor(RT[:, p // 4, n, (p % 4) * P:(p % 4 + 1) * P]
                                          .rearrange("p (h d) -> p h d", h=2),
                                          B[7][:, 0:P].rearrange("p (h d) -> p h d", h=2),
                                          ES[:, s, cs].unsqueeze(2).to_broadcast([P, 2, HD]), ALU.mult)\
                           .then_inc(y_rdy, 1)
                    if t == 6 and not last:
                        normed_qk(n + 1)
                    if t == 8 and not last:
                        lo_qk(n + 1)
                    if s == 1 and t >= 9:
                        for k in KS_D[t - 9]:
                            if k < KT - 1:
                                split_lo(SLAB_D + pr + 1, k)
                    if t % 3 == 2 and kind == 1:
                        q = t // 3
                        dve.wait_ge(th_rdy, 8 * (pr - 2) + 4 * s + q + 1)
                        dve.scalar_tensor_tensor(out=TB[:, q % 2, :], in0=TB[:, q % 2, :], scalar=1.0,
                                                 in1=B[q % 2][:, :], op0=ALU.add, op1=ALU.mult)\
                           .then_inc(a_free, 1)
                    if t == 11 and s == 1 and not last:
                        split_lo(SLAB_D + pr + 1, KT - 1)

            with dve.Fori(0, 2) as pr:
                for s in range(2):
                    attention_block(pr, s, 0, False)
            for pr in (2, 3):
                for s in range(2):
                    attention_block(pr, s, 1, pr == 3 and s == 1)

            def scale_yr(b):
                dve.wait_ge(yb_full[b % 2], 16 * (b // 2 + 1))
                if b == 0:
                    dve.wait_ge(gm_full, 16)
                    dve.wait_ge(scr_step, 2)
                if b >= 1:
                    dve.wait_ge(yt_full, 2 * b)
                for h in range(HR):
                    y = dve.scalar_tensor_tensor(out=ST[:, h * RV:(h + 1) * RV],
                                                 in0=YB[:, b % 2, h * RV:(h + 1) * RV],
                                                 scalar=SCR[:, b, h:h + 1], in1=GBR[:, h * RV:(h + 1) * RV],
                                                 op0=ALU.mult, op1=ALU.mult)
                y.then_inc(ysc_rdy, 1)

            def gate_yr(b):
                for u in range(2):
                    dve.wait_ge(yt_full, 2 * b + u + 1)
                    if u == 0:
                        dve.wait_ge(gb_full[b % 2], 32 * (b // 2 + 1))
                        if b == 0:
                            dve.wait_ge(gst_done[0], 16 * (24 + START))
                            dve.wait_ge(gst_done[1], 16 * (24 + START))
                    dve.tensor_tensor(TB[:, u, :].rearrange("p (k t) -> p k t", k=4),
                                      B[2 + u][:, :].rearrange("p (k t) -> p k t", k=4),
                                      GB[:, b % 2, 4 * u:4 * u + 4, :], ALU.mult).then_inc(yt_rdy, 1)
                for u in range(2):
                    cols = slice((b % 4) * P, (b % 4 + 1) * P)
                    dve.wait_ge(yh_rdy, 2 * b + u + 1)
                    dve.tensor_tensor(YR[b // 4][:, 1, 4 * u:4 * u + 4, cols],
                                      TB[:, u, :].rearrange("p (k t) -> p k t", k=4),
                                      YR[b // 4][:, 0, 4 * u:4 * u + 4, cols].bitcast(F32), ALU.subtract)\
                       .then_inc(yl_rdy, 1)

            def lo_ys(i, b, u, bank):
                cols = slice((b % 4) * P, (b % 4 + 1) * P)
                dve.wait_ge(sh_rdy, i + 1)
                dve.tensor_tensor(YS[b // 4][:, 1, 4 * u:4 * u + 4, cols],
                                  bank[:, :].rearrange("p (k t) -> p k t", k=4),
                                  YS[b // 4][:, 0, 4 * u:4 * u + 4, cols].bitcast(F32), ALU.subtract)\
                   .then_inc(ysl_rdy, 1)

            for u in range(2):
                for b in range(4):
                    lo_ys(4 * u + b, b, u, ys_bank(b, u))
            for j in range(32):
                if j == 0:
                    split_lo(SLAB_E, KT - 1)
                if j < 4:
                    for u in range(2):
                        lo_ys(8 + 2 * j + u, 4 + j, u, B[4 + u])
                if j % 8 == 7:
                    next_lo(SLAB_E + j // 8 + 1, KT)
                if 4 <= j < 7:
                    gate_yr(j - 4)
                elif 12 <= j < 15:
                    gate_yr(j - 8)
                i = j % 16
                f, half = 4 * (i // 8) + i % 4, (i // 4) % 2
                hs = slice(half * SL, (half + 1) * SL)
                dve.wait_ge(d_full, j + 1)
                dve.wait_ge(tg_full[j % 4], 16 * (j // 4 + 1))
                if j < 16:
                    dve.scalar_tensor_tensor(out=MR[:, f, hs], in0=TH[:, j % 4, :], scalar=1.0, in1=B[6 + j % 2][:, :],
                                             op0=ALU.add, op1=ALU.mult).then_inc(d_free, 1)
                    if j in (7, 15):
                        gate_yr(3 + 4 * (j // 8))
                    if 3 <= j < 7:
                        scale_yr(j - 3)
                    if 11 <= j < 15:
                        scale_yr(j - 7)
                else:
                    if j == 16:
                        dve.wait_ge(yl_rdy, 2 * NB)
                    dve.scalar_tensor_tensor(out=TB[:, 0, :], in0=TH[:, j % 4, :], scalar=1.0, in1=B[6 + j % 2][:, :],
                                             op0=ALU.add, op1=ALU.mult).then_inc(d_free, 1)
                    dve.wait_ge(d_free, j + 1)
                    dve.tensor_tensor(TB[:, 1, :], TB[:, 0, :], MR[:, f, hs], ALU.add).then_inc(e2_sum, 1)
                    dve.wait_ge(e2_hi, i + 1)
                    dve.tensor_tensor(MG[1][:, f, hs], TB[:, 1, :], MG[0][:, f, hs].bitcast(F32), ALU.subtract)\
                       .then_inc(mg_rdy, 1)

            def norm_h(b):
                dve.wait_ge(std_rdy, NB + 1 + b + 1)
                dve.reciprocal(RSTD2[:, b:b + 1], STD2[:, b:b + 1]).then_inc(rstd_rdy, 1)
                dve.wait_ge(rstd_rdy, NB + 1 + b + 1)
                if b == 0:
                    dve.wait_ge(gm_full, 32)
                else:
                    dve.wait_ge(xt_full, 2 * (NB + 1) + 2 * b)
                dve.scalar_tensor_tensor(out=ST[:, :], in0=H1[:, b, :], scalar=RSTD2[:, b:b + 1],
                                         in1=GBM[:, :], op0=ALU.mult, op1=ALU.mult).then_inc(xn_rdy, 1)

            def lo_h(b):
                cols = slice((b % 4) * P, (b % 4 + 1) * P)
                for u in range(2):
                    dve.wait_ge(hn_hi, 2 * (NB + 1) + 2 * b + u + 1)
                    dve.tensor_tensor(HN2[b // 4][:, 1, 4 * u:4 * u + 4, cols],
                                      B[2 + u][:, :].rearrange("p (k t) -> p k t", k=4),
                                      HN2[b // 4][:, 0, 4 * u:4 * u + 4, cols].bitcast(F32), ALU.subtract)\
                       .then_inc(hn_lo, 1)

            for c in range(2):
                for b in range(NB):
                    j = DVE_F + 8 * c + b
                    if c == 1 and b >= 2:
                        lo_h(b - 2)
                    if b == NB - 1:
                        next_lo(SLAB_F + c + 1, KT)
                    if c == 0:
                        dve.wait_ge(xres_full[b], 16)
                    dve.wait_ge(d_full, j + 1)
                    dve.scalar_tensor_tensor(out=H1[:, b, c * SL:(c + 1) * SL], in0=B[6 + j % 2][:, :], scalar=0.5,
                                             in1=H1[:, b, c * SL:(c + 1) * SL], op0=ALU.mult, op1=ALU.add)\
                       .then_inc(d_free, 1)
                    if c == 1:
                        norm_h(b)
            def mlp(g, last):
                for c in range(2):
                    for gi in range(8):
                        if isinstance(g, int) and g == c == 0 and gi in (0, 2):
                            lo_h(NB - 2 + gi // 2)
                        if gi == 7:
                            next_lo(SLAB_H + 4 * g + c + 1, KT)
                        i = 16 * g + 8 * c + gi
                        fs, hs = 4 * c + gi % 4, slice((gi // 4) * SL, (gi // 4 + 1) * SL)
                        dve.wait_ge(a_free, ACT_H + i + 1)
                        dve.tensor_tensor(TU[:, gi % 2, :], TB[:, gi % 2, :], TB[:, gi % 2, :], ALU.mult)\
                           .then_inc(sq_rdy, 1)
                        dve.wait_ge(uh_rdy, i + 1)
                        dve.tensor_tensor(U[1][:, fs, hs], TU[:, gi % 2, :], U[0][:, fs, hs].bitcast(F32),
                                          ALU.subtract).then_inc(u_rdy, 1)
                for c in range(2):
                    for b in range(NB):
                        if b == NB - 1 and not (last and c == 1):
                            next_lo(SLAB_H + 4 * g + 3 + c, KT)
                        dve.wait_ge(d_full, DVE_H + 16 * g + 8 * c + b + 1)
                        dve.tensor_tensor(H1[:, b, c * SL:(c + 1) * SL], B[6 + b % 2][:, :],
                                          H1[:, b, c * SL:(c + 1) * SL], ALU.add).then_inc(d_free, 1)

            mlp(0, False)
            with dve.Fori(1, FF_GROUPS - 1) as g:
                mlp(g, False)
            mlp(FF_GROUPS - 1, True)


_INS = ["x", "meta_tokens", "mix_norm_g", "w_in", "ret_norm_g", "q_norm_g", "k_norm_g", "sinks",
        "w_ret_branch", "w_swa_branch", "w_out", "mlp_norm_g", "w_up", "w_down"]


def kernel(**inputs):
    import concourse.bacc as bacc
    from concourse.bass_utils import run_bass_kernel_spmd

    nc = bacc.Bacc("TRN2", target_bir_lowering=False, num_devices=1, dynamic_dma_scratch_size=4096)
    shapes = {"x": (T, D), "q_norm_g": (HD,), "k_norm_g": (HD,), "mix_norm_g": (D,), "mlp_norm_g": (D,),
              "ret_norm_g": (HR * RV,), "sinks": (HS,)}
    arrays, args = {}, []
    for name in _INS:
        a = np.ascontiguousarray(inputs[name])
        a = a.reshape(shapes.get(name, a.shape[-2:]))
        arrays[f"in_{name}"] = a
    arrays.update(shape_constants())
    for name, a in arrays.items():
        args.append(nc.dram_tensor(name, a.shape, mybir.dt.from_np(a.dtype), kind="ExternalInput").ap())
    args.append(nc.dram_tensor("h_out", (T, D), F32, kind="ExternalOutput").ap())
    build(nc, *args)
    r = run_bass_kernel_spmd(nc, [arrays], core_ids=[0])
    return r.results[0]["h_out"].reshape(1, T, D)
```
